# Optimizing a Trainium2 kernel written in Bass

```python
import jax, jax.numpy as jnp
from jax import lax
import numpy as np

D_MODEL = 1024
BATCH = 1
SEQ = 512
DEPTH = 1

HEAD_DIM = 64
MIX_WIDTH = D_MODEL
RWKV_WIDTH = MIX_WIDTH // 2
FOX_WIDTH = MIX_WIDTH - RWKV_WIDTH
RWKV_HEADS = RWKV_WIDTH // HEAD_DIM
FOX_HEADS = FOX_WIDTH // HEAD_DIM
DECAY_LORA = 64
AAA_LORA = 64
GATE_LORA = 128
RWKV_IN = 3 * RWKV_WIDTH + DECAY_LORA + AAA_LORA + GATE_LORA
FOX_IN = 3 * FOX_WIDTH + FOX_HEADS
IN_WIDTH = RWKV_IN + FOX_IN
RWKV_SPLITS = [RWKV_WIDTH, 2 * RWKV_WIDTH, 3 * RWKV_WIDTH,
               3 * RWKV_WIDTH + DECAY_LORA, 3 * RWKV_WIDTH + DECAY_LORA + AAA_LORA]
FOX_SPLITS = [FOX_WIDTH, 2 * FOX_WIDTH, 3 * FOX_WIDTH]
Q_BLOCK = 128
N_EXPERTS = 32
TOP_K = 4
D_FF = D_MODEL
MOE_BLOCK = 128
SWIGLU_ALPHA = 1.702
SWIGLU_LIMIT = 7.0
RMS_EPS = 1e-5
RWKV_GN_EPS = 64e-5

kernel_name = "hymba_rwkv7_fox_moe_layer"

def rms_norm(x, g, eps=RMS_EPS):
    xf = x.astype(jnp.float32)
    y = xf * lax.rsqrt(jnp.mean(xf * xf, axis=-1, keepdims=True) + eps)
    return (y * g.astype(jnp.float32)).astype(x.dtype)

def rwkv7_group(u, mu, w0, w_up, a0, a_up, g_up, k_k, k_a, r_k, ln_w, ln_b):
    B, T, _ = u.shape
    H, N = RWKV_HEADS, HEAD_DIM
    u = u.astype(jnp.float32)
    u_prev = jnp.pad(u[:, :-1], ((0, 0), (1, 0), (0, 0)))
    u = u + (u_prev - u) * mu
    r, k, v, wl, al, gl = jnp.split(u, RWKV_SPLITS, axis=-1)
    w = -jax.nn.softplus(-(w0 + jnp.tanh(wl) @ w_up)) - 0.5
    decay = jnp.exp(-jnp.exp(w))
    a = jax.nn.sigmoid(a0 + al @ a_up)
    g = jax.nn.sigmoid(gl) @ g_up
    kk = (k * k_k).reshape(B, T, H, N)
    kk = kk / jnp.maximum(jnp.sqrt(jnp.sum(kk * kk, axis=-1, keepdims=True)), 1e-12)
    k = k * (1.0 + (a - 1.0) * k_a)
    r, k, v, decay, a = (t.reshape(B, T, H, N) for t in (r, k, v, decay, a))

    def step(S, inp):
        r_t, w_t, k_t, v_t, kk_t, a_t = inp
        s_kk = jnp.einsum('bhvk,bhk->bhv', S, kk_t)
        S = (S * w_t[:, :, None, :]
             - s_kk[..., None] * (kk_t * a_t)[:, :, None, :]
             + v_t[..., None] * k_t[:, :, None, :])
        return S, jnp.einsum('bhvk,bhk->bhv', S, r_t)

    S0 = jnp.zeros((B, H, N, N), jnp.float32)
    seq_inputs = tuple(jnp.moveaxis(t, 1, 0) for t in (r, decay, k, v, kk, a))
    _, y = lax.scan(step, S0, seq_inputs)
    y = jnp.moveaxis(y, 0, 1)
    mean = jnp.mean(y, axis=-1, keepdims=True)
    var = jnp.mean(jnp.square(y - mean), axis=-1, keepdims=True)
    y = ((y - mean) * lax.rsqrt(var + RWKV_GN_EPS)).reshape(B, T, RWKV_WIDTH) * ln_w + ln_b
    bonus = jnp.sum(r * k * r_k, axis=-1, keepdims=True) * v
    return (y + bonus.reshape(B, T, RWKV_WIDTH)) * g

def fox_group(u, f_bias, out_g):
    B, T, _ = u.shape
    H, Dh = FOX_HEADS, HEAD_DIM
    q, k, v, fl = jnp.split(u.astype(jnp.float32), FOX_SPLITS, axis=-1)
    q = q.reshape(B, T, H, Dh) * (Dh ** -0.5)
    k = k.reshape(B, T, H, Dh)
    v = v.reshape(B, T, H, Dh)
    log_f = jax.nn.log_sigmoid(fl + f_bias)
    c = jnp.transpose(jnp.cumsum(log_f, axis=1), (0, 2, 1))
    key_pos = jnp.arange(T)

    def query_block(i):
        start = i * Q_BLOCK
        qb = lax.dynamic_slice_in_dim(q, start, Q_BLOCK, axis=1)
        cb = lax.dynamic_slice_in_dim(c, start, Q_BLOCK, axis=2)
        s = jnp.einsum('bqhd,bkhd->bhqk', qb, k) + cb[..., :, None] - c[..., None, :]
        q_pos = start + jnp.arange(Q_BLOCK)
        s = jnp.where(key_pos[None, :] <= q_pos[:, None], s, -jnp.inf)
        p = jax.nn.softmax(s, axis=-1)
        return jnp.einsum('bhqk,bkhd->bqhd', p, v)

    o = lax.map(query_block, jnp.arange(T // Q_BLOCK))
    o = jnp.transpose(o, (1, 0, 2, 3, 4)).reshape(B, T, H, Dh)
    o = o * lax.rsqrt(jnp.mean(o * o, axis=-1, keepdims=True) + RMS_EPS)
    return o.reshape(B, T, FOX_WIDTH) * out_g

def clamped_swiglu(h):
    glu, lin = h[..., ::2], h[..., 1::2]
    glu = jnp.minimum(glu, SWIGLU_LIMIT)
    lin = jnp.clip(lin, -SWIGLU_LIMIT, SWIGLU_LIMIT)
    return glu * jax.nn.sigmoid(SWIGLU_ALPHA * glu) * (lin + 1.0)

def moe_ffn(h, router_w, router_b, w1, b1, w2, b2):
    B, T, D = h.shape
    n_tok = B * T
    n_slots = n_tok * TOP_K
    xt = h.reshape(n_tok, D)
    logits = (xt @ router_w + router_b).astype(jnp.float32)
    top_val, top_idx = lax.top_k(logits, TOP_K)
    gates = jax.nn.softmax(top_val, axis=-1)
    flat_e = top_idx.reshape(-1)
    order = jnp.argsort(flat_e)
    sorted_e = flat_e[order]
    sorted_tok = (order // TOP_K).astype(jnp.int32)
    sorted_gate = gates.reshape(-1)[order]
    sizes = jnp.bincount(flat_e, length=N_EXPERTS).astype(jnp.int32)
    padded = (sizes + MOE_BLOCK - 1) // MOE_BLOCK * MOE_BLOCK
    starts = jnp.cumsum(sizes) - sizes
    pad_ends = jnp.cumsum(padded)
    pad_starts = pad_ends - padded
    dest = pad_starts[sorted_e] + jnp.arange(n_slots, dtype=jnp.int32) - starts[sorted_e]
    n_pad = n_slots + N_EXPERTS * MOE_BLOCK
    n_blocks = n_pad // MOE_BLOCK
    slot_tok = jnp.zeros((n_pad,), jnp.int32).at[dest].set(sorted_tok)
    slot_gate = jnp.zeros((n_pad,), jnp.float32).at[dest].set(sorted_gate)
    block_start = jnp.arange(n_blocks, dtype=jnp.int32) * MOE_BLOCK
    block_e = jnp.minimum(jnp.searchsorted(pad_ends, block_start, side='right'), N_EXPERTS - 1)

    def expert_block(args):
        tok, gate, e = args
        hid = xt[tok] @ w1[e] + b1[e]
        out = clamped_swiglu(hid) @ w2[e] + b2[e]
        return out * gate[:, None].astype(out.dtype)

    outs = lax.map(expert_block, (slot_tok.reshape(n_blocks, MOE_BLOCK),
                                  slot_gate.reshape(n_blocks, MOE_BLOCK), block_e))
    y = jnp.zeros((n_tok, D), outs.dtype).at[slot_tok].add(outs.reshape(n_pad, D))
    return y.reshape(B, T, D).astype(h.dtype)

def setup_inputs(seed: int = 0) -> dict:
    key = jax.random.key(seed)
    ks = jax.random.split(key, 25)
    L = DEPTH
    f32 = jnp.float32

    def nrm(k, shape, scale):
        return scale * jax.random.normal(k, shape, f32)

    return {
        "x": jax.random.normal(ks[0], (BATCH, SEQ, D_MODEL), f32),
        "attn_norm_g": 1.0 + nrm(ks[1], (L, D_MODEL), 0.02),
        "w_in": nrm(ks[2], (L, D_MODEL, IN_WIDTH), D_MODEL ** -0.5),
        "rwkv_mu": jax.random.uniform(ks[3], (L, RWKV_IN), f32),
        "rwkv_w0": jax.random.uniform(ks[4], (L, RWKV_WIDTH), f32, -6.0, -0.5),
        "rwkv_w_up": nrm(ks[5], (L, DECAY_LORA, RWKV_WIDTH), 0.5 * DECAY_LORA ** -0.5),
        "rwkv_a0": nrm(ks[6], (L, RWKV_WIDTH), 0.5),
        "rwkv_a_up": nrm(ks[7], (L, AAA_LORA, RWKV_WIDTH), AAA_LORA ** -0.5),
        "rwkv_g_up": nrm(ks[8], (L, GATE_LORA, RWKV_WIDTH), GATE_LORA ** -0.5),
        "rwkv_k_k": 0.85 + nrm(ks[9], (L, RWKV_WIDTH), 0.02),
        "rwkv_k_a": 1.0 + nrm(ks[10], (L, RWKV_WIDTH), 0.02),
        "rwkv_r_k": nrm(ks[11], (L, RWKV_HEADS, HEAD_DIM), 0.1),
        "rwkv_ln_w": 1.0 + nrm(ks[12], (L, RWKV_WIDTH), 0.02),
        "rwkv_ln_b": nrm(ks[13], (L, RWKV_WIDTH), 0.01),
        "fox_f_bias": jax.random.uniform(ks[14], (L, FOX_HEADS), f32, 1.0, 4.0),
        "fox_out_g": 1.0 + nrm(ks[15], (L, FOX_WIDTH), 0.02),
        "w_out": nrm(ks[16], (L, MIX_WIDTH, D_MODEL), MIX_WIDTH ** -0.5),
        "ffn_norm_g": 1.0 + nrm(ks[17], (L, D_MODEL), 0.02),
        "router_w": nrm(ks[18], (L, D_MODEL, N_EXPERTS), D_MODEL ** -0.5),
        "router_b": nrm(ks[19], (L, N_EXPERTS), 0.01),
        "expert_w1": nrm(ks[20], (L, N_EXPERTS, D_MODEL, 2 * D_FF), D_MODEL ** -0.5),
        "expert_b1": nrm(ks[21], (L, N_EXPERTS, 2 * D_FF), 0.01),
        "expert_w2": nrm(ks[22], (L, N_EXPERTS, D_FF, D_MODEL), D_FF ** -0.5),
        "expert_b2": nrm(ks[23], (L, N_EXPERTS, D_MODEL), 0.01),
        "final_norm_g": 1.0 + nrm(ks[24], (D_MODEL,), 0.02),
    }

def reference(x, attn_norm_g, w_in, rwkv_mu, rwkv_w0, rwkv_w_up, rwkv_a0, rwkv_a_up,
              rwkv_g_up, rwkv_k_k, rwkv_k_a, rwkv_r_k, rwkv_ln_w, rwkv_ln_b,
              fox_f_bias, fox_out_g, w_out, ffn_norm_g, router_w, router_b,
              expert_w1, expert_b1, expert_w2, expert_b2, final_norm_g):
    for l in range(DEPTH):
        h = rms_norm(x, attn_norm_g[l])
        u = h @ w_in[l]
        y_rwkv = rwkv7_group(u[..., :RWKV_IN], rwkv_mu[l], rwkv_w0[l], rwkv_w_up[l],
                             rwkv_a0[l], rwkv_a_up[l], rwkv_g_up[l], rwkv_k_k[l],
                             rwkv_k_a[l], rwkv_r_k[l], rwkv_ln_w[l], rwkv_ln_b[l])
        y_fox = fox_group(u[..., RWKV_IN:], fox_f_bias[l], fox_out_g[l])
        mix = jnp.concatenate([y_rwkv.astype(x.dtype), y_fox.astype(x.dtype)], axis=-1)
        x = x + mix @ w_out[l]
        x = x + moe_ffn(rms_norm(x, ffn_norm_g[l]), router_w[l], router_b[l],
                        expert_w1[l], expert_b1[l], expert_w2[l], expert_b2[l])
    return rms_norm(x, final_norm_g)


_drawn_inputs = setup_inputs


def setup_inputs(seed=0):
    import zlib

    import numpy as np

    out = dict(_drawn_inputs(seed))
    spreads = {}
    factors = {'rwkv_w_up': 2.772,
     'rwkv_k_k': 3.683,
     'rwkv_ln_w': 3.328,
     'rwkv_ln_b': 6.506,
     'expert_b1': 8.0,
     'expert_b2': 8.0,
     'final_norm_g': 2.852}
    for name, (base, spread) in spreads.items():
        noise = np.random.default_rng([zlib.crc32(name.encode()), seed]).standard_normal(out[name].shape)
        drawn = base * np.exp(spread * noise) if base else spread * noise
        out[name] = __import__('jax').numpy.asarray(drawn.astype(out[name].dtype))
    for name, factor in factors.items():
        out[name] = (out[name] * factor).astype(out[name].dtype)
    return out
```

```python
import concourse.bass as bass
from concourse import mybir
from contextlib import ExitStack


def hymba_layer(nc, x, attn_norm_g, w_in, mu, w0, w_up, a0, a_up, g_up, k_k, k_a, r_k, ln_w, ln_b,
                f_bias, out_g, w_out, ffn_norm_g, router_w, router_b, w1, b1, w2, b2, final_norm_g, out):
    f32 = mybir.dt.float32
    bf16 = mybir.dt.bfloat16
    i32 = mybir.dt.int32
    u32 = mybir.dt.uint32
    ALU = mybir.AluOpType
    ACT = mybir.ActivationFunctionType
    AX = mybir.AxisListType.X

    P = 128
    T, D = x.shape[1], x.shape[2]
    TT, KT = T // P, D // P
    H, N = r_k.shape[1], r_k.shape[2]
    HW = H * N
    JT = HW // P
    LORA = w_up.shape[1]
    C = 64
    NC = T // C
    FOX0 = 3 * HW + 2 * LORA + g_up.shape[1]
    E, F2 = router_w.shape[2], w1.shape[3]
    FT = F2 // 2 // P
    TOPK = 4
    NS = 96
    EXTRA = -(-T // NS) - 1
    NOVF = 22
    assert NOVF >= T * TOPK // NS and NOVF % 2 == 0
    NB = E + NOVF
    CH = 6
    CW = 512
    W1C = F2 // CW
    KAPPA = 0.6065306597126334
    LEVELS = 6
    RMS_EPS, GN_EPS = 1e-5, 64e-5

    slot_tokens = nc.dram_tensor("slot_tokens", [(NB + 2) * NS, 1], i32).ap()
    h2_rows = nc.dram_tensor("h2_rows", [T, D], f32).ap()
    expert_rows = nc.dram_tensor("expert_rows", [NB * NS, D], f32).ap()

    ctx = ExitStack()
    with ctx:
        def sb(name, shape, dt=f32):
            return ctx.enter_context(nc.sbuf_tensor(name, shape, dt))

        def sem(name):
            return ctx.enter_context(nc.semaphore(name))

        slots = sb("slots", [P, CH, KT, CW])
        xs = sb("xs", [P, TT, D])
        hT = sb("hT", [P, KT, T])
        AR = sb("AR", [P, JT, NC, 2 * C])
        BK = sb("BK", [P, JT, NC, 2 * C])
        qk = sb("qk", [P, 2, JT, T])
        shiftbuf = sb("shiftbuf", [P, 2, T + 1])

        def region(t2d, off, size):
            return t2d[:, off:off + size]

        slot_flat = [slots[:, s].rearrange("p k f -> p (k f)") for s in range(CH)]
        S4 = KT * CW
        decay_s = region(slot_flat[3], 0, JT * T).rearrange("p (j t) -> p j t", j=JT)
        decay_c = region(slot_flat[3], JT * T, JT * T).rearrange("p (j t) -> p j t", j=JT)
        vT = region(slot_flat[4], 0, JT * T).rearrange("p (j t) -> p j t", j=JT)
        aT = region(slot_flat[4], JT * T, JT * T).rearrange("p (j t) -> p j t", j=JT)
        G = region(slot_flat[5], 0, TT * HW).rearrange("p (t c) -> p t c", t=TT)
        foxv = region(slot_flat[5], TT * HW, TT * HW).rearrange("p (t c) -> p t c", t=TT)
        decay_e = region(slot_flat[2], 0, JT * T).rearrange("p (j t) -> p j t", j=JT)
        wa = region(slot_flat[2], 4 * T, T)
        gl = region(slot_flat[2], 5 * T, T)
        lora_up = region(slot_flat[2], 6 * T, HW)
        gup = region(slot_flat[2], 7 * T, HW)
        zrow = aT[:, 2:4, :].rearrange("p j t -> p (j t)")
        fP = region(slot_flat[3], 0, 2 * T).rearrange("p (b t) -> p b t", b=2)
        fPT = region(slot_flat[3], 2 * T, 2 * T).rearrange("p (b t) -> p b t", b=2)
        fo = region(slot_flat[3], 4 * T, 2 * HW).rearrange("p (b c) -> p b c", b=2)
        fsq = region(slot_flat[3], 6 * T, HW)
        cf = region(slot_flat[3], 7 * T, T)[0:H, :]
        cb = region(slot_flat[2], 0, T).bitcast(bf16).rearrange("p (g t) -> p g t", g=2)[0:H]
        blocks = region(slot_flat[3], 0, (LEVELS + 1) * C).rearrange("p (l c) -> p l c", c=C)[0:C]
        qkf = qk[:, :, :, :].rearrange("p a j t -> p (a j t)")
        SCm = region(qkf, 0, 2 * H * 2 * C).rearrange("p (c h t) -> p c h t", c=2, h=H)
        UV = region(qkf, 2048, 2 * HW).rearrange("p (c h v) -> p c h v", c=2, h=H)
        BKtok = region(qkf, 3072, 2 * HW).rearrange("p (c h v) -> p c h v", c=2, h=H)
        s2 = slot_flat[2]
        Atok = region(s2, 0, 1024).rearrange("p (c h v) -> p c h v", c=2, h=H)
        MV = region(s2, 1024, 1024).rearrange("p (c h v) -> p c h v", c=2, h=H)
        Xm = region(s2, 2048, 1024).rearrange("p (c h v) -> p c h v", c=2, h=H)
        XT = region(s2, 3072, 1024).rearrange("p (c h v) -> p c h v", c=2, h=H)
        s3 = slot_flat[3]
        Pm = region(s3, 0, 1024).rearrange("p (c h v) -> p c h v", c=2, h=H)
        CT = region(s3, 1024, 2048).rearrange("p (c b h v) -> p c b h v", c=2, b=2, h=H)
        WT = region(s3, 3072, 512).rearrange("p (c j t) -> p c j t", c=2, j=JT)
        STt = region(s3, 3840, 256).rearrange("p (j v) -> p j v", j=JT)
        fv2 = slot_flat[5]
        Vtok = region(fv2, 2048, 512)
        Yc = region(fv2, 2560, 512)
        Yq = region(fv2, 3072, 512)
        ST = region(fv2, 3584, JT * P).rearrange("p (j v) -> p j v", j=JT)
        STc = region(s3, 3584, JT * N).rearrange("p (j v) -> p j v", j=JT)
        ARf = AR[:, :, :, :].rearrange("p j c t -> p (j c t)")
        BKf = BK[:, :, :, :].rearrange("p j c t -> p (j c t)")
        hTf = hT[:, :, :].rearrange("p k t -> p (k t)")
        hrow = region(BKf, 0, 2 * D).rearrange("p (b d) -> p b d", b=2)
        junk = region(ARf, 0, D)
        xg = region(ARf, 0, 2 * D).rearrange("p (b d) -> p b d", b=2)
        xT = region(ARf, 2048, 2 * KT * NS).rearrange("p (b k s) -> p b k s", b=2, k=KT)
        hg = region(BKf, 0, 4 * NS).rearrange("p (b i s) -> p b i s", b=2, i=2)
        hl = region(BKf, 384, 4 * NS).rearrange("p (b i s) -> p b i s", b=2, i=2)
        hs = region(BKf, 768, 4 * NS).rearrange("p (b i s) -> p b i s", b=2, i=2)
        hm = region(BKf, 1152, 4 * NS).rearrange("p (b i s) -> p b i s", b=2, i=2)
        actT = region(BKf, 1536, 2 * FT * NS).rearrange("p (b f s) -> p b f s", b=2, f=FT)
        oTs = region(BKf, 3072, 8 * NS).rearrange("p (b i s) -> p b i s", b=2, i=4)
        ovcmp = region(BKf, 3072, NOVF * E).rearrange("p (o e) -> p o e", e=E)
        onehot = region(ARf, 3584, TT * TOPK * E).rearrange("p (t k e) -> p t k e", t=TT, e=E)
        ob = region(hTf, 0, 2 * D).rearrange("p (b d) -> p b d", b=2)
        gfin = region(hTf, 2048, D)
        outb = [region(hTf, 3072, D), region(hTf, 0, D)]
        b1rows = region(slot_flat[5], 0, F2)
        b2rows = region(slot_flat[5], F2, D)

        VR = {}
        vrow = 0
        for nm, src in (("g1", attn_norm_g), ("mu", mu), ("w0", w0), ("a0", a0), ("kk", k_k), ("ka", k_a),
                        ("rk", r_k), ("og", out_g), ("g2", ffn_norm_g)):
            n = 1
            for d in src.shape:
                n *= d
            VR[nm] = (vrow, n // P)
            vrow += n // P
        vec_rows = sb("vec_rows", [vrow, P])
        vecT = sb("vecT", [P, vrow + JT])

        def vec(nm, j=None):
            a, n = VR[nm]
            return vecT[:, a:a + n] if j is None else vecT[:, a + j:a + j + 1]

        one_minus_ka = vecT[:, vrow:vrow + JT]
        lnw = sb("lnw", [P, HW])
        lnb = sb("lnb", [P, HW])
        rw = sb("rw", [P, KT, E])
        rb = sb("rb", [P, E])
        fb = sb("fb", [P, H])
        wff = sb("wff", [P, KT, H])
        b1T = sb("b1T", [P, 2 * FT, E])
        b2T = sb("b2T", [P, KT, E])
        b1c = sb("b1c", [P, 2, 2 * FT])
        b2c = sb("b2c", [P, 2, KT])
        ident = sb("ident", [P, P])
        blk = sb("blk", [P, P])
        OFF = (TT - 1) * P
        stepm = sb("stepm", [P, OFF + T])
        maskSC = sb("maskSC", [P, 2 * C])
        levmask = sb("levmask", [C, LEVELS, C])
        reset = sb("reset", [P, NC, C])
        identb = sb("identb", [P, P], bf16)
        causal = sb("causal", [P, P], bf16)
        selh = sb("selh", [96, H, P], bf16)
        c3 = sb("c3", [96, T], bf16)
        ss = sb("ss", [P, TT])
        eps = sb("eps", [P, 2])
        rstd = sb("rstd", [P, TT])
        ffz = sb("ffz", [P, 5, TT, H])
        nmx = sb("nmx", [P, TT * H])
        rsum = sb("rsum", [P, TT * H])
        rrec = sb("rrec", [P, H])
        fst = sb("fst", [P, H])
        dend = sb("dend", [P, JT, NC])
        bonus = sb("bonus", [P, TT, H])
        gst = sb("gst", [P, 3, H])
        zero_i = sb("zero_i", [P, (NB + 2) * NS // P + 1], i32)
        iotaE = sb("iotaE", [P, E])
        iotaO = sb("iotaO", [P, NOVF])
        iotaEi = sb("iotaEi", [P, E], i32)
        iotaOi = sb("iotaOi", [P, NOVF], i32)
        tokid = sb("tokid", [P, TT], i32)
        lg = sb("lg", [P, TT, E])
        m8 = sb("m8", [P, TT, 8])
        i8 = sb("i8", [P, TT, 8], u32)
        i8f = sb("i8f", [P, TT, 8])
        Msel = sb("Msel", [P, TT, E])
        nm0 = sb("nm0", [P, TT])
        gate = sb("gate", [P, TT, TOPK])
        gsum = sb("gsum", [P, TT])
        cnt = sb("cnt", [P, E])
        rt = sb("rt", [P, 6, E])
        ovf_end = sb("ovf_end", [P, E])
        ovf_base = sb("ovf_base", [P, E])
        pos = sb("pos", [P, E])
        qd = sb("qd", [P, E])
        slotm = sb("slotm", [P, E])
        slotk = sb("slotk", [P, TOPK, E])
        slotf = sb("slotf", [P, TT, TOPK])
        sloti = sb("sloti", [P, TT, TOPK], i32)
        ovexp = sb("ovexp", [P, NOVF])
        blkexp = sb("blkexp", [P, NOVF], i32)
        pairs_f = sb("pairs_f", [P, 2])
        pairs_i = sb("pairs_i", [P, 1], i32)
        idx_all = sb("idx_all", [NS, NB + 2], i32)
        idx = sb("idx", [NS, 2], i32)

        bank = [ctx.enter_context(nc.psum_tensor(f"bank{b}", [P, 512], f32)) for b in range(8)]

        bank_full = [sem(f"bank_full{b}") for b in range(8)]
        bank_free = [sem(f"bank_free{b}") for b in range(8)]
        x_in = [sem(f"x_in{t}") for t in range(TT)]
        vec_in = sem("vec_in")
        bias_in = sem("bias_in")
        small_in = sem("small_in")
        w_in_loaded = [sem(f"w_in_loaded{s}") for s in range(2)]
        ff_in = sem("ff_in")
        w_out_loaded = [sem(f"w_out_loaded{s}") for s in range(2)]
        pool_step = sem("pool_step")
        consts_ready = sem("consts_ready")
        dve_step = sem("dve_step")
        act_step = sem("act_step")
        vec_ready = sem("vec_ready")
        hrow_ready = sem("hrow_ready")
        act_sq = sem("act_sq")
        sumsq_ready = sem("sumsq_ready")
        mixed = sem("mixed")
        lora_ready = sem("lora_ready")
        cum_ready = sem("cum_ready")
        kksq_ready = sem("kksq_ready")
        kksum_ready = sem("kksum_ready")
        kknorm_ready = sem("kknorm_ready")
        fox_ms_ready = sem("fox_ms_ready")
        fox_rms_ready = sem("fox_rms_ready")
        gn_var_ready = sem("gn_var_ready")
        gn_std_ready = sem("gn_std_ready")
        exps_ready = sem("exps_ready")
        elem_done = sem("elem_done")
        ffln_ready = sem("ffln_ready")
        nlf_ready = sem("nlf_ready")
        c3_ready = sem("c3_ready")
        negmax_ready = sem("negmax_ready")
        fo_ready = sem("fo_ready")
        values_done = sem("values_done")
        fox_o_free = sem("fox_o_free")
        scm_ready = sem("scm_ready")
        xt0_ready = sem("xt0_ready")
        ct_ready = sem("ct_ready")
        state_ready = sem("state_ready")
        y_ready = sem("y_ready")
        gates_ready = sem("gates_ready")
        gmax_ready = sem("gmax_ready")
        sel_ready = sem("sel_ready")
        slots_ready = sem("slots_ready")
        tables_ready = sem("tables_ready")
        zeros_stored = sem("zeros_stored")
        rows_zeroed = sem("rows_zeroed")
        tokens_stored = sem("tokens_stored")
        idx_in = sem("idx_in")
        h2_stored = [sem(f"h2_stored{t}") for t in range(TT)]
        idx_copied = sem("idx_copied")
        waited = sem("waited")
        xg_loaded = [sem(f"xg_loaded{q}") for q in range(2)]
        w_loaded = [sem(f"w_loaded{c}") for c in range(CH)]
        xt_full = sem("xt_full")
        xt_free = sem("xt_free")
        hid_full = [sem(f"hid_full{p}") for p in range(2)]
        hid_free = [sem(f"hid_free{p}") for p in range(2)]
        bias_ready = sem("bias_ready")
        glu_ready = sem("glu_ready")
        sig_ready = sem("sig_ready")
        lin_ready = sem("lin_ready")
        swi_ready = sem("swi_ready")
        act_ready = sem("act_ready")
        ot_full = [sem(f"ot_full{p}") for p in range(2)]
        ot_free = [sem(f"ot_free{p}") for p in range(2)]
        y_full = [sem(f"y_full{p}") for p in range(2)]
        y_free = [sem(f"y_free{p}") for p in range(2)]
        store_done = [sem(f"store_done{q}") for q in range(2)]
        gathered = [sem(f"gathered{t}") for t in range(TT)]
        gfin_in = sem("gfin_in")
        summed = sem("summed")
        normed = sem("normed")
        out_ready = sem("out_ready")
        out_stored = [sem(f"out_stored{t}") for t in range(TT)]

        plan, uses = {}, [0] * 8

        def put(name, b):
            plan[name] = (b, uses[b])
            uses[b] += 1

        U_ORDER = [12, 13, 14, 15, 0, 1, 2, 3, 4, 5, 6, 7, 8, 9, 10, 11, 16, 17, 18, 19, 20, 21]
        put(("vec",), 0)
        for tt in range(TT):
            for half in range(2):
                put(("hT", tt, half), (1 + 2 * tt + half) % 4)
        put(("b1",), 4)
        put(("b2",), 5)
        nrot = 0

        def rot(name):
            nonlocal nrot
            put(name, nrot % 8)
            nrot += 1

        for m in U_ORDER:
            rot(("u", m))
            if m == 3:
                for j in range(JT):
                    rot(("z", j))
                for j in range(JT):
                    rot(("a", j))
            if m == 11:
                for j in range(JT):
                    rot(("ss", j))
                for tt in range(TT):
                    rot(("g", tt))
        for tt in range(TT):
            rot(("fv", tt))
        rot(("ff",))
        rot(("bonus",))
        rot(("cT",))
        units = [(qb, h) for qb in range(TT) for h in range(H)]
        uses_before_fox = list(uses)
        for i, (qb, h) in enumerate(units):
            put(("S", qb, h), i % 2)
            put(("PT", qb, h), 2 + i % 2)
            if h == H - 1:
                put(("foT", qb), 6)
        for tt in range(TT):
            put(("vt", tt), 2)
            for c in range(2):
                put(("SC", tt, c, 0), 0)
                put(("SC", tt, c, 1), 1)
                for nm in ("bkt", "at", "mv", "X0"):
                    put((nm, tt, c), 4 + c)
                for lv in range(1, LEVELS):
                    put(("P", tt, c, lv), 4 + c)
                    put(("XT", tt, c, lv), 4 + c)
                    if lv < LEVELS - 1:
                        put(("X", tt, c, lv), 4 + c)
                put(("W", tt, c), 4 + c)
                put(("U", tt, c), 6)
                put(("state", tt, c), 6)
            put(("Y", tt), 7)
            put(("yT", tt), 3)
        for tt in range(TT):
            for half in range(2):
                put(("o", tt, half), 2 * tt % 4 + half)
        for tt in range(TT):
            for half in range(2):
                put(("h2T", tt, half), 4 + half)
        for tt in range(TT):
            put(("lg", tt), 6)
        put(("cnt",), 7)
        for tt in range(TT):
            put(("pos", tt), tt % 2)

        def filled(eng, *name):
            b, n = plan[name]
            eng.wait_ge(bank_full[b], n + 1)

        def emptied(eng, *name):
            b, n = plan[name]
            eng.wait_ge(bank_free[b], n + 1)

        def free_of(name):
            return bank_free[plan[name][0]]

        def every_other(ap, s):
            return ap.rearrange("p (f s) -> p f s", s=2)[:, :, s]

        block = ctx.enter_context(nc.Block())

        W_CHUNKS = [3, 0, 1, 2, 4, 5, 6]
        W1_T = w1[0].rearrange("e (k p) f -> p e k f", p=P)
        W2_T = w2[0].rearrange("e (k p) f -> p e k f", p=P)

        def load_expert_chunk(eng, e, c):
            src, off = (W1_T, c * CW) if c < W1C else (W2_T, (c - W1C) * CW)
            eng.dma_start(slots[:, c], src[:, bass.ds(e, 1), :, off:off + CW].rearrange("p a k f -> p (a k) f"))\
               .then_inc(w_loaded[c], 16)

        @block.sync
        def _(sp):
            for tt in range(TT):
                sp.dma_start(xs[:, tt, :], x[0, tt * P:(tt + 1) * P, :]).then_inc(x_in[tt], 16)
            w_in_v = w_in[0].rearrange("(k p) f -> p k f", p=P)
            for n, ch in enumerate(W_CHUNKS):
                if n >= 2:
                    filled(sp, "u", [m for m in U_ORDER if m // 4 == W_CHUNKS[n - 2]][-1])
                lo = ch * CW
                if ch == 5:
                    sp.dma_start(slots[:, n % 2, :, 0:256], w_in_v[:, :, lo:lo + 256]).then_inc(w_in_loaded[n % 2], 16)
                elif ch == 6:
                    sp.dma_start(slots[:, n % 2], w_in_v[:, :, lo - 256:lo + 256]).then_inc(w_in_loaded[n % 2], 16)
                else:
                    sp.dma_start(slots[:, n % 2], w_in_v[:, :, lo:lo + CW]).then_inc(w_in_loaded[n % 2], 16)
            w_out_v = w_out[0].rearrange("(k p) f -> p k f", p=P)
            for half in range(2):
                if half == 0:
                    filled(sp, "fv", TT - 1)
                else:
                    filled(sp, "u", U_ORDER[-1])
                sp.dma_start(slots[:, half], w_out_v[:, :, half * CW:(half + 1) * CW]).then_inc(w_out_loaded[half], 16)
            filled(sp, "yT", TT - 1)
            emptied(sp, "state", TT - 1, 1)
            sp.wait_ge(state_ready, NC + 1)
            for c in range(2, CH):
                load_expert_chunk(sp, 0, c)
            for c in range(2):
                filled(sp, "o", TT - 1, c)
                load_expert_chunk(sp, 0, c)

            def next_expert(b, e):
                for c in range(CH):
                    if c < W1C:
                        sp.wait_ge(hid_full[c % 2], b * 2 + (c // 2 - 1))
                    else:
                        sp.wait_ge(ot_full[c - W1C], b)
                    load_expert_chunk(sp, e, c)

            with sp.Fori(1, E) as b:
                next_expert(b, b)
            sp.wait_ge(tables_ready, 1)
            npairs = sp.value_load(pairs_i[0:1, 0:1], min_val=E // 2, max_val=NB // 2)
            with sp.Fori(E // 2, NB // 2) as i:
                with sp.If(i < npairs):
                    for q in range(2):
                        e = sp.value_load(blkexp[0:1, bass.ds(i * 2 + (q - E), 1)], min_val=0, max_val=E - 1)
                        next_expert(i * 2 + q, e)
            for tt in range(TT):
                sp.wait_ge(out_ready, tt + 1)
                sp.dma_start(out[0, tt * P:(tt + 1) * P, :], outb[tt % 2]).then_inc(out_stored[tt], 16)
            for tt in range(TT):
                sp.wait_ge(out_stored[tt], 16)

        @block.gpsimd
        def _(pool):
            steps = [0]

            def step(ins):
                steps[0] += 1
                ins.then_inc(pool_step, 1)
                pool.wait_ge(pool_step, steps[0])

            def select(dst, pattern, op, fill, base, cm):
                step(nc.gpsimd.affine_select(out=dst, in_=dst, compare_op=op, fill=fill, base=base,
                                             pattern=pattern, channel_multiplier=cm))

            step(nc.gpsimd.memset(eps[:, 0:1], RMS_EPS))
            step(nc.gpsimd.memset(eps[:, 1:2], GN_EPS))
            step(nc.gpsimd.memset(ident[:, :], 0.0))
            select(ident[:, :], [[-1, P]], ALU.not_equal, 1.0, 0, 1)
            pool.sem_inc(consts_ready, 1)
            step(nc.gpsimd.memset(shiftbuf[:, :, 0:1], 0.0))
            step(nc.gpsimd.memset(blk[:, :], 0.0))
            step(nc.gpsimd.memset(blk[0:N, 0:N], 1.0))
            step(nc.gpsimd.memset(blk[N:P, N:P], 1.0))
            step(nc.gpsimd.memset(reset[:, :, :], 1.0))
            step(nc.gpsimd.memset(reset[:, :, 0:1], 0.0))
            pool.sem_inc(consts_ready, 1)
            step(nc.gpsimd.memset(zrow, 0.0))
            for o in range(NOVF):
                pool.dma_start(expert_rows[(E + o) * NS:(E + o + 1) * NS, :], zrow[0:NS, :]).then_inc(rows_zeroed, 16)
            step(nc.gpsimd.memset(stepm[:, :], 1.0))
            select(stepm[:, :], [[1, OFF + T]], ALU.is_ge, 0.0, -OFF, -1)
            step(nc.gpsimd.memset(identb[:, :], 0.0))
            select(identb[:, :], [[-1, P]], ALU.not_equal, 1.0, 0, 1)
            step(nc.gpsimd.memset(causal[:, :], 0.0))
            select(causal[:, :], [[-1, P]], ALU.is_ge, -1e30, 0, 1)
            step(nc.gpsimd.memset(selh[:, :, :], 0.0))
            for g in range(3):
                select(selh[:, :, :], [[-1, H], [0, P]], ALU.not_equal, 1.0, -32 * g, 1)
            step(nc.gpsimd.memset(c3[:, :], 0.0))
            step(nc.gpsimd.memset(maskSC[:, :], 1.0))
            for s in range(2):
                select(maskSC[s * C:(s + 1) * C, 0:C], [[1, C]], ALU.is_ge, 0.0, -1, -1)
                select(maskSC[s * C:(s + 1) * C, C:2 * C], [[1, C]], ALU.is_ge, 0.0, 0, -1)
            step(nc.gpsimd.memset(blocks[:, :, :], 1.0))
            for lv in range(LEVELS):
                w = 1 << lv
                select(blocks[:, lv, :], [[-w, C // w], [0, w]], ALU.is_ge, 0.0, 0, 1)
                select(blocks[:, lv, :], [[w, C // w], [0, w]], ALU.is_ge, 0.0, w - 1, -1)
            step(nc.gpsimd.tensor_tensor(levmask[:, :, :], blocks[:, 1:, :], blocks[:, 0:LEVELS, :], ALU.subtract))
            pool.sem_inc(consts_ready, 1)
            step(nc.gpsimd.iota(iotaEi[:, :], pattern=[[1, E]], base=0, channel_multiplier=0))
            step(nc.gpsimd.iota(iotaOi[:, :], pattern=[[1, NOVF]], base=0, channel_multiplier=0))
            step(nc.gpsimd.iota(tokid[:, :], pattern=[[P, TT]], base=0, channel_multiplier=1))
            step(nc.gpsimd.tensor_copy(iotaE[:, :], iotaEi[:, :]))
            step(nc.gpsimd.tensor_copy(iotaO[:, :], iotaOi[:, :]))
            step(nc.gpsimd.memset(zero_i[:, :], 0))
            pool.sem_inc(consts_ready, 1)
            nrow = (NB + 2) * NS // P
            pool.dma_start(slot_tokens.rearrange("(p n) a -> p (n a)", p=P), zero_i[:, 0:nrow]).then_inc(zeros_stored, 16)

            for tt in range(TT):
                for lv in range(1, LEVELS):
                    for c in range(2):
                        pool.wait_ge(scm_ready, 2 * tt + c + 1)
                        if lv > 2:
                            filled(pool, "P", tt, c, lv - 2)
                        elif tt > 0:
                            filled(pool, "P", tt - 1, c, LEVELS - lv)
                        nc.gpsimd.tensor_tensor(
                            CT[0:C, c, lv % 2], SCm[0:C, c, :, 0:C],
                            levmask[:, lv, :].unsqueeze(1).to_broadcast([C, H, C]), ALU.mult).then_inc(ct_ready, 1)

            pool.wait_ge(zeros_stored, 16)
            for tt in range(TT):
                pool.wait_ge(slots_ready, tt + 1)
                for k in range(TOPK):
                    pool.indirect_dma_start(
                        slot_tokens, bass.IndirectOffsetOnAxis(ap=sloti[:, tt, k:k + 1], axis=0),
                        tokid[:, tt:tt + 1], None).then_inc(tokens_stored, 16)
            pool.wait_ge(tokens_stored, 16 * TT * TOPK)
            pool.dma_start(idx_all[:, :], slot_tokens.rearrange("(b s) a -> s (b a)", s=NS),
                           allow_slow_non_contiguous=True).then_inc(idx_in, 16)
            pool.wait_ge(idx_in, 16)
            for tt in range(TT):
                pool.wait_ge(h2_stored[tt], 16)

            def gather(b, q, reused=True):
                if reused:
                    pool.wait_ge(xt_full, b)
                    pool.sem_inc(waited, 1)
                nc.gpsimd.tensor_copy(idx[:, q:q + 1], idx_all[:, bass.ds(b, 1)]).then_inc(idx_copied, 1)
                pool.wait_ge(idx_copied, b + 1)
                pool.sem_inc(waited, 1)
                pool.indirect_dma_start(xg[0:NS, q, :], None, h2_rows,
                                        bass.IndirectOffsetOnAxis(ap=idx[:, q:q + 1], axis=0))\
                    .then_inc(xg_loaded[q], 16)

            gather(0, 0, False)
            with pool.Fori(0, E // 2) as i:
                gather(i * 2 + 1, 1)
                gather(i * 2 + 2, 0)
            npairs = pool.value_load(pairs_i[0:1, 0:1], min_val=E // 2, max_val=NB // 2)
            with pool.Fori(E // 2, NB // 2) as i:
                with pool.If(i < npairs):
                    gather(i * 2 + 1, 1)
                    gather(i * 2 + 2, 0)
            for q in range(2):
                pool.wait_ge(store_done[q], npairs * 16 + 16)
            pool.sem_inc(waited, 1)
            for tt in range(TT):
                for k in range(TOPK):
                    pool.indirect_dma_start(
                        slots[:, tt, 2 * k:2 * k + 2, :].rearrange("p a f -> p (a f)"), None, expert_rows,
                        bass.IndirectOffsetOnAxis(ap=sloti[:, tt, k:k + 1], axis=0)).then_inc(gathered[tt], 16)

        def fox_rms(act, qb):
            act.wait_ge(fox_ms_ready, qb + 1)
            nc.scalar.activation(fst[:, :], fst[:, :], ACT.Sqrt, bias=eps[:, 0:1], scale=1.0 / N).then_inc(fox_rms_ready, 1)

        def fox_out_T(act, qb):
            filled(act, "foT", qb)
            for j in range(JT):
                ins = nc.scalar.mul(hT[:, JT + j, qb * P:(qb + 1) * P], bank[6][:, j * P:(j + 1) * P], vec("og", j))
            ins.then_inc(free_of(("foT", qb)), 1)

        @block.scalar
        def _(act):
            at = 0
            for src in (attn_norm_g, mu, w0, a0, k_k, k_a, None, out_g, ffn_norm_g):
                v = r_k[0].rearrange("h n -> (h n)") if src is None else src[0]
                n = v.shape[0] // P
                act.dma_start(vec_rows[at:at + n, :], v.rearrange("(j p) -> j p", p=P)).then_inc(vec_in, 16)
                at += n
            act.dma_start(wff[:, :, :], w_in[0, :, w_in.shape[2] - H:].rearrange("(k p) f -> p k f", p=P)).then_inc(ff_in, 16)
            act.dma_start(b1rows[0:E, :], b1[0]).then_inc(bias_in, 16)
            act.dma_start(b2rows[0:E, :], b2[0]).then_inc(bias_in, 16)
            act.dma_start(lora_up[0:LORA, :], w_up[0]).then_inc(small_in, 16)
            act.dma_start(lora_up[LORA:P, :], a_up[0]).then_inc(small_in, 16)
            act.dma_start(gup, g_up[0]).then_inc(small_in, 16)
            act.dma_start(lnw[:, :], ln_w.to_broadcast([P, HW])).then_inc(small_in, 16)
            act.dma_start(lnb[:, :], ln_b.to_broadcast([P, HW])).then_inc(small_in, 16)
            act.dma_start(rw[:, :, :], router_w[0].rearrange("(k p) e -> p k e", p=P)).then_inc(small_in, 16)
            act.dma_start(rb[:, :], router_b.to_broadcast([P, E])).then_inc(small_in, 16)
            act.dma_start(fb[:, :], f_bias.to_broadcast([P, H])).then_inc(small_in, 16)
            steps = [0]

            def step(ins):
                steps[0] += 1
                ins.then_inc(act_step, 1)
                act.wait_ge(act_step, steps[0])

            def root_mean(tt, n, done):
                act.wait_ge(act_sq, n)
                nc.scalar.activation(ss[:, tt:tt + 1], ss[:, tt:tt + 1], ACT.Sqrt, bias=eps[:, 0:1], scale=1.0 / D)\
                    .then_inc(done, 1)

            act.wait_ge(consts_ready, 1)
            for tt in range(TT):
                act.wait_ge(x_in[tt], 16)
                nc.scalar.activation(junk, xs[:, tt, :], ACT.Square, accum_out=ss[:, tt:tt + 1]).then_inc(act_sq, 1)
                root_mean(tt, tt + 1, sumsq_ready)
            filled(act, "b1")
            nc.scalar.copy(b1T[:, :, :], bank[4][:, 0:2 * FT * E].rearrange("p (j e) -> p j e", e=E)).then_inc(free_of(("b1",)), 1)
            filled(act, "b2")
            nc.scalar.copy(b2T[:, :, :], bank[5][:, 0:KT * E].rearrange("p (j e) -> p j e", e=E)).then_inc(free_of(("b2",)), 1)
            act.wait_ge(vec_ready, 1)
            act.wait_ge(consts_ready, 3)
            nth = 0
            for m in U_ORDER:
                filled(act, "u", m)
                src = bank[plan[("u", m)][0]][:, :]
                if m < 14:
                    if nth >= 2:
                        act.wait_ge(mixed, nth - 1)
                    nc.scalar.copy(shiftbuf[:, nth % 2, 1:T + 1], src).then_inc(free_of(("u", m)), 1)
                    nth += 1
                elif m < 18:
                    nc.scalar.mul(qk[:, 0, m - 14, :], src, float(N) ** -0.5).then_inc(free_of(("u", m)), 1)
                else:
                    nc.scalar.copy(qk[:, 1, m - 18, :], src).then_inc(free_of(("u", m)), 1)
                if m == 13:
                    act.wait_ge(mixed, 2)
                    step(nc.scalar.activation(wa[0:LORA, :], wa[0:LORA, :], ACT.Tanh))
                    step(nc.scalar.activation(gl, gl, ACT.Sigmoid))
                    act.sem_inc(lora_ready, 1)
                if m == 3:
                    act.wait_ge(rows_zeroed, 16 * NOVF)
                    for nm, dst, bias in (("z", decay_s, "w0"), ("a", aT, "a0")):
                        for j in range(JT):
                            filled(act, nm, j)
                            nc.scalar.activation(dst[:, j, :], bank[plan[(nm, j)][0]][:, :], ACT.Sigmoid,
                                                 bias=vec(bias, j)).then_inc(free_of((nm, j)), 1)
                if m == 11:
                    for j in range(JT):
                        act.wait_ge(kksum_ready, j + 1)
                        nc.scalar.activation(AR[:, j, :, 0:C], AR[:, j, :, 0:C], ACT.Sqrt).then_inc(kknorm_ready, 1)
                    for tt in range(TT):
                        filled(act, "g", tt)
                        nc.scalar.copy(G[:, tt, :], bank[plan[("g", tt)][0]][:, :]).then_inc(free_of(("g", tt)), 1)
                    for j in range(JT):
                        act.wait_ge(cum_ready, j + 1)
                        step(nc.scalar.activation(decay_e[:, j, :], decay_c[:, j, :], ACT.Exp, scale=-KAPPA))
                        step(nc.scalar.activation(decay_c[:, j, :], decay_c[:, j, :], ACT.Exp, scale=KAPPA))
                        nc.scalar.activation(decay_s[:, j, :], decay_s[:, j, :], ACT.Exp, scale=-KAPPA).then_inc(exps_ready, 1)
            for tt in range(TT):
                filled(act, "fv", tt)
                nc.scalar.copy(foxv[:, tt, :], bank[plan[("fv", tt)][0]][:, :]).then_inc(free_of(("fv", tt)), 1)
            emptied(act, "ff")
            step(nc.scalar.activation(ffz[:, 1], ffz[:, 0], ACT.Abs))
            step(nc.scalar.activation(ffz[:, 2], ffz[:, 1], ACT.Exp, scale=-1.0))
            nc.scalar.activation(ffz[:, 3], ffz[:, 2], ACT.Ln, bias=1.0).then_inc(ffln_ready, 1)
            filled(act, "bonus")
            nc.scalar.copy(bonus[:, :, :], bank[plan[("bonus",)][0]][:, 0:TT * H].rearrange("p (t h) -> p t h", h=H))\
                .then_inc(free_of(("bonus",)), 1)
            act.wait_ge(elem_done, JT)
            for i, (qb, h) in enumerate(units):
                keys = (qb + 1) * P
                act.wait_ge(negmax_ready, i + 1)
                if i >= 2:
                    filled(act, "PT", *units[i - 2])
                nc.scalar.activation(fP[:, i % 2, 0:keys], bank[i % 2][:, 0:keys], ACT.Exp, bias=nmx[:, i:i + 1],
                                     accum_out=rsum[:, i:i + 1]).then_inc(free_of(("S", qb, h)), 1)
                if h == 1 and qb > 0:
                    fox_rms(act, qb - 1)
                if h == 2 and qb > 0:
                    fox_out_T(act, qb - 1)
            fox_rms(act, TT - 1)
            fox_out_T(act, TT - 1)

            def move(name, dst, src):
                filled(act, *name)
                nc.scalar.copy(dst, src).then_inc(free_of(name), 1)

            def head_view(b, parts=C):
                return bank[b][0:parts, :].rearrange("p (h v) -> p h v", h=H)

            for tt in range(TT):
                filled(act, "vt", tt)
                if tt > 0:
                    act.wait_ge(y_ready, tt)
                    filled(act, "Y", tt - 1)
                for c in range(2):
                    step(nc.scalar.copy(UV[C:P, c], bank[2][c * C:(c + 1) * C, :].rearrange("p (h v) -> p h v", h=H)))
                nc.scalar.copy(Vtok, bank[2][:, :]).then_inc(free_of(("vt", tt)), 1)
                for c in range(2):
                    b = 4 + c
                    move(("bkt", tt, c), BKtok[:, c], head_view(b, P))
                    move(("at", tt, c), Atok[0:C, c], head_view(b))
                for c in range(2):
                    b = 4 + c
                    move(("mv", tt, c), MV[0:C, c], head_view(b))
                    move(("X0", tt, c), Xm[0:C, c], head_view(b))
                for lv in range(1, LEVELS):
                    for c in range(2):
                        move(("P", tt, c, lv), Pm[0:C, c], head_view(4 + c))
                    if lv < LEVELS - 1:
                        for c in range(2):
                            move(("X", tt, c, lv), Xm[0:C, c], head_view(4 + c))
                for c in range(2):
                    move(("W", tt, c), WT[:, c], bank[4 + c][:, 0:JT * C].rearrange("p (j t) -> p j t", j=JT))
                act.wait_ge(gn_var_ready, tt + 1)
                nc.scalar.activation(gst[:, 1, :], gst[:, 1, :], ACT.Sqrt, bias=eps[:, 1:2], scale=1.0 / N)\
                    .then_inc(gn_std_ready, 1)
                filled(act, "yT", tt)
                nc.scalar.copy(hT[:, 0:JT, tt * P:(tt + 1) * P],
                               bank[3][:, :].rearrange("p (j t) -> p j t", j=JT)).then_inc(free_of(("yT", tt)), 1)
            for tt in range(TT):
                emptied(act, "o", tt, 1)
                emptied(act, "o", tt, 0)
                nc.scalar.activation(junk, xs[:, tt, :], ACT.Square, accum_out=ss[:, tt:tt + 1]).then_inc(act_sq, 1)
                root_mean(tt, TT + tt + 1, sumsq_ready)
            for tt in range(TT):
                act.wait_ge(hrow_ready, TT + tt + 1)
                act.dma_start(h2_rows[tt * P:(tt + 1) * P, :], hrow[:, tt % 2, :]).then_inc(h2_stored[tt], 16)
            for tt in range(TT):
                act.wait_ge(gmax_ready, tt + 1)
                nc.scalar.activation(gate[:, tt, :], m8[:, tt, 0:TOPK], ACT.Exp, bias=nm0[:, tt:tt + 1],
                                     accum_out=gsum[:, tt:tt + 1]).then_inc(gates_ready, 1)

            def block_work(i, q):
                b = i * 2 + q
                for c in range(W1C):
                    act.wait_ge(glu_ready, b * W1C + (c + 1))
                    nc.scalar.activation(hs[:, c % 2], hg[:, c % 2], ACT.Sigmoid, scale=1.702).then_inc(sig_ready, 1)
                act.wait_ge(bias_ready, b + 1)
                for h in range(2):
                    act.wait_ge(ot_full[h], b + 1)
                    for t in range(4):
                        ins = nc.scalar.activation(oTs[:, h, t], bank[4 + h][:, t * NS:(t + 1) * NS], ACT.Identity,
                                                   bias=b2c[:, q, 4 * h + t:4 * h + t + 1])
                    ins.then_inc(ot_free[h], 1)
                act.wait_ge(store_done[q], i * 16 + 16)
                for h in range(2):
                    act.wait_ge(y_full[h], b + 1)
                    nc.scalar.copy(ob[0:NS, q, h * CW:(h + 1) * CW], bank[6 + h][0:NS, :]).then_inc(y_free[h], 1)
                for h in range(2):
                    act.wait_ge(y_free[h], b + 2)
                act.dma_start(expert_rows[bass.ds(b * NS, NS), :], ob[0:NS, q, :]).then_inc(store_done[q], 16)

            act.wait_ge(tables_ready, 1)
            for q in range(2):
                act.sem_inc(ot_free[q], 1)
                act.sem_inc(y_free[q], 1)
                act.sem_inc(store_done[q], 16)
            with act.Fori(0, E // 2) as i:
                for q in range(2):
                    block_work(i, q)
            npairs = act.value_load(pairs_i[0:1, 0:1], min_val=E // 2, max_val=NB // 2)
            with act.Fori(E // 2, NB // 2) as i:
                with act.If(i < npairs):
                    for q in range(2):
                        block_work(i, q)
            act.dma_start(gfin, final_norm_g.rearrange("(a d) -> a d", a=1).to_broadcast([P, D])).then_inc(gfin_in, 16)
            for tt in range(TT):
                act.wait_ge(summed, tt + 1)
                nc.scalar.activation(junk, xs[:, tt, :], ACT.Square, accum_out=ss[:, tt:tt + 1]).then_inc(act_sq, 1)
                root_mean(tt, 2 * TT + tt + 1, normed)

        @block.tensor
        def _(pe):
            def begin(*name):
                b, n = plan[name]
                if n > 0:
                    pe.wait_ge(bank_free[b], n)
                return bank[b]

            def end(ins, *name):
                ins.then_inc(bank_full[plan[name][0]], 1)

            pe.wait_ge(consts_ready, 1)
            pe.wait_ge(vec_in, 16 * 9)
            ps = begin("vec")
            end(nc.tensor.transpose(ps[:, 0:vrow], vec_rows[:, :], ident[0:vrow, 0:vrow]), "vec")
            for tt in range(TT):
                pe.wait_ge(hrow_ready, tt + 1)
                for half in range(2):
                    ps = begin("hT", tt, half)
                    for k in range(4):
                        o = (half * 4 + k) * P
                        ins = nc.tensor.transpose(ps[:, k * P:(k + 1) * P], hrow[:, tt % 2, o:o + P], ident[:, :])
                    end(ins, "hT", tt, half)
            pe.wait_ge(bias_in, 32)
            ps = begin("b1")
            for j in range(FT):
                for s in range(2):
                    n = 2 * j + s
                    ins = nc.tensor.transpose(ps[:, n * E:(n + 1) * E], every_other(b1rows[0:E, 2 * j * P:2 * (j + 1) * P], s),
                                              ident[0:E, 0:E])
            end(ins, "b1")
            ps = begin("b2")
            for j in range(KT):
                ins = nc.tensor.transpose(ps[:, j * E:(j + 1) * E], b2rows[0:E, j * P:(j + 1) * P], ident[0:E, 0:E])
            end(ins, "b2")

            for tt in range(TT):
                emptied(pe, "hT", tt, 0)
                emptied(pe, "hT", tt, 1)
            pe.wait_ge(small_in, 16 * 8)
            chunk = -1
            for nth, m in enumerate(U_ORDER):
                ch = m // 4
                if nth == 0 or U_ORDER[nth - 1] // 4 != ch:
                    chunk += 1
                    pe.wait_ge(w_in_loaded[chunk % 2], 16 * (chunk // 2 + 1))
                ps = begin("u", m)
                col = (m % 4) * P
                for k in range(KT):
                    ins = nc.tensor.matmul(ps[:, :], slots[:, chunk % 2, k, col:col + P], hT[:, k, :],
                                           start=(k == 0), stop=(k == KT - 1))
                end(ins, "u", m)
                if m == 3:
                    pe.wait_ge(lora_ready, 1)
                    for nm, lo in (("z", 0), ("a", LORA)):
                        for j in range(JT):
                            ps = begin(nm, j)
                            end(nc.tensor.matmul(ps[:, :], lora_up[lo:lo + LORA, j * P:(j + 1) * P],
                                                 wa[lo:lo + LORA, :], start=True, stop=True), nm, j)
                if m == 11:
                    for j in range(JT):
                        ps = begin("ss", j)
                        pe.wait_ge(kksq_ready, j + 1)
                        end(nc.tensor.matmul(ps[:, :], blk[:, :], AR[:, j, :, 0:C], start=True, stop=True), "ss", j)
                    for tt in range(TT):
                        ps = begin("g", tt)
                        end(nc.tensor.matmul(ps[:, :], gl[:, tt * P:(tt + 1) * P], gup, start=True, stop=True), "g", tt)
            chunk += 1
            pe.wait_ge(w_in_loaded[chunk % 2], 16 * (chunk // 2 + 1))
            for tt in range(TT):
                ps = begin("fv", tt)
                for k in range(KT):
                    ins = nc.tensor.matmul(ps[:, :], hT[:, k, tt * P:(tt + 1) * P], slots[:, chunk % 2, k, :],
                                           start=(k == 0), stop=(k == KT - 1))
                end(ins, "fv", tt)
            pe.wait_ge(ff_in, 16)
            ps = begin("ff")
            for tt in range(TT):
                for k in range(KT):
                    ins = nc.tensor.matmul(ps[:, tt * H:(tt + 1) * H], hT[:, k, tt * P:(tt + 1) * P], wff[:, k, :],
                                           start=(k == 0), stop=(k == KT - 1))
            end(ins, "ff")
            pe.wait_ge(elem_done, JT)
            ps = begin("bonus")
            for tt in range(TT):
                for j in range(JT):
                    ins = nc.tensor.matmul(ps[:, tt * H + 2 * j:tt * H + 2 * j + 2], aT[:, j, tt * P:(tt + 1) * P],
                                           blk[:, 0:P:N], start=True, stop=True)
            end(ins, "bonus")
            pe.wait_ge(nlf_ready, 1)
            pe.wait_ge(consts_ready, 3)
            ps = begin("cT")
            for tt in range(TT):
                o = OFF - tt * P
                ins = nc.tensor.matmul(ps[0:H, :], ffz[:, 4, tt, :], stepm[:, o:o + T], start=(tt == 0), stop=(tt == TT - 1))
            end(ins, "cT")

            pe.wait_ge(c3_ready, 1)
            for tt in range(TT):
                emptied(pe, "fv", tt)
            for m in range(14, 22):
                emptied(pe, "u", m)

            def scores(i):
                qb, h = units[i]
                j, lo = h // 2, (h % 2) * N
                keys = (qb + 1) * P
                ps = begin("S", qb, h)
                nc.tensor.matmul(ps[:, 0:keys], qk[lo:lo + N, 0, j, qb * P:(qb + 1) * P], qk[lo:lo + N, 1, j, 0:keys],
                                 start=True, stop=False)
                nc.tensor.matmul(ps[:, qb * P:keys], identb[:, :], causal[:, :], start=False, stop=False,
                                 skip_group_check=True)
                end(nc.tensor.matmul(ps[:, 0:keys], selh[:, h, :], c3[:, 0:keys], start=False, stop=True), "S", qb, h)

            def transposes(i):
                qb, h = units[i]
                ps = begin("PT", qb, h)
                emptied(pe, "S", qb, h)
                for kb in range(qb + 1):
                    ins = nc.tensor.transpose(ps[:, kb * P:(kb + 1) * P], fP[:, i % 2, kb * P:(kb + 1) * P], ident[:, :])
                end(ins, "PT", qb, h)

            def values(i):
                qb, h = units[i]
                ps = bank[4 + qb % 2]
                if h == 0 and qb < 2:
                    pe.wait_ge(bank_free[4 + qb], uses_before_fox[4 + qb])
                elif h == 0:
                    pe.wait_ge(fox_o_free, qb - 1)
                emptied(pe, "PT", qb, h)
                for kb in range(qb + 1):
                    ins = nc.tensor.matmul(ps[:, h * N:(h + 1) * N], fPT[:, i % 2, kb * P:(kb + 1) * P],
                                           foxv[:, kb, h * N:(h + 1) * N], start=(kb == 0), stop=(kb == qb))
                ins.then_inc(values_done, 1)

            def fo_transposes(qb):
                ps = begin("foT", qb)
                pe.wait_ge(fo_ready, qb + 1)
                for j in range(JT):
                    ins = nc.tensor.transpose(ps[:, j * P:(j + 1) * P], fo[:, qb % 2, j * P:(j + 1) * P], ident[:, :])
                end(ins, "foT", qb)

            for i in range(len(units) + 2):
                if i < len(units):
                    scores(i)
                if 1 <= i <= len(units):
                    transposes(i - 1)
                if i >= 2:
                    values(i - 2)
                if i >= 4 and (i - 4) % H == H - 1:
                    fo_transposes((i - 4) // H)
            fo_transposes(TT - 1)

            pe.wait_ge(fox_o_free, TT)
            heads = [(h, h // 2, (h % 2) * N) for h in range(H)]
            for tt in range(TT):
                ps = begin("vt", tt)
                for j in range(JT):
                    ins = nc.tensor.transpose(ps[:, j * P:(j + 1) * P], vT[:, j, tt * P:(tt + 1) * P], ident[:, :])
                end(ins, "vt", tt)
                for c in range(2):
                    cc = 2 * tt + c
                    for g in range(2):
                        ps = begin("SC", tt, c, g)
                        for h, j, lo in heads[g::2]:
                            ins = nc.tensor.matmul(ps[:, j * P:(j + 1) * P], BK[lo:lo + N, j, cc, :],
                                                   AR[lo:lo + N, j, cc, :], start=True, stop=True)
                        end(ins, "SC", tt, c, g)
                    ps = begin("bkt", tt, c)
                    for j in range(JT):
                        ins = nc.tensor.transpose(ps[:, j * P:(j + 1) * P], BK[:, j, cc, :], ident[:, :])
                    end(ins, "bkt", tt, c)
                    ps = begin("at", tt, c)
                    for j in range(JT):
                        ins = nc.tensor.transpose(ps[0:C, j * P:(j + 1) * P], AR[:, j, cc, 0:C], ident[:, :])
                    end(ins, "at", tt, c)
                emptied(pe, "vt", tt)
                for c in range(2):
                    ps = begin("mv", tt, c)
                    pe.wait_ge(scm_ready, 2 * tt + c + 1)
                    for h, j, lo in heads:
                        ins = nc.tensor.matmul(ps[0:C, h * N:(h + 1) * N], SCm[C:P, c, h, 0:C], UV[C:P, c, h, :],
                                               start=True, stop=True)
                    end(ins, "mv", tt, c)
                    ps = begin("X0", tt, c)
                    pe.wait_ge(xt0_ready, 2 * tt + c + 1)
                    for h in range(H):
                        ins = nc.tensor.transpose(ps[0:C, h * C:(h + 1) * C], XT[0:C, c, h, :], ident[0:C, 0:C])
                    end(ins, "X0", tt, c)
                for lv in range(1, LEVELS):
                    for c in range(2):
                        ps = begin("P", tt, c, lv)
                        pe.wait_ge(ct_ready, (tt * (LEVELS - 1) + lv - 1) * 2 + c + 1)
                        for h in range(H):
                            ins = nc.tensor.matmul(ps[0:C, h * C:(h + 1) * C], CT[0:C, c, lv % 2, h, :], Xm[0:C, c, h, :],
                                                   start=True, stop=True)
                        end(ins, "P", tt, c, lv)
                    for c in range(2):
                        ps = begin("XT", tt, c, lv)
                        for h in range(H):
                            ins = nc.tensor.matmul(ps[0:C, h * C:(h + 1) * C], Pm[0:C, c, h, :], XT[0:C, c, h, :],
                                                   start=True, stop=True)
                        end(ins, "XT", tt, c, lv)
                    if lv < LEVELS - 1:
                        for c in range(2):
                            ps = begin("X", tt, c, lv)
                            for h in range(H):
                                ins = nc.tensor.transpose(ps[0:C, h * C:(h + 1) * C], XT[0:C, c, h, :], ident[0:C, 0:C])
                            end(ins, "X", tt, c, lv)
                for c in range(2):
                    ps = begin("W", tt, c)
                    for h, j, lo in heads:
                        ins = nc.tensor.matmul(ps[lo:lo + N, j * C:(j + 1) * C], Atok[0:C, c, h, :], XT[0:C, c, h, :],
                                               start=True, stop=True)
                    end(ins, "W", tt, c)
                psy = begin("Y", tt)
                for c in range(2):
                    cc = 2 * tt + c
                    ps = begin("U", tt, c)
                    emptied(pe, "W", tt, c)
                    pe.wait_ge(state_ready, cc + 1)
                    for j in range(JT):
                        nc.tensor.matmul(ps[0:C, j * P:(j + 1) * P], WT[:, c, j, :], ST[:, j, :],
                                         start=(j == 0), stop=False, skip_group_check=True)
                    for h in range(H):
                        ins = nc.tensor.matmul(ps[0:C, h * N:(h + 1) * N], XT[0:C, c, h, :], MV[0:C, c, h, :],
                                               start=False, stop=True, skip_group_check=True)
                    end(ins, "U", tt, c)
                    for j in range(JT):
                        nc.tensor.matmul(psy[c * C:(c + 1) * C, j * P:(j + 1) * P], AR[:, j, cc, C:2 * C], ST[:, j, :],
                                         start=(j == 0), stop=False, skip_group_check=True)
                    ps = begin("state", tt, c)
                    for h, j, lo in heads:
                        ins = nc.tensor.matmul(ps[lo:lo + N, j * N:(j + 1) * N], BKtok[:, c, h, :], UV[:, c, h, :],
                                               start=True, stop=True)
                    end(ins, "state", tt, c)
                    for h, j, lo in heads:
                        ins = nc.tensor.matmul(psy[c * C:(c + 1) * C, h * N:(h + 1) * N], SCm[:, c, h, C:2 * C], UV[:, c, h, :],
                                               start=False, stop=True, skip_group_check=True)
                end(ins, "Y", tt)
                ps = begin("yT", tt)
                pe.wait_ge(y_ready, tt + 1)
                for j in range(JT):
                    ins = nc.tensor.transpose(ps[:, j * P:(j + 1) * P], Yq[:, j * P:(j + 1) * P], ident[:, :])
                end(ins, "yT", tt)

            for qb in range(TT):
                emptied(pe, "foT", qb)
            for half in range(2):
                pe.wait_ge(w_out_loaded[half], 16)
            for tt in range(TT):
                emptied(pe, "yT", tt)
                for half in range(2):
                    ps = begin("o", tt, half)
                    for k in range(KT):
                        ins = nc.tensor.matmul(ps[:, :], hT[:, k, tt * P:(tt + 1) * P], slots[:, half, k, :],
                                               start=(k == 0), stop=(k == KT - 1))
                    end(ins, "o", tt, half)
            for tt in range(TT):
                pe.wait_ge(hrow_ready, TT + tt + 1)
                for half in range(2):
                    ps = begin("h2T", tt, half)
                    for k in range(4):
                        o = (half * 4 + k) * P
                        ins = nc.tensor.transpose(ps[:, k * P:(k + 1) * P], hrow[:, tt % 2, o:o + P], ident[:, :])
                    end(ins, "h2T", tt, half)
            for tt in range(TT):
                emptied(pe, "h2T", tt, 0)
                emptied(pe, "h2T", tt, 1)
                ps = begin("lg", tt)
                for k in range(KT):
                    ins = nc.tensor.matmul(ps[:, 0:E], hT[:, k, tt * P:(tt + 1) * P], rw[:, k, :],
                                           start=(k == 0), stop=(k == KT - 1))
                end(ins, "lg", tt)
            pe.wait_ge(sel_ready, TT)
            ps = begin("cnt")
            for t2 in range(TT):
                ins = nc.tensor.matmul(ps[:, 0:E], stepm[:, OFF + P:OFF + 2 * P], Msel[:, t2, :],
                                       start=(t2 == 0), stop=(t2 == TT - 1))
            end(ins, "cnt")
            for tt in range(TT):
                ps = begin("pos", tt)
                for t2 in range(tt):
                    nc.tensor.matmul(ps[:, 0:E], stepm[:, OFF + P:OFF + 2 * P], Msel[:, t2, :],
                                     start=(t2 == 0), stop=False)
                end(nc.tensor.matmul(ps[:, 0:E], stepm[:, OFF - 1:OFF - 1 + P], Msel[:, tt, :],
                                     start=(tt == 0), stop=True), "pos", tt)
            for tt in range(TT):
                emptied(pe, "pos", tt)

            def x_transposes(b, q, n):
                pe.wait_ge(xg_loaded[q], n * 16 + 16)
                pe.wait_ge(xt_free, b + 1)
                for k in range(KT):
                    ins = nc.tensor.transpose(bank[k // 4][:, (k % 4) * NS:(k % 4 + 1) * NS],
                                              xg[0:NS, q, k * P:(k + 1) * P], ident[0:NS, 0:NS])
                ins.then_inc(xt_full, 1)

            def block_work(i, q):
                b = i * 2 + q
                pe.wait_ge(xt_free, b + 2)
                for c in range(W1C):
                    pe.wait_ge(w_loaded[c], b * 16 + 16)
                    pe.wait_ge(hid_free[c % 2], b * 2 + (c // 2 + 1))
                    for t in range(2):
                        for s in range(2):
                            o = (2 * t + s) * NS
                            for k in range(KT):
                                ins = nc.tensor.matmul(bank[2 + c % 2][:, o:o + NS], every_other(slots[:, c, k, 2 * t * P:2 * (t + 1) * P], s),
                                                       xT[:, q, k, :], start=(k == 0), stop=(k == KT - 1))
                    ins.then_inc(hid_full[c % 2], 1)
                x_transposes(b + 1, 1 - q, i + q)
                pe.wait_ge(act_ready, b * W1C + W1C)
                for h in range(2):
                    pe.wait_ge(w_loaded[W1C + h], b * 16 + 16)
                    pe.wait_ge(ot_free[h], b + 1)
                    for t in range(4):
                        for f in range(FT):
                            ins = nc.tensor.matmul(bank[4 + h][:, t * NS:(t + 1) * NS],
                                                   slots[:, W1C + h, f, t * P:(t + 1) * P], actT[:, q, f, :],
                                                   start=(f == 0), stop=(f == FT - 1))
                    ins.then_inc(ot_full[h], 1)
                for h in range(2):
                    pe.wait_ge(ot_free[h], b + 2)
                    pe.wait_ge(y_free[h], b + 1)
                    for t in range(4):
                        ins = nc.tensor.transpose(bank[6 + h][0:NS, t * P:(t + 1) * P], oTs[:, h, t, :], ident[:, :])
                    ins.then_inc(y_full[h], 1)

            pe.sem_inc(xt_full, 1)
            x_transposes(0, 0, 0)
            pe.wait_ge(tables_ready, 1)
            with pe.Fori(0, E // 2) as i:
                for q in range(2):
                    block_work(i, q)
            npairs = pe.value_load(pairs_i[0:1, 0:1], min_val=E // 2, max_val=NB // 2)
            with pe.Fori(E // 2, NB // 2) as i:
                with pe.If(i < npairs):
                    for q in range(2):
                        block_work(i, q)

        @block.vector
        def _(dve):
            steps = [0]

            def step(ins):
                steps[0] += 1
                ins.then_inc(dve_step, 1)
                dve.wait_ge(dve_step, steps[0])

            tensor_tensor, tensor_scalar = nc.vector.tensor_tensor, nc.vector.tensor_scalar

            def heads_of(ap):
                return ap.rearrange("p (h v) -> p h v", h=H)

            def per_head(st, parts=P):
                return st.unsqueeze(2).to_broadcast([parts, H, N])

            def normalize(tt, again):
                dve.wait_ge(sumsq_ready, TT * again + tt + 1)
                step(nc.vector.reciprocal(ss[:, tt:tt + 1], ss[:, tt:tt + 1]))
                if tt >= 2:
                    for half in range(2):
                        filled(dve, "h2T" if again else "hT", tt - 2, half)
                    if again:
                        dve.wait_ge(h2_stored[tt - 2], 16)
                tensor_scalar(hrow[:, tt % 2, :], xs[:, tt, :], ss[:, tt:tt + 1], None, ALU.mult).then_inc(hrow_ready, 1)

            def take_transposed(name, tt, gain):
                for half in range(2):
                    filled(dve, name, tt, half)
                    b = plan[(name, tt, half)][0]
                    tensor_tensor(hT[:, half * 4:half * 4 + 4, tt * P:(tt + 1) * P],
                                  bank[b][:, :].rearrange("p (k t) -> p k t", k=4),
                                  vec(gain)[:, half * 4:half * 4 + 4].unsqueeze(2).to_broadcast([P, 4, P]),
                                  ALU.mult).then_inc(free_of((name, tt, half)), 1)

            filled(dve, "vec")
            nc.vector.tensor_copy(vecT[:, 0:vrow], bank[0][:, 0:vrow]).then_inc(free_of(("vec",)), 1)
            emptied(dve, "vec")
            step(tensor_scalar(one_minus_ka, vec("ka"), -1.0, 1.0, ALU.mult, ALU.add))
            dve.sem_inc(vec_ready, 1)
            for tt in range(TT + 1):
                if tt < TT:
                    normalize(tt, 0)
                if tt > 0:
                    take_transposed("hT", tt - 1, "g1")

            dve.wait_ge(consts_ready, 3)

            def mix(nth, m):
                emptied(dve, "u", m)
                cur = shiftbuf[:, nth % 2, 1:T + 1]
                prev = shiftbuf[:, nth % 2, 0:T]
                if m < 8:
                    dst = (AR if m < 4 else BK)[:, m % 4, :, C:2 * C]
                    cur, prev = (v.rearrange("p (c t) -> p c t", t=C) for v in (cur, prev))
                else:
                    dst = vT[:, m - 8, :] if m < 12 else wa if m == 12 else gl
                step(tensor_tensor(dst, prev, cur, ALU.subtract))
                nc.vector.scalar_tensor_tensor(dst, dst, vec("mu", m), cur, ALU.mult, ALU.add).then_inc(mixed, 1)
                dve.wait_ge(mixed, nth + 1)

            rwkv_order = [m for m in U_ORDER if m < 14]
            for nth, m in enumerate(rwkv_order[:10]):
                mix(nth, m)
            for j in range(JT):
                emptied(dve, "z", j)
                step(nc.vector.tensor_tensor_scan(decay_c[:, j, :], reset[:, :, :].rearrange("p c t -> p (c t)"),
                                                  decay_s[:, j, :], 0.0, ALU.mult, ALU.add))
                tensor_tensor(decay_s[:, j, :], decay_c[:, j, :], decay_s[:, j, :], ALU.subtract).then_inc(cum_ready, 1)
                step(tensor_scalar(BK[:, j, :, 0:C], BK[:, j, :, C:2 * C], vec("kk", j), None, ALU.mult))
                tensor_tensor(AR[:, j, :, 0:C], BK[:, j, :, 0:C], BK[:, j, :, 0:C], ALU.mult).then_inc(kksq_ready, 1)
            for nth, m in enumerate(rwkv_order[10:]):
                mix(10 + nth, m)

            def chunks_of(ap):
                return ap.rearrange("p (c t) -> p c t", t=C)

            for j in range(JT):
                filled(dve, "ss", j)
                tensor_scalar(AR[:, j, :, 0:C], chunks_of(bank[plan[("ss", j)][0]][:, :]), 1e-24, None, ALU.max)\
                    .then_inc(free_of(("ss", j)), 1)
                emptied(dve, "ss", j)
                dve.sem_inc(kksum_ready, 1)
            for j in range(JT):
                A_, R_, B_, K_ = AR[:, j, :, 0:C], AR[:, j, :, C:2 * C], BK[:, j, :, 0:C], BK[:, j, :, C:2 * C]
                a_ = chunks_of(aT[:, j, :])
                dve.wait_ge(kknorm_ready, j + 1)
                step(nc.vector.reciprocal(A_, A_))
                step(tensor_tensor(B_, B_, A_, ALU.mult))
                dve.wait_ge(exps_ready, j + 1)
                step(tensor_tensor(A_, B_, chunks_of(decay_s[:, j, :]), ALU.mult))
                emptied(dve, "a", j)
                step(tensor_tensor(B_, B_, a_, ALU.mult))
                step(tensor_tensor(B_, B_, chunks_of(decay_c[:, j, :]), ALU.mult))
                step(tensor_scalar(a_, a_, vec("ka", j), one_minus_ka[:, j:j + 1], ALU.mult, ALU.add))
                step(tensor_tensor(K_, K_, a_, ALU.mult))
                step(nc.vector.scalar_tensor_tensor(a_, R_, vec("rk", j), K_, ALU.mult, ALU.mult))
                step(tensor_tensor(K_, K_, chunks_of(decay_c[:, j, :]), ALU.mult))
                step(tensor_tensor(R_, R_, chunks_of(decay_e[:, j, :]), ALU.mult))
                nc.vector.tensor_copy(dend[:, j, :], chunks_of(decay_e[:, j, :])[:, :, C - 1]).then_inc(elem_done, 1)
            dve.wait_ge(elem_done, JT)

            filled(dve, "ff")
            tensor_tensor(ffz[:, 0], bank[plan[("ff",)][0]][:, 0:TT * H].rearrange("p (t h) -> p t h", h=H),
                          fb[:, :].unsqueeze(1).to_broadcast([P, TT, H]), ALU.add).then_inc(free_of(("ff",)), 1)
            emptied(dve, "ff")
            step(tensor_scalar(ffz[:, 4], ffz[:, 0], 0.0, None, ALU.min))
            dve.wait_ge(ffln_ready, 1)
            tensor_tensor(ffz[:, 4], ffz[:, 3], ffz[:, 4], ALU.subtract).then_inc(nlf_ready, 1)
            filled(dve, "cT")
            nc.vector.tensor_copy(cf[:, :], bank[plan[("cT",)][0]][0:H, :]).then_inc(free_of(("cT",)), 1)
            emptied(dve, "cT")
            for g in range(2):
                step(nc.vector.tensor_copy(cb[:, g, :], cf[:, :]))
                step(tensor_tensor(cf[:, :], cf[:, :], cb[:, g, :], ALU.subtract))
                step(nc.vector.tensor_copy(c3[32 * g:32 * g + H, :], cb[:, g, :]))
            nc.vector.tensor_copy(c3[64:64 + H, :], cf[:, :]).then_inc(c3_ready, 1)

            def finish_fox(qb):
                dve.wait_ge(values_done, H * (qb + 1))
                u0 = qb * H
                emptied(dve, "S", qb, H - 1)
                step(nc.vector.reciprocal(rrec[:, :], rsum[:, u0:u0 + H]))
                if qb >= 2:
                    filled(dve, "foT", qb - 2)
                f = heads_of(fo[:, qb % 2, :])
                tensor_tensor(f, heads_of(bank[4 + qb % 2][:, :]), per_head(rrec[:, :]), ALU.mult).then_inc(fox_o_free, 1)
                dve.wait_ge(fox_o_free, qb + 1)
                step(tensor_tensor(heads_of(fsq), f, f, ALU.mult))
                nc.vector.tensor_reduce(fst[:, :], heads_of(fsq), AX, ALU.add).then_inc(fox_ms_ready, 1)
                dve.wait_ge(fox_rms_ready, qb + 1)
                step(nc.vector.reciprocal(fst[:, :], fst[:, :]))
                tensor_tensor(f, f, per_head(fst[:, :]), ALU.mult).then_inc(fo_ready, 1)

            for i in range(len(units) + 2):
                if i < len(units):
                    filled(dve, "S", *units[i])
                    nc.vector.tensor_reduce(nmx[:, i:i + 1], bank[i % 2][:, 0:(units[i][0] + 1) * P], AX, ALU.max,
                                            negate=True).then_inc(negmax_ready, 1)
                if 1 <= i <= len(units):
                    filled(dve, "PT", *units[i - 1])
                    if i >= 3:
                        dve.wait_ge(values_done, i - 2)
                    keys = (units[i - 1][0] + 1) * P
                    nc.vector.tensor_copy(fPT[:, (i - 1) % 2, 0:keys], bank[2 + (i - 1) % 2][:, 0:keys])\
                        .then_inc(free_of(("PT", *units[i - 1])), 1)
                if i >= H + 1 and (i - H - 1) % H == 0:
                    finish_fox((i - H - 1) // H)

            def pairs_of(ap):
                return ap.rearrange("p (j g) t -> p j g t", g=2)

            step(nc.vector.memset(STc, 0.0))
            nc.vector.memset(ST, 0.0).then_inc(state_ready, 1)
            for tt in range(TT):
                for c in range(2):
                    for g in range(2):
                        filled(dve, "SC", tt, c, g)
                        tensor_tensor(pairs_of(SCm[:, c])[:, :, g, :], bank[g][:, :].rearrange("p (h t) -> p h t", h=4),
                                      maskSC[:, :].unsqueeze(1).to_broadcast([P, 4, 2 * C]), ALU.mult)\
                            .then_inc(free_of(("SC", tt, c, g)), 1)
                    for g in range(2):
                        emptied(dve, "SC", tt, c, g)
                    dve.sem_inc(scm_ready, 1)
                    step(tensor_tensor(XT[0:C, c], SCm[0:C, c, :, 0:C],
                                       levmask[:, 0, :].unsqueeze(1).to_broadcast([C, H, C]), ALU.mult))
                    tensor_tensor(XT[0:C, c], ident[0:C, 0:C].unsqueeze(1).to_broadcast([C, H, C]), XT[0:C, c],
                                  ALU.subtract).then_inc(xt0_ready, 1)
                for lv in range(1, LEVELS):
                    for c in range(2):
                        filled(dve, "XT", tt, c, lv)
                        if lv == 1:
                            dve.wait_ge(xt0_ready, 2 * tt + c + 1)
                        else:
                            emptied(dve, "XT", tt, c, lv - 1)
                        tensor_tensor(XT[0:C, c], XT[0:C, c], heads_of(bank[4 + c][0:C, :]), ALU.subtract)\
                            .then_inc(free_of(("XT", tt, c, lv)), 1)
                for c in range(2):
                    cc = 2 * tt + c
                    filled(dve, "U", tt, c)
                    tensor_scalar(UV[0:C, c], heads_of(bank[6][0:C, :]), -1.0, None, ALU.mult)\
                        .then_inc(free_of(("U", tt, c)), 1)
                    filled(dve, "state", tt, c)
                    dve.wait_ge(state_ready, cc + 1)
                    tensor_tensor(STt, STc, bank[6][:, 0:JT * N].rearrange("p (j v) -> p j v", j=JT), ALU.add)\
                        .then_inc(free_of(("state", tt, c)), 1)
                    emptied(dve, "state", tt, c)
                    for g in range(2):
                        r = slice(g * N, (g + 1) * N)
                        ins = tensor_tensor(ST[r, :, r], STt[r], dend[r, :, cc:cc + 1].to_broadcast([N, JT, N]), ALU.mult)
                    ins.then_inc(state_ready, 1)
                    step(tensor_tensor(STc, STt, dend[:, :, cc:cc + 1].to_broadcast([P, JT, N]), ALU.mult))
                filled(dve, "Y", tt)
                y, yc, yq = heads_of(bank[7][:, :]), heads_of(Yc), heads_of(Yq)
                mean, var = gst[:, 0, :], gst[:, 1, :]
                step(nc.vector.tensor_reduce(mean, y, AX, ALU.add))
                step(tensor_scalar(mean, mean, 1.0 / N, None, ALU.mult))
                tensor_tensor(yc, y, per_head(mean), ALU.subtract).then_inc(free_of(("Y", tt)), 1)
                emptied(dve, "Y", tt)
                if tt > 0:
                    filled(dve, "yT", tt - 1)
                step(tensor_tensor(yq, yc, yc, ALU.mult))
                nc.vector.tensor_reduce(var, yq, AX, ALU.add).then_inc(gn_var_ready, 1)
                dve.wait_ge(gn_std_ready, tt + 1)
                step(nc.vector.reciprocal(var, var))
                step(tensor_tensor(yc, yc, per_head(var), ALU.mult))
                step(tensor_tensor(Yc, Yc, lnw[:, :], ALU.mult))
                step(tensor_tensor(Yc, Yc, lnb[:, :], ALU.add))
                emptied(dve, "vt", tt)
                emptied(dve, "bonus")
                step(tensor_tensor(yq, heads_of(Vtok), per_head(bonus[:, tt, :]), ALU.mult))
                step(tensor_tensor(Yc, Yc, Yq, ALU.add))
                emptied(dve, "g", tt)
                tensor_tensor(Yq, Yc, G[:, tt, :], ALU.mult).then_inc(y_ready, 1)

            for tt in range(TT):
                for half in range(2):
                    filled(dve, "o", tt, half)
                    o = xs[:, tt, half * CW:(half + 1) * CW]
                    tensor_tensor(o, o, bank[plan[("o", tt, half)][0]][:, :], ALU.add).then_inc(free_of(("o", tt, half)), 1)
            for tt in range(TT + 1):
                if tt < TT:
                    normalize(tt, 1)
                if tt > 0:
                    take_transposed("h2T", tt - 1, "g2")

            dve.wait_ge(consts_ready, 4)
            for tt in range(TT):
                filled(dve, "lg", tt)
                tensor_tensor(lg[:, tt, :], bank[6][:, 0:E], rb[:, :], ALU.add).then_inc(free_of(("lg", tt)), 1)
                emptied(dve, "lg", tt)
                step(nc.vector.max(m8[:, tt, :], lg[:, tt, :]))
                step(nc.vector.max_index(i8[:, tt, :], m8[:, tt, :], lg[:, tt, :]))
                tensor_scalar(nm0[:, tt:tt + 1], m8[:, tt, 0:1], -1.0, None, ALU.mult).then_inc(gmax_ready, 1)
                step(nc.vector.tensor_copy(i8f[:, tt, :], i8[:, tt, :]))
                step(tensor_tensor(onehot[:, tt], iotaE[:, :].unsqueeze(1).to_broadcast([P, TOPK, E]),
                                   i8f[:, tt, 0:TOPK].unsqueeze(2).to_broadcast([P, TOPK, E]), ALU.is_equal))
                nc.vector.tensor_reduce(Msel[:, tt, :], onehot[:, tt].rearrange("p k e -> p e k"), AX, ALU.add)\
                    .then_inc(sel_ready, 1)
            for tt in range(TT):
                dve.wait_ge(gates_ready, tt + 1)
                step(nc.vector.reciprocal(gsum[:, tt:tt + 1], gsum[:, tt:tt + 1]))
                step(tensor_scalar(gate[:, tt, :], gate[:, tt, :], gsum[:, tt:tt + 1], None, ALU.mult))
            filled(dve, "cnt")
            nc.vector.tensor_copy(cnt[:, :], bank[7][:, 0:E]).then_inc(free_of(("cnt",)), 1)
            emptied(dve, "cnt")
            extra = rt[:, 0, :]
            step(tensor_scalar(extra, cnt[:, :], float(NS), None, ALU.is_gt))
            for n in range(2, EXTRA + 1):
                step(nc.vector.scalar_tensor_tensor(extra, cnt[:, :], float(n * NS), extra, ALU.is_gt, ALU.add))
            step(nc.vector.tensor_tensor_scan(ovf_end[:, :], stepm[:, OFF + P:OFF + P + E], extra, 0.0, ALU.mult, ALU.add))
            step(tensor_tensor(ovf_base[:, :], ovf_end[:, :], extra, ALU.subtract))
            step(tensor_scalar(rt[:, 1, 0:NOVF // 2], iotaO[:, 0:NOVF // 2], 2.0, ovf_end[:, E - 1:E], ALU.mult, ALU.is_lt))
            step(nc.vector.tensor_reduce(pairs_f[:, 0:1], rt[:, 1, 0:NOVF // 2], AX, ALU.add))
            step(tensor_scalar(pairs_f[:, 1:2], pairs_f[:, 0:1], float(E // 2), None, ALU.add))
            step(nc.vector.tensor_copy(pairs_i[:, :], pairs_f[:, 1:2]))
            step(tensor_tensor(ovcmp[:, :, :], ovf_end[:, :].unsqueeze(1).to_broadcast([P, NOVF, E]),
                               iotaO[:, :].unsqueeze(2).to_broadcast([P, NOVF, E]), ALU.is_le))
            step(nc.vector.tensor_reduce(ovexp[:, :], ovcmp[:, :, :], AX, ALU.add))
            step(tensor_scalar(ovexp[:, :], ovexp[:, :], float(E - 1), None, ALU.min))
            step(nc.vector.tensor_copy(blkexp[:, :], ovexp[:, :]))
            dve.sem_inc(tables_ready, 1)
            for tt in range(TT):
                filled(dve, "pos", tt)
                nc.vector.tensor_copy(pos[:, :], bank[plan[("pos", tt)][0]][:, 0:E]).then_inc(free_of(("pos", tt)), 1)
                emptied(dve, "pos", tt)
                step(tensor_scalar(qd[:, :], pos[:, :], float(NS), None, ALU.is_ge))
                for n in range(2, EXTRA + 1):
                    step(nc.vector.scalar_tensor_tensor(qd[:, :], pos[:, :], float(n * NS), qd[:, :], ALU.is_ge, ALU.add))
                first, later, blkid = rt[:, 2, :], rt[:, 3, :], rt[:, 4, :]
                step(tensor_scalar(first, qd[:, :], 0.0, None, ALU.is_equal))
                step(nc.vector.scalar_tensor_tensor(later, qd[:, :], float(E - 1), ovf_base[:, :], ALU.add, ALU.add))
                step(tensor_tensor(blkid, iotaE[:, :], later, ALU.subtract))
                step(tensor_tensor(blkid, blkid, first, ALU.mult))
                step(tensor_tensor(blkid, blkid, later, ALU.add))
                step(tensor_tensor(blkid, blkid, qd[:, :], ALU.subtract))
                step(nc.vector.scalar_tensor_tensor(slotm[:, :], blkid, float(NS), pos[:, :], ALU.mult, ALU.add))
                step(tensor_tensor(slotk[:, :, :], onehot[:, tt], slotm[:, :].unsqueeze(1).to_broadcast([P, TOPK, E]), ALU.mult))
                step(nc.vector.tensor_reduce(slotf[:, tt, :], slotk[:, :, :], AX, ALU.add))
                nc.vector.tensor_copy(sloti[:, tt, :], slotf[:, tt, :]).then_inc(slots_ready, 1)

            for tt in range(TT):
                dve.wait_ge(h2_stored[tt], 16)

            def take_x(b, q):
                dve.wait_ge(xt_full, b + 2)
                for half in range(2):
                    ins = tensor_tensor(xT[:, q, half * 4:half * 4 + 4, :],
                                        bank[half][:, 0:4 * NS].rearrange("p (k s) -> p k s", k=4),
                                        vec("g2")[:, half * 4:half * 4 + 4].unsqueeze(2).to_broadcast([P, 4, NS]), ALU.mult)
                ins.then_inc(xt_free, 1)

            def block_work(i, q, e):
                b = i * 2 + q
                nc.vector.tensor_copy(b1c[:, q, :].unsqueeze(2), b1T[:, :, bass.ds(e, 1)])
                nc.vector.tensor_copy(b2c[:, q, :].unsqueeze(2), b2T[:, :, bass.ds(e, 1)]).then_inc(bias_ready, 1)
                dve.wait_ge(bias_ready, b + 1)
                for c in range(W1C):
                    p, n = c % 2, b * 2 + c // 2
                    dve.wait_ge(hid_full[p], n + 1)
                    for s, dst, done in ((0, hg, glu_ready), (1, hl, hid_free[p])):
                        for t in range(2):
                            o = (2 * t + s) * NS
                            v = 2 * (2 * c + t) + s
                            ins = tensor_scalar(dst[:, p, t], bank[2 + p][:, o:o + NS], b1c[:, q, v:v + 1], 7.0,
                                                ALU.add, ALU.min)
                        ins.then_inc(done, 1)
                    dve.wait_ge(hid_free[p], n + 2)
                    tensor_scalar(hm[:, p], hl[:, p], -7.0, 1.0, ALU.max, ALU.add).then_inc(lin_ready, 1)
                    dve.wait_ge(sig_ready, b * W1C + (c + 1))
                    tensor_tensor(hg[:, p], hg[:, p], hs[:, p], ALU.mult).then_inc(swi_ready, 1)
                    dve.wait_ge(lin_ready, b * W1C + (c + 1))
                    dve.wait_ge(swi_ready, b * W1C + (c + 1))
                    tensor_tensor(actT[:, q, 2 * c:2 * c + 2, :], hg[:, p], hm[:, p], ALU.mult).then_inc(act_ready, 1)
                take_x(b + 1, 1 - q)

            dve.sem_inc(xt_free, 1)
            for p in range(2):
                dve.sem_inc(hid_free[p], 1)
            take_x(0, 0)
            with dve.Fori(0, E // 2) as i:
                for q in range(2):
                    block_work(i, q, i * 2 + q)
            npairs = dve.value_load(pairs_i[0:1, 0:1], min_val=E // 2, max_val=NB // 2)
            with dve.Fori(E // 2, NB // 2) as i:
                with dve.If(i < npairs):
                    for q in range(2):
                        e = dve.value_load(blkexp[0:1, bass.ds(i * 2 + (q - E), 1)], min_val=0, max_val=E - 1)
                        block_work(i, q, e)

            dve.wait_ge(gfin_in, 16)
            for tt in range(TT):
                dve.wait_ge(gathered[tt], 16 * TOPK)
                for k in range(TOPK):
                    rows = slots[:, tt, 2 * k:2 * k + 2, :].rearrange("p a f -> p (a f)")
                    step(nc.vector.scalar_tensor_tensor(xs[:, tt, :], rows, gate[:, tt, k:k + 1], xs[:, tt, :],
                                                        ALU.mult, ALU.add))
                dve.sem_inc(summed, 1)
                dve.wait_ge(normed, tt + 1)
                step(nc.vector.reciprocal(ss[:, tt:tt + 1], ss[:, tt:tt + 1]))
                if tt >= 2:
                    dve.wait_ge(out_stored[tt - 2], 16)
                nc.vector.scalar_tensor_tensor(outb[tt % 2], xs[:, tt, :], ss[:, tt:tt + 1], gfin, ALU.mult, ALU.mult)\
                    .then_inc(out_ready, 1)


_INS = ['x', 'attn_norm_g', 'w_in', 'rwkv_mu', 'rwkv_w0', 'rwkv_w_up', 'rwkv_a0', 'rwkv_a_up', 'rwkv_g_up',
        'rwkv_k_k', 'rwkv_k_a', 'rwkv_r_k', 'rwkv_ln_w', 'rwkv_ln_b', 'fox_f_bias', 'fox_out_g', 'w_out',
        'ffn_norm_g', 'router_w', 'router_b', 'expert_w1', 'expert_b1', 'expert_w2', 'expert_b2', 'final_norm_g']
_OUTS = [((1, 512, 1024), 'float32')]


def kernel(**inputs):
    import numpy as _np
    import concourse.bacc as _bacc
    from concourse import mybir as _mybir
    from concourse.bass_utils import run_bass_kernel_spmd as _run

    nc = _bacc.Bacc("TRN2", target_bir_lowering=False, num_devices=1)
    arrays, args = {}, []
    for name in _INS:
        a = _np.ascontiguousarray(inputs[name])
        arrays[f"in_{name}_dram"] = a
        args.append(nc.dram_tensor(f"in_{name}_dram", a.shape, _mybir.dt.from_np(a.dtype), kind="ExternalInput").ap())
    for i, (shape, dtype) in enumerate(_OUTS):
        dt = _mybir.dt.from_np(_np.dtype(dtype))
        args.append(nc.dram_tensor(f"out_{i}_dram", shape, dt, kind="ExternalOutput").ap())
    hymba_layer(nc, *args)
    r = _run(nc, [arrays], core_ids=[0])
    got = tuple(r.results[0][f"out_{i}_dram"] for i in range(len(_OUTS)))
    return got[0]
```

```python
import concourse.bass as bass
from concourse import mybir
from contextlib import ExitStack


def hymba_layer(nc, x, attn_norm_g, w_in, mu, w0, w_up, a0, a_up, g_up, k_k, k_a, r_k, ln_w, ln_b,
                f_bias, out_g, w_out, ffn_norm_g, router_w, router_b, w1, b1, w2, b2, final_norm_g, out):
    f32 = mybir.dt.float32
    f32r = mybir.dt.float32r
    bf16 = mybir.dt.bfloat16
    i32 = mybir.dt.int32
    u32 = mybir.dt.uint32
    ALU = mybir.AluOpType
    ACT = mybir.ActivationFunctionType
    AX = mybir.AxisListType.X

    P = 128
    T, D = x.shape[1], x.shape[2]
    TT, KT = T // P, D // P
    H, N = r_k.shape[1], r_k.shape[2]
    HW = H * N
    JT = HW // P
    LORA = w_up.shape[1]
    C = P
    NC = T // C
    MID = C // 2
    FOX0 = 3 * HW + 2 * LORA + g_up.shape[1]
    E, F2 = router_w.shape[2], w1.shape[3]
    FT = F2 // 2 // P
    TOPK = 4
    NS = 96
    EXTRA = -(-T // NS) - 1
    NOVF = 22
    assert NOVF >= T * TOPK // NS and NOVF % 2 == 0
    NB = E + NOVF
    CH = 6
    CW = 512
    W1C = F2 // CW
    UNITS = 2 * CH
    RAW, HI, LO = 6, 4, 3
    assert 2 * UNITS % RAW == 0 and 2 * UNITS % HI == 0 and 2 * UNITS % LO == 0
    UNIT_OF = [(c, kh) for c in range(W1C) for kh in range(2)] + [(c, kh) for kh in range(2) for c in range(W1C, CH)]
    ROWB = NB + 6
    assert ROWB * NS % P == 0
    KAPPA = 0.6065306597126334
    LEVELS = 7
    RMS_EPS, GN_EPS = 1e-5, 64e-5

    slot_tokens = nc.dram_tensor("slot_tokens", [ROWB * NS, 1], i32).ap()
    h2_rows = nc.dram_tensor("h2_rows", [T, D], f32).ap()
    expert_rows = nc.dram_tensor("expert_rows", [(NB + 1) * NS, D], f32).ap()

    ctx = ExitStack()
    with ctx:
        end_of = {}

        def sb(name, shape, dt=f32):
            tensor = ctx.enter_context(nc.sbuf_tensor(name, shape, dt))
            end_of[name] = nc.sbuf_base
            return tensor

        def rounded(name, owner, owner_words, first_word, shape):
            return nc.alloc_sbuf_tensor_at(name, shape, f32r, offset=end_of[owner] - 4 * (owner_words - first_word))

        def sem(name):
            return ctx.enter_context(nc.semaphore(name))

        slots = sb("slots", [P, CH, KT, CW])
        xs = sb("xs", [P, TT, D])
        hT = sb("hT", [P, KT, T])
        AR = sb("AR", [P, JT, NC, 2 * C])
        BK = sb("BK", [P, JT, NC, 2 * C])
        qk = sb("qk", [P, 2, JT, T])
        shiftbuf = sb("shiftbuf", [P, 2, T + 1])

        def region(t2d, off, size):
            return t2d[:, off:off + size]

        slot_flat = [slots[:, s].rearrange("p k f -> p (k f)") for s in range(CH)]
        S4 = KT * CW
        decay_s = region(slot_flat[3], 0, JT * T).rearrange("p (j t) -> p j t", j=JT)
        decay_c = region(slot_flat[3], JT * T, JT * T).rearrange("p (j t) -> p j t", j=JT)
        vT = region(slot_flat[4], 0, JT * T).rearrange("p (j t) -> p j t", j=JT)
        aT = region(slot_flat[4], JT * T, JT * T).rearrange("p (j t) -> p j t", j=JT)
        G = region(slot_flat[5], 0, TT * HW).rearrange("p (t c) -> p t c", t=TT)
        foxv = region(slot_flat[5], TT * HW, TT * HW).rearrange("p (t c) -> p t c", t=TT)
        decay_e = region(slot_flat[2], 0, JT * T).rearrange("p (j t) -> p j t", j=JT)
        wa = region(slot_flat[2], 4 * T, T)
        gl = region(slot_flat[2], 5 * T, T)
        lora_up = region(slot_flat[2], 6 * T, HW)
        gup = region(slot_flat[2], 7 * T, HW)
        zrow = aT[:, 2:4, :].rearrange("p j t -> p (j t)")
        fP = region(slot_flat[3], 0, 2 * T).rearrange("p (b t) -> p b t", b=2)
        fPT = region(slot_flat[3], 2 * T, 2 * T).rearrange("p (b t) -> p b t", b=2)
        fo = region(slot_flat[3], 4 * T, 2 * HW).rearrange("p (b c) -> p b c", b=2)
        fsq = region(slot_flat[3], 6 * T, HW)
        cf = region(slot_flat[3], 7 * T, T)[0:H, :]
        cb = region(slot_flat[2], 0, T).bitcast(bf16).rearrange("p (g t) -> p g t", g=2)[0:H]
        blocks = region(slot_flat[3], 0, (LEVELS + 1) * C).rearrange("p (l c) -> p l c", c=C)
        s1 = slot_flat[1]
        Xm = region(s1, 0, 2 * H * C).rearrange("p (q h t) -> p q h t", q=2, h=H)
        Pm = region(s1, 2 * H * C, 2 * H * C).rearrange("p (q h t) -> p q h t", q=2, h=H)
        Lm = region(slot_flat[4], JT * T, 2 * H * C).rearrange("p (q h t) -> p q h t", q=2, h=H)
        s3 = slot_flat[3]
        CT = region(s3, 0, 2 * H * C).rearrange("p (q h t) -> p q h t", q=2, h=H)
        XT = region(slot_flat[2], 0, NC * H * C).rearrange("p (q h t) -> p q h t", q=NC, h=H)
        qkf = qk[:, :, :, :].rearrange("p a j t -> p (a j t)")
        fv2 = slot_flat[5]
        Lf, CTf, XTf = region(slot_flat[4], JT * T, 2 * H * C), region(s3, 0, 2 * H * C), slot_flat[2]

        def per_chunk(usual, last):
            return [usual] * (NC - 1) + [last]

        KAR = per_chunk(*(region(m, 0, H * 2 * C).rearrange("p (h t) -> p h t", h=H) for m in (qkf, CTf)))
        BR = per_chunk(*(region(m, o, H * C).rearrange("p (h t) -> p h t", h=H) for m, o in ((qkf, 2 * H * C), (Lf, 0))))
        Atok = per_chunk(region(qkf, 3 * H * C, HW), region(Lf, H * C, HW))
        MV = per_chunk(region(qkf, 3 * H * C + HW, HW), region(Lf, H * C + HW, HW))
        Btok = per_chunk(region(fv2, TT * HW, HW), region(XTf, 0, HW))
        Ktok = per_chunk(region(fv2, TT * HW + HW, HW), region(XTf, HW, HW))
        U = per_chunk(region(fv2, TT * HW + 2 * HW, HW), region(XTf, H * C, HW))
        V0 = region(fv2, TT * HW + 3 * HW, HW)
        sbf = shiftbuf[:, :, :].rearrange("p b t -> p (b t)")
        V = [V0, region(sbf, 0, HW)]
        WT = per_chunk(*(region(m, o, JT * C).rearrange("p (j t) -> p j t", j=JT)
                         for m, o in ((sbf, HW), (XTf, H * C + HW))))
        Yc = region(s3, 2 * H * C, HW)
        Yq = region(s3, 2 * H * C + HW, HW)
        ST = region(s3, 2 * H * C + 2 * HW, JT * P).rearrange("p (j v) -> p j v", j=JT)
        STc = region(s3, 2 * H * C + 3 * HW, JT * N).rearrange("p (j v) -> p j v", j=JT)
        STt = region(s3, 2 * H * C + 3 * HW + JT * N, JT * N).rearrange("p (j v) -> p j v", j=JT)
        ARf = AR[:, :, :, :].rearrange("p j c t -> p (j c t)")
        BKf = BK[:, :, :, :].rearrange("p j c t -> p (j c t)")
        hTf = hT[:, :, :].rearrange("p k t -> p (k t)")
        hrow = region(BKf, 0, 2 * D).rearrange("p (b d) -> p b d", b=2)
        junk = region(ARf, 0, D)
        squares = region(BKf, 2 * D, D)
        xg = region(ARf, 0, 2 * D).rearrange("p (b d) -> p b d", b=2)
        xTf = region(ARf, 2 * D, KT * NS)
        act = region(ARf, 2 * D + KT * NS, FT * P)
        hg, hs, hl = (region(BKf, n * CW, CW).rearrange("p (b s) -> p b s", b=2) for n in range(3))
        ovcmp = region(BKf, 3072, NOVF * E).rearrange("p (o e) -> p o e", e=E)
        rt = region(BKf, 3072 + NOVF * E, 6 * E).rearrange("p (n e) -> p n e", e=E)
        BW = JT * NC * 2 * C
        x_hi, x_lo = (rounded(f"x_{nm}", "BK", BW, o, [P, KT, NS]) for nm, o in (("hi", 3 * CW), ("lo", 3 * CW + KT * NS)))
        a_hi = rounded("a_hi", "BK", BW, 3072, [P, FT, NS])
        sel = rounded("sel", "BK", BW, 3072 + FT * NS, [2 * E, 2, NS])
        a_lo = rounded("a_lo", "hT", BW, 3 * D, [P, FT, NS])
        b2r = rounded("b2r", "hT", BW, 2 * D, [2 * E, D])
        b1r = rounded("b1r", "qk", BW, 2 * D, [2 * E, F2])
        raw = [slots[:, 2 + r // 2, r % 2 * 4:r % 2 * 4 + 4, :] for r in range(RAW)]
        w_hi = [rounded(f"hi{r}", "slots", CH * S4, r * S4 // 2, [P, KT // 2, CW]) for r in range(HI)]
        w_lo = [rounded(f"lo{r}", "slots", CH * S4, (10 + r) * S4 // 2, [P, KT // 2, CW]) for r in range(2)]
        w_lo.append(rounded("lo2", "qk", BW, 0, [P, KT // 2, CW]))
        onehot = region(qkf, 0, TT * TOPK * E).rearrange("p (t k e) -> p t k e", t=TT, e=E)
        ob = region(hTf, 0, 2 * D).rearrange("p (b d) -> p b d", b=2)
        gfin = region(hTf, 2048, D)
        outb = [region(hTf, 3072, D), region(hTf, 0, D)]
        biasrows = region(slot_flat[0], 0, F2 + D)

        VR = {}
        vrow = 0
        for nm, src in (("g1", attn_norm_g), ("mu", mu), ("w0", w0), ("a0", a0), ("kk", k_k), ("ka", k_a),
                        ("rk", r_k), ("og", out_g), ("g2", ffn_norm_g)):
            n = 1
            for d in src.shape:
                n *= d
            VR[nm] = (vrow, n // P)
            vrow += n // P
        vec_rows = sb("vec_rows", [vrow, P])
        vecT = sb("vecT", [P, vrow + JT])

        def vec(nm, j=None):
            a, n = VR[nm]
            return vecT[:, a:a + n] if j is None else vecT[:, a + j:a + j + 1]

        one_minus_ka = vecT[:, vrow:vrow + JT]
        lnw = sb("lnw", [P, HW])
        lnb = sb("lnb", [P, HW])
        rw = sb("rw", [P, KT, E])
        rb = sb("rb", [P, E])
        expert_row = sb("expert_row", [2 * E, E])
        fb = sb("fb", [P, H])
        wff = sb("wff", [P, KT, H])
        ident = sb("ident", [P, P])
        blk = sb("blk", [P, P])
        OFF = (TT - 1) * P
        stepm = sb("stepm", [P, OFF + T])
        maskSC = sb("maskSC", [P, 2 * C])
        levmask = sb("levmask", [C, LEVELS, C])
        identb = sb("identb", [P, P], bf16)
        causal = sb("causal", [P, P], bf16)
        selh = sb("selh", [96, H, P], bf16)
        c3 = sb("c3", [96, T], bf16)
        ss = sb("ss", [P, TT])
        eps = sb("eps", [P, 2])
        rstd = sb("rstd", [P, TT])
        ffz = sb("ffz", [P, 5, TT, H])
        nmx = sb("nmx", [P, TT * H])
        rsum = sb("rsum", [P, TT * H])
        rrec = sb("rrec", [P, H])
        fst = sb("fst", [P, H])
        dend = sb("dend", [P, JT, NC])
        mid = sb("mid", [P, JT, NC])
        bonus = sb("bonus", [P, TT, H])
        gst = sb("gst", [P, 3, H])
        zero_i = sb("zero_i", [P, ROWB * NS // P], i32)
        iotaE = sb("iotaE", [P, E])
        iotaO = sb("iotaO", [P, NOVF])
        iotaEi = sb("iotaEi", [P, E], i32)
        iotaOi = sb("iotaOi", [P, NOVF], i32)
        tokid = sb("tokid", [P, TT], i32)
        lg = sb("lg", [P, TT, E])
        m8 = sb("m8", [P, TT, 8])
        i8 = sb("i8", [P, TT, 8], u32)
        i8f = sb("i8f", [P, TT, 8])
        Msel = sb("Msel", [P, TT, E])
        nm0 = sb("nm0", [P, TT])
        gate = sb("gate", [P, TT, TOPK])
        gsum = sb("gsum", [P, TT])
        cnt = sb("cnt", [P, E])
        ovf_end = sb("ovf_end", [P, E])
        ovf_base = sb("ovf_base", [P, E])
        pos = sb("pos", [P, E])
        qd = sb("qd", [P, E])
        slotm = sb("slotm", [P, E])
        slotk = sb("slotk", [P, TOPK, E])
        slotf = sb("slotf", [P, TT, TOPK])
        sloti = sb("sloti", [P, TT, TOPK], i32)
        ovexp = sb("ovexp", [P, NOVF])
        blkexp = sb("blkexp", [P, NOVF], i32)
        pairs_f = sb("pairs_f", [P, 2])
        pairs_i = sb("pairs_i", [P, 1], i32)
        idx_all = sb("idx_all", [NS, ROWB], i32)
        idx = sb("idx", [NS, 2], i32)

        bank = [ctx.enter_context(nc.psum_tensor(f"bank{b}", [P, 512], f32)) for b in range(8)]

        bank_full = [sem(f"bank_full{b}") for b in range(8)]
        bank_free = [sem(f"bank_free{b}") for b in range(8)]
        x_in = [sem(f"x_in{t}") for t in range(TT)]
        vec_in = sem("vec_in")
        bias_in = sem("bias_in")
        small_in = sem("small_in")
        w_in_loaded = [sem(f"w_in_loaded{s}") for s in range(2)]
        ff_in = sem("ff_in")
        w_out_loaded = [sem(f"w_out_loaded{s}") for s in range(2)]
        pool_step = sem("pool_step")
        consts_ready = sem("consts_ready")
        dve_step = sem("dve_step")
        act_step = sem("act_step")
        vec_ready = sem("vec_ready")
        hrow_ready = sem("hrow_ready")
        act_sq = sem("act_sq")
        sumsq_ready = sem("sumsq_ready")
        mixed = sem("mixed")
        lora_ready = sem("lora_ready")
        cum_ready = sem("cum_ready")
        kksq_ready = sem("kksq_ready")
        kksum_ready = sem("kksum_ready")
        kknorm_ready = sem("kknorm_ready")
        fox_ms_ready = sem("fox_ms_ready")
        fox_rms_ready = sem("fox_rms_ready")
        gn_var_ready = sem("gn_var_ready")
        gn_std_ready = sem("gn_std_ready")
        exps_ready = sem("exps_ready")
        elem_done = sem("elem_done")
        ffln_ready = sem("ffln_ready")
        nlf_ready = sem("nlf_ready")
        c3_ready = sem("c3_ready")
        negmax_ready = sem("negmax_ready")
        fo_ready = sem("fo_ready")
        values_done = sem("values_done")
        fox_o_free = sem("fox_o_free")
        scm_ready = sem("scm_ready")
        xt0_ready = sem("xt0_ready")
        ct_ready = sem("ct_ready")
        state_ready = sem("state_ready")
        gn_rstd_ready = sem("gn_rstd_ready")
        scores_masked = sem("scores_masked")
        y_ready = sem("y_ready")
        gates_ready = sem("gates_ready")
        gmax_ready = sem("gmax_ready")
        sel_ready = sem("sel_ready")
        slots_ready = sem("slots_ready")
        tables_ready = sem("tables_ready")
        zeros_stored = sem("zeros_stored")
        rows_zeroed = sem("rows_zeroed")
        tokens_stored = sem("tokens_stored")
        idx_in = sem("idx_in")
        h2_stored = [sem(f"h2_stored{t}") for t in range(TT)]
        idx_copied = sem("idx_copied")
        waited = sem("waited")
        xg_loaded = [sem(f"xg_loaded{q}") for q in range(2)]
        raw_loaded = [sem(f"raw_loaded{r}") for r in range(RAW)]
        hi_ready = sem("hi_ready")
        lo_ready = [sem(f"lo_ready{n}") for n in range(2)]
        unit_used = sem("unit_used")
        bias_split = sem("bias_split")
        xt_full = sem("xt_full")
        xt_free = sem("xt_free")
        x_hi_ready = sem("x_hi_ready")
        x_lo_ready = sem("x_lo_ready")
        sel_set = sem("sel_set")
        hid_free = [sem(f"hid_free{p}") for p in range(2)]
        glu_ready = sem("glu_ready")
        sig_ready = sem("sig_ready")
        lin_ready = sem("lin_ready")
        act_ready = sem("act_ready")
        at_full = sem("at_full")
        a_hi_ready = sem("a_hi_ready")
        a_lo_ready = sem("a_lo_ready")
        y_free = [sem(f"y_free{p}") for p in range(2)]
        store_done = [sem(f"store_done{q}") for q in range(2)]
        gathered = [sem(f"gathered{t}") for t in range(TT)]
        gfin_in = sem("gfin_in")
        summed = sem("summed")
        normed = sem("normed")
        out_ready = sem("out_ready")
        out_stored = [sem(f"out_stored{t}") for t in range(TT)]

        plan, uses = {}, [0] * 8

        def put(name, b):
            plan[name] = (b, uses[b])
            uses[b] += 1

        U_ORDER = [12, 13, 14, 15, 0, 1, 2, 3, 4, 5, 6, 7, 8, 9, 10, 11, 16, 17, 18, 19, 20, 21]
        put(("vec",), 0)
        for tt in range(TT):
            for half in range(2):
                put(("hT", tt, half), (1 + 2 * tt + half) % 4)
        nrot = 0

        def rot(name):
            nonlocal nrot
            put(name, nrot % 8)
            nrot += 1

        for m in U_ORDER:
            rot(("u", m))
            if m == 3:
                for j in range(JT):
                    rot(("z", j))
                for j in range(JT):
                    rot(("a", j))
            if m == 11:
                for j in range(JT):
                    rot(("ss", j))
                for tt in range(TT):
                    rot(("g", tt))
        for tt in range(TT):
            rot(("fv", tt))
        rot(("ff",))
        rot(("bonus",))
        rot(("cT",))
        units = [(qb, h) for qb in range(TT) for h in range(H)]
        uses_before_fox = list(uses)
        for i, (qb, h) in enumerate(units):
            put(("S", qb, h), i % 2)
            put(("PT", qb, h), 2 + i % 2)
            if h == H - 1:
                put(("foT", qb), 6)
        def inversion(pair):
            st = [("L", tt, g) for tt in pair for g in range(2)]
            st += [("X0", tt, hf) for tt in pair for hf in range(2)]
            for lv in range(1, LEVELS):
                st += [("P", tt, lv, hf) for tt in pair for hf in range(2)]
                for tt in pair:
                    for hf in range(2):
                        if lv < LEVELS - 1:
                            st.append(("X", tt, lv, hf))
                        st.append(("XT", tt, lv, hf))
            return st

        def prepare(tt):
            return [("vt", tt), ("bt", tt), ("kt", tt), ("at", tt)] \
                + [("KAR", tt, g, jj) for jj in range(2) for g in range(2)] + [("BR", tt, g) for g in range(2)] \
                + [("MV", tt), ("W", tt)]

        def between(a, b):
            st, taken = [], 0
            for n, stage in enumerate(a):
                st.append(stage)
                while taken * len(a) < (n + 1) * len(b) and taken < len(b):
                    st.append(b[taken])
                    taken += 1
            return st

        rwkv_stages = inversion((0, 1))
        rwkv_stages += between(inversion((2, 3)),
                               prepare(0) + [("U", 0), ("Yfrom", 0), ("state", 0), ("Y", 0)]
                               + prepare(1) + [("U", 1), ("yT", 0), ("Yfrom", 1), ("state", 1), ("Y", 1)]
                               + prepare(2)[:-1])
        rwkv_stages += [("W", 2)] + between(prepare(3), [("U", 2), ("Yfrom", 2), ("state", 2), ("yT", 1), ("Y", 2)])
        rwkv_stages += [("U", 3), ("o", 0, 0), ("Yfrom", 3), ("o", 0, 1), ("yT", 2), ("Y", 3), ("norm", 0),
                        ("o", 1, 0), ("h2T", 0, 0), ("h2T", 0, 1), ("o", 1, 1), ("lg", 0), ("norm", 1),
                        ("yT", 3), ("o", 2, 0), ("h2T", 1, 0), ("h2T", 1, 1), ("o", 2, 1), ("lg", 1), ("norm", 2),
                        ("o", 3, 0), ("h2T", 2, 0), ("h2T", 2, 1), ("o", 3, 1), ("lg", 2), ("norm", 3),
                        ("h2T", 3, 0), ("h2T", 3, 1), ("lg", 3)]
        nth_of = {0: 0, 1: 0, "r": 0}
        for st in rwkv_stages:
            kind, tt = st[0], st[1]
            if kind in ("L", "X0", "P", "X", "XT"):
                put(st, 3 * (tt % 2) + nth_of[tt % 2] % 3)
                nth_of[tt % 2] += 1
            elif kind == "Yfrom":
                put(("Y", tt), 7)
            elif kind in ("U", "state", "yT") or kind in ("vt", "bt", "kt", "at", "KAR", "BR", "MV", "W") and tt < 3:
                put(st, 6)
            elif kind not in ("Y", "norm"):
                put(st, nth_of["r"] % 6)
                nth_of["r"] += 1
        put(("cnt",), 7)
        for tt in range(TT):
            put(("pos", tt), tt % 2)

        def filled(eng, *name):
            b, n = plan[name]
            eng.wait_ge(bank_full[b], n + 1)

        def emptied(eng, *name):
            b, n = plan[name]
            eng.wait_ge(bank_free[b], n + 1)

        def free_of(name):
            return bank_free[plan[name][0]]

        def by_gpsimd(n):
            return n % 3 == 1

        def low_part(i, n):
            m = 2 * UNITS // 3 * i
            if by_gpsimd(n):
                return lo_ready[1], m + (n // 3 + 1 + RAW // 3)
            return lo_ready[0], m * 2 + (n // 3 * 2 + 1 + (n % 3 == 2) + RAW // 3 * 2)

        def wait_used(eng, i, n):
            eng.wait_ge(unit_used, i * (2 * UNITS) + (n + 1 + HI))

        block = ctx.enter_context(nc.Block())

        W_CHUNKS = [3, 0, 1, 2, 4, 5, 6]
        W1_T = w1[0].rearrange("e (k p) f -> p e k f", p=P)
        W2_T = w2[0].rearrange("e (k p) f -> p e k f", p=P)

        def load_unit(eng, e, n):
            c, kh = UNIT_OF[n % UNITS]
            src, off = (W1_T, c * CW) if c < W1C else (W2_T, (c - W1C) * CW)
            k = slice(kh * KT // 2, (kh + 1) * KT // 2)
            eng.dma_start(raw[n % RAW], src[:, bass.ds(e, 1), k, off:off + CW].rearrange("p a k f -> p (a k) f"))\
               .then_inc(raw_loaded[n % RAW], 16)

        @block.sync
        def _(sp):
            for tt in range(TT):
                sp.dma_start(xs[:, tt, :], x[0, tt * P:(tt + 1) * P, :]).then_inc(x_in[tt], 16)
            w_in_v = w_in[0].rearrange("(k p) f -> p k f", p=P)
            for n, ch in enumerate(W_CHUNKS):
                if n >= 2:
                    filled(sp, "u", [m for m in U_ORDER if m // 4 == W_CHUNKS[n - 2]][-1])
                lo = ch * CW
                if ch == 5:
                    sp.dma_start(slots[:, n % 2, :, 0:256], w_in_v[:, :, lo:lo + 256]).then_inc(w_in_loaded[n % 2], 16)
                elif ch == 6:
                    sp.dma_start(slots[:, n % 2], w_in_v[:, :, lo - 256:lo + 256]).then_inc(w_in_loaded[n % 2], 16)
                else:
                    sp.dma_start(slots[:, n % 2], w_in_v[:, :, lo:lo + CW]).then_inc(w_in_loaded[n % 2], 16)
            w_out_v = w_out[0].rearrange("(k p) f -> p k f", p=P)
            for half in range(2):
                if half == 0:
                    filled(sp, "fv", TT - 1)
                else:
                    filled(sp, "XT", TT - 1, LEVELS - 1, 1)
                sp.dma_start(slots[:, half], w_out_v[:, :, half * CW:(half + 1) * CW]).then_inc(w_out_loaded[half], 16)
            filled(sp, "yT", TT - 1)
            emptied(sp, "Y", TT - 1)
            for n in range(RAW):
                load_unit(sp, 0, n)
            filled(sp, "o", TT - 1, 0)
            for g in range(2):
                sp.dma_start(biasrows[g * E:(g + 1) * E, 0:F2], b1[0]).then_inc(bias_in, 16)
                sp.dma_start(biasrows[g * E:(g + 1) * E, F2:F2 + D], b2[0]).then_inc(bias_in, 16)

            def next_units(i, q, e, first=0):
                for u in range(first, UNITS):
                    n = q * UNITS + u
                    sp.wait_ge(*low_part(i, n - RAW))
                    load_unit(sp, e, n)

            next_units(0, 0, 0, RAW)
            next_units(0, 1, 1)
            with sp.Fori(1, E // 2) as i:
                for q in range(2):
                    next_units(i, q, i * 2 + q)
            sp.wait_ge(tables_ready, 1)
            npairs = sp.value_load(pairs_i[0:1, 0:1], min_val=E // 2, max_val=NB // 2)
            with sp.Fori(E // 2, NB // 2) as i:
                with sp.If(i < npairs):
                    for q in range(2):
                        e = sp.value_load(blkexp[0:1, bass.ds(i * 2 + (q - E), 1)], min_val=0, max_val=E - 1)
                        next_units(i, q, e)
            for tt in range(TT):
                sp.wait_ge(out_ready, tt + 1)
                sp.dma_start(out[0, tt * P:(tt + 1) * P, :], outb[tt % 2]).then_inc(out_stored[tt], 16)
            for tt in range(TT):
                sp.wait_ge(out_stored[tt], 16)

        @block.gpsimd
        def _(pool):
            steps = [0]

            def step(ins):
                steps[0] += 1
                ins.then_inc(pool_step, 1)
                pool.wait_ge(pool_step, steps[0])

            def select(dst, pattern, op, fill, base, cm):
                step(nc.gpsimd.affine_select(out=dst, in_=dst, compare_op=op, fill=fill, base=base,
                                             pattern=pattern, channel_multiplier=cm))

            step(nc.gpsimd.memset(eps[:, 0:1], RMS_EPS))
            step(nc.gpsimd.memset(eps[:, 1:2], GN_EPS))
            step(nc.gpsimd.memset(ident[:, :], 0.0))
            select(ident[:, :], [[-1, P]], ALU.not_equal, 1.0, 0, 1)
            pool.sem_inc(consts_ready, 1)
            step(nc.gpsimd.memset(shiftbuf[:, :, 0:1], 0.0))
            step(nc.gpsimd.memset(blk[:, :], 0.0))
            step(nc.gpsimd.memset(blk[0:N, 0:N], 1.0))
            step(nc.gpsimd.memset(blk[N:P, N:P], 1.0))
            pool.sem_inc(consts_ready, 1)
            step(nc.gpsimd.memset(zrow, 0.0))
            for o in range(NOVF):
                pool.dma_start(expert_rows[(E + o + 1) * NS:(E + o + 2) * NS, :], zrow[0:NS, :]).then_inc(rows_zeroed, 16)
            step(nc.gpsimd.memset(stepm[:, :], 1.0))
            select(stepm[:, :], [[1, OFF + T]], ALU.is_ge, 0.0, -OFF, -1)
            step(nc.gpsimd.memset(identb[:, :], 0.0))
            select(identb[:, :], [[-1, P]], ALU.not_equal, 1.0, 0, 1)
            step(nc.gpsimd.memset(causal[:, :], 0.0))
            select(causal[:, :], [[-1, P]], ALU.is_ge, -1e30, 0, 1)
            step(nc.gpsimd.memset(selh[:, :, :], 0.0))
            for g in range(3):
                select(selh[:, :, :], [[-1, H], [0, P]], ALU.not_equal, 1.0, -32 * g, 1)
            step(nc.gpsimd.memset(c3[:, :], 0.0))
            step(nc.gpsimd.memset(maskSC[:, :], 1.0))
            select(maskSC[:, 0:C], [[1, C]], ALU.is_ge, 0.0, -1, -1)
            select(maskSC[:, C:2 * C], [[1, C]], ALU.is_ge, 0.0, 0, -1)
            step(nc.gpsimd.memset(blocks[:, :, :], 1.0))
            for lv in range(LEVELS):
                w = 1 << lv
                select(blocks[:, lv, :], [[-w, C // w], [0, w]], ALU.is_ge, 0.0, 0, 1)
                select(blocks[:, lv, :], [[w, C // w], [0, w]], ALU.is_ge, 0.0, w - 1, -1)
            step(nc.gpsimd.tensor_tensor(levmask[:, :, :], blocks[:, 1:, :], blocks[:, 0:LEVELS, :], ALU.subtract))
            pool.sem_inc(consts_ready, 1)
            step(nc.gpsimd.iota(iotaEi[:, :], pattern=[[1, E]], base=0, channel_multiplier=0))
            step(nc.gpsimd.iota(iotaOi[:, :], pattern=[[1, NOVF]], base=0, channel_multiplier=0))
            step(nc.gpsimd.iota(tokid[:, :], pattern=[[P, TT]], base=0, channel_multiplier=1))
            step(nc.gpsimd.tensor_copy(iotaE[:, :], iotaEi[:, :]))
            step(nc.gpsimd.tensor_copy(iotaO[:, :], iotaOi[:, :]))
            step(nc.gpsimd.memset(zero_i[:, :], 0))
            pool.sem_inc(consts_ready, 1)
            nrow = ROWB * NS // P
            pool.dma_start(slot_tokens.rearrange("(p n) a -> p (n a)", p=P), zero_i[:, 0:nrow]).then_inc(zeros_stored, 16)

            for st in rwkv_stages:
                kind, tt = st[0], st[1]
                if kind == "X0" and st[2] == 1 or kind == "P" and st[3] == 1 and st[2] < LEVELS - 1:
                    lv = 1 if kind == "X0" else st[2] + 1
                    if lv == 1:
                        pool.wait_ge(scm_ready, tt + 1)
                        if tt >= 2:
                            filled(pool, "P", tt - 2, LEVELS - 1, 1)
                    else:
                        filled(pool, *st)
                    nc.gpsimd.tensor_tensor(CT[:, tt % 2], Lm[:, tt % 2],
                                            levmask[:, lv, :].unsqueeze(1).to_broadcast([C, H, C]), ALU.mult)\
                        .then_inc(ct_ready, 1)
                if kind == "yT":
                    def heads(ap):
                        return ap.rearrange("p (h v) -> p h v", h=H)
                    pool.wait_ge(gn_rstd_ready, tt + 1)
                    emptied(pool, "vt", tt)
                    emptied(pool, "bonus")
                    emptied(pool, "g", tt)
                    step(nc.gpsimd.tensor_tensor(heads(Yc), heads(Yc), gst[:, 1, :].unsqueeze(2).to_broadcast([P, H, N]), ALU.mult))
                    step(nc.gpsimd.tensor_tensor(heads(Yq), heads(V[tt % 2]),
                                                 bonus[:, tt, :].unsqueeze(2).to_broadcast([P, H, N]), ALU.mult))
                    step(nc.gpsimd.tensor_tensor(Yc, Yc, lnw[:, :], ALU.mult))
                    step(nc.gpsimd.tensor_tensor(Yq, Yq, lnb[:, :], ALU.add))
                    step(nc.gpsimd.tensor_tensor(Yc, Yc, Yq, ALU.add))
                    nc.gpsimd.tensor_tensor(Yq, Yc, G[:, tt, :], ALU.mult).then_inc(y_ready, 1)

            pool.wait_ge(zeros_stored, 16)
            for tt in range(TT):
                pool.wait_ge(slots_ready, tt + 1)
                for k in range(TOPK):
                    pool.indirect_dma_start(
                        slot_tokens, bass.IndirectOffsetOnAxis(ap=sloti[:, tt, k:k + 1], axis=0),
                        tokid[:, tt:tt + 1], None).then_inc(tokens_stored, 16)
            pool.wait_ge(tokens_stored, 16 * TT * TOPK)
            pool.dma_start(idx_all[:, :], slot_tokens.rearrange("(b s) a -> s (b a)", s=NS),
                           allow_slow_non_contiguous=True).then_inc(idx_in, 16)
            pool.wait_ge(idx_in, 16)
            for tt in range(TT):
                pool.wait_ge(h2_stored[tt], 16)

            def gather(b, q, reused=True):
                if reused:
                    pool.wait_ge(xt_full, b)
                    pool.sem_inc(waited, 1)
                nc.gpsimd.tensor_copy(idx[:, q:q + 1], idx_all[:, bass.ds(b + 1, 1)]).then_inc(idx_copied, 1)
                pool.wait_ge(idx_copied, b + 1)
                pool.sem_inc(waited, 1)
                pool.indirect_dma_start(xg[0:NS, q, :], None, h2_rows,
                                        bass.IndirectOffsetOnAxis(ap=idx[:, q:q + 1], axis=0))\
                    .then_inc(xg_loaded[q], 16)

            def low_parts(i, n):
                wait_used(pool, i, n - LO)
                pool.wait_ge(hi_ready, i * (2 * UNITS) + (n + 1))
                nc.gpsimd.tensor_tensor(w_lo[n % LO][:, :, :], raw[n % RAW], w_hi[n % HI][:, :, :], ALU.subtract)\
                    .then_inc(lo_ready[1], 1)

            def block_work(i, q):
                for u in range(UNITS):
                    n = q * UNITS + u
                    if by_gpsimd(n):
                        low_parts(i, n)
                    if u == 1:
                        gather(i * 2 + (q + 1), 1 - q)

            gather(0, 0, False)
            pool.sem_inc(lo_ready[1], RAW // 3)
            pool.wait_ge(bias_split, 1)
            with pool.Fori(0, E // 2) as i:
                for q in range(2):
                    block_work(i, q)
            npairs = pool.value_load(pairs_i[0:1, 0:1], min_val=E // 2, max_val=NB // 2)
            with pool.Fori(E // 2, NB // 2) as i:
                with pool.If(i < npairs):
                    for q in range(2):
                        block_work(i, q)
            for q in range(2):
                pool.wait_ge(store_done[q], npairs * 16 + (16 + 16 * q))
            pool.sem_inc(waited, 1)
            for tt in range(TT):
                for k in range(TOPK):
                    pool.indirect_dma_start(
                        slots[:, tt, 2 * k:2 * k + 2, :].rearrange("p a f -> p (a f)"), None, expert_rows,
                        bass.IndirectOffsetOnAxis(ap=sloti[:, tt, k:k + 1], axis=0)).then_inc(gathered[tt], 16)

        def fox_rms(act, qb):
            act.wait_ge(fox_ms_ready, qb + 1)
            nc.scalar.activation(fst[:, :], fst[:, :], ACT.Sqrt, bias=eps[:, 0:1], scale=1.0 / N).then_inc(fox_rms_ready, 1)

        def fox_out_T(act, qb):
            filled(act, "foT", qb)
            for j in range(JT):
                ins = nc.scalar.mul(hT[:, JT + j, qb * P:(qb + 1) * P], bank[6][:, j * P:(j + 1) * P], vec("og", j))
            ins.then_inc(free_of(("foT", qb)), 1)

        @block.scalar
        def _(act):
            at = 0
            for src in (attn_norm_g, mu, w0, a0, k_k, k_a, None, out_g, ffn_norm_g):
                v = r_k[0].rearrange("h n -> (h n)") if src is None else src[0]
                n = v.shape[0] // P
                act.dma_start(vec_rows[at:at + n, :], v.rearrange("(j p) -> j p", p=P)).then_inc(vec_in, 16)
                at += n
            act.dma_start(wff[:, :, :], w_in[0, :, w_in.shape[2] - H:].rearrange("(k p) f -> p k f", p=P)).then_inc(ff_in, 16)
            act.dma_start(lora_up[0:LORA, :], w_up[0]).then_inc(small_in, 16)
            act.dma_start(lora_up[LORA:P, :], a_up[0]).then_inc(small_in, 16)
            act.dma_start(gup, g_up[0]).then_inc(small_in, 16)
            act.dma_start(lnw[:, :], ln_w.to_broadcast([P, HW])).then_inc(small_in, 16)
            act.dma_start(lnb[:, :], ln_b.to_broadcast([P, HW])).then_inc(small_in, 16)
            act.dma_start(rw[:, :, :], router_w[0].rearrange("(k p) e -> p k e", p=P)).then_inc(small_in, 16)
            act.dma_start(rb[:, :], router_b.to_broadcast([P, E])).then_inc(small_in, 16)
            act.dma_start(fb[:, :], f_bias.to_broadcast([P, H])).then_inc(small_in, 16)
            steps = [0]

            def step(ins):
                steps[0] += 1
                ins.then_inc(act_step, 1)
                act.wait_ge(act_step, steps[0])

            def root_mean(tt, n, done):
                act.wait_ge(act_sq, n)
                nc.scalar.activation(ss[:, tt:tt + 1], ss[:, tt:tt + 1], ACT.Sqrt, bias=eps[:, 0:1], scale=1.0 / D)\
                    .then_inc(done, 1)

            act.wait_ge(consts_ready, 1)
            for tt in range(TT):
                act.wait_ge(x_in[tt], 16)
                nc.scalar.activation(junk, xs[:, tt, :], ACT.Square, accum_out=ss[:, tt:tt + 1]).then_inc(act_sq, 1)
                root_mean(tt, tt + 1, sumsq_ready)
            act.wait_ge(vec_ready, 1)
            act.wait_ge(consts_ready, 3)
            nth = 0
            for m in U_ORDER:
                filled(act, "u", m)
                src = bank[plan[("u", m)][0]][:, :]
                if m < 14:
                    if nth >= 2:
                        act.wait_ge(mixed, nth - 1)
                    nc.scalar.copy(shiftbuf[:, nth % 2, 1:T + 1], src).then_inc(free_of(("u", m)), 1)
                    nth += 1
                elif m < 18:
                    nc.scalar.mul(qk[:, 0, m - 14, :], src, float(N) ** -0.5).then_inc(free_of(("u", m)), 1)
                else:
                    nc.scalar.copy(qk[:, 1, m - 18, :], src).then_inc(free_of(("u", m)), 1)
                if m == 13:
                    act.wait_ge(mixed, 2)
                    step(nc.scalar.activation(wa[0:LORA, :], wa[0:LORA, :], ACT.Tanh))
                    step(nc.scalar.activation(gl, gl, ACT.Sigmoid))
                    act.sem_inc(lora_ready, 1)
                if m == 3:
                    act.wait_ge(rows_zeroed, 16 * NOVF)
                    for nm, dst, bias in (("z", decay_s, "w0"), ("a", aT, "a0")):
                        for j in range(JT):
                            filled(act, nm, j)
                            nc.scalar.activation(dst[:, j, :], bank[plan[(nm, j)][0]][:, :], ACT.Sigmoid,
                                                 bias=vec(bias, j)).then_inc(free_of((nm, j)), 1)
                if m == 11:
                    for j in range(JT):
                        act.wait_ge(kksum_ready, j + 1)
                        nc.scalar.activation(AR[:, j, :, 0:C], AR[:, j, :, 0:C], ACT.Sqrt).then_inc(kknorm_ready, 1)
                    for tt in range(TT):
                        filled(act, "g", tt)
                        nc.scalar.copy(G[:, tt, :], bank[plan[("g", tt)][0]][:, :]).then_inc(free_of(("g", tt)), 1)
                    for j in range(JT):
                        act.wait_ge(cum_ready, j + 1)
                        step(nc.scalar.activation(decay_e[:, j, :], decay_c[:, j, :], ACT.Exp, scale=-KAPPA))
                        step(nc.scalar.activation(decay_c[:, j, :], decay_c[:, j, :], ACT.Exp, scale=KAPPA))
                        step(nc.scalar.activation(dend[:, j, 0:NC - 1], dend[:, j, 0:NC - 1], ACT.Exp, scale=-KAPPA))
                        nc.scalar.activation(decay_s[:, j, :], decay_s[:, j, :], ACT.Exp, scale=-KAPPA).then_inc(exps_ready, 1)
            for tt in range(TT):
                filled(act, "fv", tt)
                nc.scalar.copy(foxv[:, tt, :], bank[plan[("fv", tt)][0]][:, :]).then_inc(free_of(("fv", tt)), 1)
            emptied(act, "ff")
            step(nc.scalar.activation(ffz[:, 1], ffz[:, 0], ACT.Abs))
            step(nc.scalar.activation(ffz[:, 2], ffz[:, 1], ACT.Exp, scale=-1.0))
            nc.scalar.activation(ffz[:, 3], ffz[:, 2], ACT.Ln, bias=1.0).then_inc(ffln_ready, 1)
            filled(act, "bonus")
            nc.scalar.copy(bonus[:, :, :], bank[plan[("bonus",)][0]][:, 0:TT * H].rearrange("p (t h) -> p t h", h=H))\
                .then_inc(free_of(("bonus",)), 1)
            act.wait_ge(elem_done, JT)
            for i, (qb, h) in enumerate(units):
                keys = (qb + 1) * P
                act.wait_ge(negmax_ready, i + 1)
                if i >= 2:
                    filled(act, "PT", *units[i - 2])
                nc.scalar.activation(fP[:, i % 2, 0:keys], bank[i % 2][:, 0:keys], ACT.Exp, bias=nmx[:, i:i + 1],
                                     accum_out=rsum[:, i:i + 1]).then_inc(free_of(("S", qb, h)), 1)
                if h == 1 and qb > 0:
                    fox_rms(act, qb - 1)
                if h == 2 and qb > 0:
                    fox_out_T(act, qb - 1)
            fox_rms(act, TT - 1)
            fox_out_T(act, TT - 1)

            def move(name, dst, src):
                filled(act, *name)
                nc.scalar.copy(dst, src).then_inc(free_of(name), 1)

            def four_heads(ap, hf):
                return ap[:, 4 * hf:4 * hf + 4, :].rearrange("p h t -> p (h t)")

            for st in rwkv_stages:
                kind, tt, q = st[0], st[1], st[1] % 2
                ps = bank[plan[st][0]][:, :] if st in plan else None
                if kind == "X0":
                    move(st, four_heads(Xm[:, q], st[2]), ps)
                elif kind == "P":
                    move(st, four_heads(Pm[:, q], st[3]), ps)
                elif kind == "vt":
                    if tt >= 2:
                        act.wait_ge(y_ready, tt - 1)
                    move(st, V[q], ps)
                elif kind == "o":
                    if st[2] == 1:
                        emptied(act, "o", tt, 1)
                        emptied(act, "o", tt, 0)
                        nc.scalar.activation(squares, xs[:, tt, :], ACT.Square, accum_out=ss[:, tt:tt + 1]).then_inc(act_sq, 1)
                        root_mean(tt, TT + tt + 1, sumsq_ready)
                elif kind == "norm":
                    act.wait_ge(hrow_ready, TT + tt + 1)
                    act.dma_start(h2_rows[tt * P:(tt + 1) * P, :], hrow[:, tt % 2, :]).then_inc(h2_stored[tt], 16)
                elif kind == "lg":
                    act.wait_ge(gmax_ready, tt + 1)
                    nc.scalar.activation(gate[:, tt, :], m8[:, tt, 0:TOPK], ACT.Exp, bias=nm0[:, tt:tt + 1],
                                         accum_out=gsum[:, tt:tt + 1]).then_inc(gates_ready, 1)
                elif kind in ("bt", "kt"):
                    if 0 < tt < NC - 1:
                        filled(act, "state", tt - 1)
                    move(st, (Btok if kind == "bt" else Ktok)[tt], ps)
                elif kind == "at":
                    move(st, Atok[tt], ps)
                elif kind == "W":
                    move(st, WT[tt], ps.rearrange("p (j t) -> p j t", j=JT))
                elif kind == "MV":
                    move(st, MV[tt], ps)
                elif kind == "Y":
                    act.wait_ge(gn_var_ready, tt + 1)
                    nc.scalar.activation(gst[:, 1, :], gst[:, 1, :], ACT.Sqrt, bias=eps[:, 1:2], scale=1.0 / N)\
                        .then_inc(gn_std_ready, 1)
                elif kind == "yT":
                    move(st, hT[:, 0:JT, tt * P:(tt + 1) * P], ps.rearrange("p (j t) -> p j t", j=JT))
            act.wait_ge(bias_in, 64)
            act.wait_ge(tables_ready, 1)
            nc.scalar.copy(b1r[:, :], biasrows[0:2 * E, 0:F2])
            nc.scalar.copy(b2r[:, :], biasrows[0:2 * E, F2:F2 + D]).then_inc(bias_split, 1)

            def high_part(i, n):
                r = n % RAW
                act.wait_ge(raw_loaded[r], i * (2 * UNITS // RAW * 16) + (n // RAW + 1) * 16)
                wait_used(act, i, n - HI)
                nc.scalar.copy(w_hi[n % HI][:, :, :], raw[r]).then_inc(hi_ready, 1)

            def x_high(b):
                act.wait_ge(xt_free, b + 2)
                nc.scalar.copy(x_hi[:, :, :], xTf.rearrange("p (k s) -> p k s", k=KT)).then_inc(x_hi_ready, 1)

            def act_high(b, c):
                act.wait_ge(at_full, b * W1C + (c + 1))
                o = c // 2 * 2 * NS
                nc.scalar.copy(a_hi[:, 2 * c:2 * c + 2, :], bank[4 + c % 2][:, o:o + 2 * NS].rearrange("p (f s) -> p f s", f=2))\
                    .then_inc(a_hi_ready, 1)

            def store_previous(i, q):
                b = i * 2 + q
                act.wait_ge(store_done[1 - q], i * 16 + 16)
                wait_used(act, i, q * UNITS - 1)
                for h in range(2):
                    nc.scalar.copy(ob[0:NS, 1 - q, h * CW:(h + 1) * CW], bank[6 + h][0:NS, :]).then_inc(y_free[h], 1)
                for h in range(2):
                    act.wait_ge(y_free[h], b + 1)
                act.dma_start(expert_rows[bass.ds(b * NS, NS), :], ob[0:NS, 1 - q, :]).then_inc(store_done[1 - q], 16)

            def block_work(i, q):
                b = i * 2 + q
                for u in range(UNITS):
                    high_part(i, q * UNITS + u)
                    if u == 3:
                        store_previous(i, q)
                    if u in (5, 7, 9, 11):
                        c = (u - 5) // 2
                        act.wait_ge(glu_ready, b * W1C + (c + 1))
                        nc.scalar.activation(hs[0:NS, c % 2], hg[0:NS, c % 2], ACT.Sigmoid, scale=1.702).then_inc(sig_ready, 1)
                    if u in (8, 10, 11):
                        act_high(b, {8: 0, 10: 1, 11: 2}[u])
                x_high(b + 1)
                act_high(b, 3)

            act.wait_ge(bias_split, 2)
            for q in range(2):
                act.sem_inc(store_done[q], 16)
            x_high(0)
            with act.Fori(0, E // 2) as i:
                for q in range(2):
                    block_work(i, q)
            npairs = act.value_load(pairs_i[0:1, 0:1], min_val=E // 2, max_val=NB // 2)
            with act.Fori(E // 2, NB // 2) as i:
                with act.If(i < npairs):
                    for q in range(2):
                        block_work(i, q)
            store_previous(npairs, 0)
            act.dma_start(gfin, final_norm_g.rearrange("(a d) -> a d", a=1).to_broadcast([P, D])).then_inc(gfin_in, 16)
            for tt in range(TT):
                act.wait_ge(summed, tt + 1)
                nc.scalar.activation(junk, xs[:, tt, :], ACT.Square, accum_out=ss[:, tt:tt + 1]).then_inc(act_sq, 1)
                root_mean(tt, 2 * TT + tt + 1, normed)

        @block.tensor
        def _(pe):
            def begin(*name):
                b, n = plan[name]
                if n > 0:
                    pe.wait_ge(bank_free[b], n)
                return bank[b]

            def end(ins, *name):
                ins.then_inc(bank_full[plan[name][0]], 1)

            pe.wait_ge(consts_ready, 1)
            pe.wait_ge(vec_in, 16 * 9)
            ps = begin("vec")
            end(nc.tensor.transpose(ps[:, 0:vrow], vec_rows[:, :], ident[0:vrow, 0:vrow]), "vec")
            for tt in range(TT):
                pe.wait_ge(hrow_ready, tt + 1)
                for half in range(2):
                    ps = begin("hT", tt, half)
                    for k in range(4):
                        o = (half * 4 + k) * P
                        ins = nc.tensor.transpose(ps[:, k * P:(k + 1) * P], hrow[:, tt % 2, o:o + P], ident[:, :])
                    end(ins, "hT", tt, half)
            for tt in range(TT):
                emptied(pe, "hT", tt, 0)
                emptied(pe, "hT", tt, 1)
            pe.wait_ge(small_in, 16 * 8)
            chunk = -1
            for nth, m in enumerate(U_ORDER):
                ch = m // 4
                if nth == 0 or U_ORDER[nth - 1] // 4 != ch:
                    chunk += 1
                    pe.wait_ge(w_in_loaded[chunk % 2], 16 * (chunk // 2 + 1))
                ps = begin("u", m)
                col = (m % 4) * P
                for k in range(KT):
                    ins = nc.tensor.matmul(ps[:, :], slots[:, chunk % 2, k, col:col + P], hT[:, k, :],
                                           start=(k == 0), stop=(k == KT - 1))
                end(ins, "u", m)
                if m == 3:
                    pe.wait_ge(lora_ready, 1)
                    for nm, lo in (("z", 0), ("a", LORA)):
                        for j in range(JT):
                            ps = begin(nm, j)
                            end(nc.tensor.matmul(ps[:, :], lora_up[lo:lo + LORA, j * P:(j + 1) * P],
                                                 wa[lo:lo + LORA, :], start=True, stop=True), nm, j)
                if m == 11:
                    for j in range(JT):
                        ps = begin("ss", j)
                        pe.wait_ge(kksq_ready, j + 1)
                        end(nc.tensor.matmul(ps[:, :], blk[:, :], AR[:, j, :, 0:C], start=True, stop=True), "ss", j)
                    for tt in range(TT):
                        ps = begin("g", tt)
                        end(nc.tensor.matmul(ps[:, :], gl[:, tt * P:(tt + 1) * P], gup, start=True, stop=True), "g", tt)
            chunk += 1
            pe.wait_ge(w_in_loaded[chunk % 2], 16 * (chunk // 2 + 1))
            for tt in range(TT):
                ps = begin("fv", tt)
                for k in range(KT):
                    ins = nc.tensor.matmul(ps[:, :], hT[:, k, tt * P:(tt + 1) * P], slots[:, chunk % 2, k, :],
                                           start=(k == 0), stop=(k == KT - 1))
                end(ins, "fv", tt)
            pe.wait_ge(ff_in, 16)
            ps = begin("ff")
            for tt in range(TT):
                for k in range(KT):
                    ins = nc.tensor.matmul(ps[:, tt * H:(tt + 1) * H], hT[:, k, tt * P:(tt + 1) * P], wff[:, k, :],
                                           start=(k == 0), stop=(k == KT - 1))
            end(ins, "ff")
            pe.wait_ge(elem_done, JT)
            ps = begin("bonus")
            for tt in range(TT):
                for j in range(JT):
                    ins = nc.tensor.matmul(ps[:, tt * H + 2 * j:tt * H + 2 * j + 2], aT[:, j, tt * P:(tt + 1) * P],
                                           blk[:, 0:P:N], start=True, stop=True)
            end(ins, "bonus")
            pe.wait_ge(nlf_ready, 1)
            pe.wait_ge(consts_ready, 3)
            ps = begin("cT")
            for tt in range(TT):
                o = OFF - tt * P
                ins = nc.tensor.matmul(ps[0:H, :], ffz[:, 4, tt, :], stepm[:, o:o + T], start=(tt == 0), stop=(tt == TT - 1))
            end(ins, "cT")

            pe.wait_ge(c3_ready, 1)
            for tt in range(TT):
                emptied(pe, "fv", tt)
            for m in range(14, 22):
                emptied(pe, "u", m)

            def scores(i):
                qb, h = units[i]
                j, lo = h // 2, (h % 2) * N
                keys = (qb + 1) * P
                ps = begin("S", qb, h)
                nc.tensor.matmul(ps[:, 0:keys], qk[lo:lo + N, 0, j, qb * P:(qb + 1) * P], qk[lo:lo + N, 1, j, 0:keys],
                                 start=True, stop=False)
                nc.tensor.matmul(ps[:, qb * P:keys], identb[:, :], causal[:, :], start=False, stop=False,
                                 skip_group_check=True)
                end(nc.tensor.matmul(ps[:, 0:keys], selh[:, h, :], c3[:, 0:keys], start=False, stop=True), "S", qb, h)

            def transposes(i):
                qb, h = units[i]
                ps = begin("PT", qb, h)
                emptied(pe, "S", qb, h)
                for kb in range(qb + 1):
                    ins = nc.tensor.transpose(ps[:, kb * P:(kb + 1) * P], fP[:, i % 2, kb * P:(kb + 1) * P], ident[:, :])
                end(ins, "PT", qb, h)

            def values(i):
                qb, h = units[i]
                ps = bank[4 + qb % 2]
                if h == 0 and qb < 2:
                    pe.wait_ge(bank_free[4 + qb], uses_before_fox[4 + qb])
                elif h == 0:
                    pe.wait_ge(fox_o_free, qb - 1)
                emptied(pe, "PT", qb, h)
                for kb in range(qb + 1):
                    ins = nc.tensor.matmul(ps[:, h * N:(h + 1) * N], fPT[:, i % 2, kb * P:(kb + 1) * P],
                                           foxv[:, kb, h * N:(h + 1) * N], start=(kb == 0), stop=(kb == qb))
                ins.then_inc(values_done, 1)

            def fo_transposes(qb):
                ps = begin("foT", qb)
                pe.wait_ge(fo_ready, qb + 1)
                for j in range(JT):
                    ins = nc.tensor.transpose(ps[:, j * P:(j + 1) * P], fo[:, qb % 2, j * P:(j + 1) * P], ident[:, :])
                end(ins, "foT", qb)

            for i in range(len(units) + 2):
                if i < len(units):
                    scores(i)
                if 1 <= i <= len(units):
                    transposes(i - 1)
                if i >= 2:
                    values(i - 2)
                if i >= 4 and (i - 4) % H == H - 1:
                    fo_transposes((i - 4) // H)
            fo_transposes(TT - 1)

            pe.wait_ge(fox_o_free, TT)
            heads = [(h, h // 2, (h % 2) * N) for h in range(H)]

            def token_tile_T(st, src):
                ps = begin(*st)
                for j in range(JT):
                    ins = nc.tensor.transpose(ps[:, j * P:(j + 1) * P], src(j), ident[:, :])
                end(ins, *st)

            ncts = 0
            for st in rwkv_stages:
                kind, tt, q = st[0], st[1], st[1] % 2
                if kind == "L":
                    ps = begin(*st)
                    for h, j, lo in heads[st[2]::2]:
                        ins = nc.tensor.matmul(ps[:, j * C:(j + 1) * C], BK[lo:lo + N, j, tt, 0:C], AR[lo:lo + N, j, tt, 0:C],
                                               start=True, stop=True)
                    end(ins, *st)
                elif kind == "X0":
                    ps = begin(*st)
                    pe.wait_ge(xt0_ready, tt + 1)
                    for n in range(4):
                        ins = nc.tensor.transpose(ps[:, n * C:(n + 1) * C], XT[:, tt, 4 * st[2] + n, :], ident[:, :])
                    end(ins, *st)
                elif kind == "P":
                    lv, hf = st[2], st[3]
                    ps = begin(*st)
                    if hf == 0:
                        ncts += 1
                        pe.wait_ge(ct_ready, ncts)
                    emptied(pe, *(("X0", tt, hf) if lv == 1 else ("X", tt, lv - 1, hf)))
                    for n in range(4):
                        h = 4 * hf + n
                        ins = nc.tensor.matmul(ps[:, n * C:(n + 1) * C], CT[:, q, h, :], Xm[:, q, h, :], start=True, stop=True)
                    end(ins, *st)
                elif kind in ("X", "XT"):
                    lv, hf = st[2], st[3]
                    ps = begin(*st)
                    emptied(pe, "P", tt, lv, hf)
                    if lv > 1:
                        emptied(pe, "XT", tt, lv - 1, hf)
                    for n in range(4):
                        h = 4 * hf + n
                        lhsT, rhs = (XT[:, tt, h, :], Pm[:, q, h, :]) if kind == "X" else (Pm[:, q, h, :], XT[:, tt, h, :])
                        ins = nc.tensor.matmul(ps[:, n * C:(n + 1) * C], lhsT, rhs, start=True, stop=True)
                    end(ins, *st)
                elif kind == "vt":
                    token_tile_T(st, lambda j: vT[:, j, tt * P:(tt + 1) * P])
                elif kind == "bt":
                    token_tile_T(st, lambda j: BK[:, j, tt, 0:C])
                elif kind == "kt":
                    token_tile_T(st, lambda j: BK[:, j, tt, C:2 * C])
                elif kind == "at":
                    token_tile_T(st, lambda j: AR[:, j, tt, 0:C])
                elif kind == "KAR":
                    ps = begin(*st)
                    for n in range(2):
                        h, j, lo = heads[4 * st[3] + 2 * n + st[2]]
                        ins = nc.tensor.matmul(ps[:, n * 2 * C:(n + 1) * 2 * C], BK[lo:lo + N, j, tt, C:2 * C],
                                               AR[lo:lo + N, j, tt, :], start=True, stop=True)
                    end(ins, *st)
                elif kind == "BR":
                    ps = begin(*st)
                    for h, j, lo in heads[st[2]::2]:
                        ins = nc.tensor.matmul(ps[:, j * C:(j + 1) * C], BK[lo:lo + N, j, tt, 0:C],
                                               AR[lo:lo + N, j, tt, C:2 * C], start=True, stop=True)
                    end(ins, *st)
                elif kind == "W":
                    ps = begin(*st)
                    emptied(pe, "at", tt)
                    for hf in range(2):
                        emptied(pe, "XT", tt, LEVELS - 1, hf)
                    for h, j, lo in heads:
                        ins = nc.tensor.matmul(ps[lo:lo + N, j * C:(j + 1) * C], Atok[tt][:, h * N:(h + 1) * N], XT[:, tt, h, :],
                                               start=True, stop=True)
                    end(ins, *st)
                elif kind == "MV":
                    ps = begin(*st)
                    emptied(pe, "vt", tt)
                    pe.wait_ge(scores_masked, 6 * tt + 4)
                    for h in range(H):
                        ins = nc.tensor.matmul(ps[:, h * N:(h + 1) * N], KAR[tt][:, h, 0:C], V[q][:, h * N:(h + 1) * N],
                                               start=True, stop=True)
                    end(ins, *st)
                elif kind == "U":
                    ps = begin(*st)
                    emptied(pe, "W", tt)
                    emptied(pe, "MV", tt)
                    pe.wait_ge(state_ready, tt + 1)
                    for h in range(H):
                        nc.tensor.matmul(ps[:, h * N:(h + 1) * N], XT[:, tt, h, :], MV[tt][:, h * N:(h + 1) * N],
                                         start=(h == 0), stop=False, skip_group_check=True)
                    for j in range(JT):
                        ins = nc.tensor.matmul(ps[:, j * P:(j + 1) * P], WT[tt][:, j, :], ST[:, j, :],
                                               start=False, stop=True, skip_group_check=True)
                    end(ins, *st)
                elif kind == "Yfrom":
                    ps = begin("Y", tt)
                    for j in range(JT):
                        nc.tensor.matmul(ps[:, j * P:(j + 1) * P], AR[:, j, tt, C:2 * C], ST[:, j, :],
                                         start=(j == 0), stop=False, skip_group_check=True)
                    for h in range(H):
                        nc.tensor.matmul(ps[:, h * N:(h + 1) * N], KAR[tt][:, h, C:2 * C], V[q][:, h * N:(h + 1) * N],
                                         start=False, stop=False, skip_group_check=True)
                elif kind == "state":
                    ps = begin(*st)
                    emptied(pe, "U", tt)
                    emptied(pe, "bt", tt)
                    emptied(pe, "kt", tt)
                    for h, j, lo in heads:
                        hv = slice(h * N, (h + 1) * N)
                        nc.tensor.matmul(ps[lo:lo + N, j * N:(j + 1) * N], Ktok[tt][:, hv], V[q][:, hv], start=True, stop=False)
                        ins = nc.tensor.matmul(ps[lo:lo + N, j * N:(j + 1) * N], Btok[tt][:, hv], U[tt][:, hv], start=False, stop=True)
                    end(ins, *st)
                elif kind == "Y":
                    emptied(pe, "U", tt)
                    pe.wait_ge(scores_masked, 6 * tt + 6)
                    for h in range(H):
                        hv = slice(h * N, (h + 1) * N)
                        ins = nc.tensor.matmul(bank[7][:, hv], BR[tt][:, h, :], U[tt][:, hv], start=False, stop=True,
                                               skip_group_check=True)
                    end(ins, *st)
                elif kind == "yT":
                    ps = begin(*st)
                    pe.wait_ge(y_ready, tt + 1)
                    for j in range(JT):
                        ins = nc.tensor.transpose(ps[:, j * P:(j + 1) * P], Yq[:, j * P:(j + 1) * P], ident[:, :])
                    end(ins, *st)
                elif kind == "o":
                    if st == ("o", 0, 0):
                        for qb in range(TT):
                            emptied(pe, "foT", qb)
                    if tt == 0:
                        pe.wait_ge(w_out_loaded[st[2]], 16)
                    emptied(pe, "yT", tt)
                    ps = begin(*st)
                    for k in range(KT):
                        ins = nc.tensor.matmul(ps[:, :], hT[:, k, tt * P:(tt + 1) * P], slots[:, st[2], k, :],
                                               start=(k == 0), stop=(k == KT - 1))
                    end(ins, *st)
                elif kind == "h2T":
                    pe.wait_ge(hrow_ready, TT + tt + 1)
                    ps = begin(*st)
                    for k in range(4):
                        o = (st[2] * 4 + k) * P
                        ins = nc.tensor.transpose(ps[:, k * P:(k + 1) * P], hrow[:, tt % 2, o:o + P], ident[:, :])
                    end(ins, *st)
                elif kind == "lg":
                    emptied(pe, "h2T", tt, 0)
                    emptied(pe, "h2T", tt, 1)
                    ps = begin(*st)
                    for k in range(KT):
                        ins = nc.tensor.matmul(ps[:, 0:E], hT[:, k, tt * P:(tt + 1) * P], rw[:, k, :],
                                               start=(k == 0), stop=(k == KT - 1))
                    end(ins, *st)

            pe.wait_ge(sel_ready, TT)
            ps = begin("cnt")
            for t2 in range(TT):
                ins = nc.tensor.matmul(ps[:, 0:E], stepm[:, OFF + P:OFF + 2 * P], Msel[:, t2, :],
                                       start=(t2 == 0), stop=(t2 == TT - 1))
            end(ins, "cnt")
            for tt in range(TT):
                ps = begin("pos", tt)
                for t2 in range(tt):
                    nc.tensor.matmul(ps[:, 0:E], stepm[:, OFF + P:OFF + 2 * P], Msel[:, t2, :],
                                     start=(t2 == 0), stop=False)
                end(nc.tensor.matmul(ps[:, 0:E], stepm[:, OFF - 1:OFF - 1 + P], Msel[:, tt, :],
                                     start=(tt == 0), stop=True), "pos", tt)
            for b in range(8):
                pe.wait_ge(bank_free[b], uses[b])

            def x_transposes(b, q, n):
                pe.wait_ge(xg_loaded[q], n * 16 + 16)
                pe.wait_ge(xt_free, b + 1)
                for k in range(KT):
                    ins = nc.tensor.transpose(bank[k // 4][:, (k % 4) * NS:(k % 4 + 1) * NS],
                                              xg[0:NS, q, k * P:(k + 1) * P], ident[0:NS, 0:NS])
                ins.then_inc(xt_full, 1)

            def unit(i, q, u, bank_, x_of, midway=None):
                n = q * UNITS + u
                c, kh = UNIT_OF[u]
                pe.wait_ge(*low_part(i, n))
                if kh == 0:
                    bias = b1r[:, c * CW:(c + 1) * CW] if c < W1C else b2r[:, (c - W1C) * CW:(c - W1C + 1) * CW]
                    nc.tensor.matmul(bank_[0:NS, :], sel[:, q, :], bias, start=True, stop=False)
                for k in range(KT // 2):
                    x_h, x_l = (x[:, kh * KT // 2 + k, :] for x in x_of)
                    w_h, w_l = w_hi[n % HI][:, k, :], w_lo[n % LO][:, k, :]
                    last = kh == 1 and k == KT // 2 - 1
                    nc.tensor.matmul(bank_[0:NS, :], x_h, w_l, start=False, stop=False)
                    nc.tensor.matmul(bank_[0:NS, :], x_h, w_h, start=False, stop=False)
                    ins = nc.tensor.matmul(bank_[0:NS, :], x_l, w_h, start=False, stop=last)
                    if k == 1 and midway:
                        midway()
                ins.then_inc(unit_used, 1)

            def act_transposes(b, c):
                pe.wait_ge(act_ready, b * W1C + (c + 1))
                if c >= 2:
                    pe.wait_ge(a_lo_ready, b * W1C + (c - 1))
                for f in range(2):
                    o = (c // 2 * 2 + f) * NS
                    ins = nc.tensor.transpose(bank[4 + c % 2][:, o:o + NS], act[0:NS, (2 * c + f) * P:(2 * c + f + 1) * P],
                                              ident[0:NS, 0:NS])
                ins.then_inc(at_full, 1)

            def block_work(i, q):
                b = i * 2 + q
                pe.wait_ge(x_lo_ready, b + 1)
                pe.wait_ge(sel_set, b + 1)
                for c in range(W1C):
                    pe.wait_ge(hid_free[c % 2], b * 2 + (c // 2 + 1))
                    for kh in range(2):
                        unit(i, q, 2 * c + kh, bank[2 + c % 2], (x_hi, x_lo))
                    if c > 0:
                        act_transposes(b, c - 1)
                for h in range(2):
                    pe.wait_ge(y_free[h], b + 1)
                pe.wait_ge(a_lo_ready, b * W1C + 2)
                unit(i, q, 8, bank[6], (a_hi, a_lo))
                x_transposes(b + 1, 1 - q, i + q)
                unit(i, q, 9, bank[7], (a_hi, a_lo), midway=lambda: act_transposes(b, 3))
                pe.wait_ge(a_lo_ready, b * W1C + 4)
                unit(i, q, 10, bank[6], (a_hi, a_lo))
                unit(i, q, 11, bank[7], (a_hi, a_lo))

            pe.sem_inc(unit_used, HI)
            pe.sem_inc(xt_full, 1)
            x_transposes(0, 0, 0)
            pe.wait_ge(tables_ready, 1)
            with pe.Fori(0, E // 2) as i:
                for q in range(2):
                    block_work(i, q)
            npairs = pe.value_load(pairs_i[0:1, 0:1], min_val=E // 2, max_val=NB // 2)
            with pe.Fori(E // 2, NB // 2) as i:
                with pe.If(i < npairs):
                    for q in range(2):
                        block_work(i, q)

        @block.vector
        def _(dve):
            steps = [0]

            def step(ins):
                steps[0] += 1
                ins.then_inc(dve_step, 1)
                dve.wait_ge(dve_step, steps[0])

            tensor_tensor, tensor_scalar = nc.vector.tensor_tensor, nc.vector.tensor_scalar

            def heads_of(ap):
                return ap.rearrange("p (h v) -> p h v", h=H)

            def per_head(st, parts=P):
                return st.unsqueeze(2).to_broadcast([parts, H, N])

            def normalize(tt, again):
                dve.wait_ge(sumsq_ready, TT * again + tt + 1)
                step(nc.vector.reciprocal(ss[:, tt:tt + 1], ss[:, tt:tt + 1]))
                if tt >= 2:
                    for half in range(2):
                        filled(dve, "h2T" if again else "hT", tt - 2, half)
                    if again:
                        dve.wait_ge(h2_stored[tt - 2], 16)
                tensor_scalar(hrow[:, tt % 2, :], xs[:, tt, :], ss[:, tt:tt + 1], None, ALU.mult).then_inc(hrow_ready, 1)

            def take_transposed(name, tt, half, gain):
                filled(dve, name, tt, half)
                b = plan[(name, tt, half)][0]
                tensor_tensor(hT[:, half * 4:half * 4 + 4, tt * P:(tt + 1) * P],
                              bank[b][:, :].rearrange("p (k t) -> p k t", k=4),
                              vec(gain)[:, half * 4:half * 4 + 4].unsqueeze(2).to_broadcast([P, 4, P]),
                              ALU.mult).then_inc(free_of((name, tt, half)), 1)

            filled(dve, "vec")
            nc.vector.tensor_copy(vecT[:, 0:vrow], bank[0][:, 0:vrow]).then_inc(free_of(("vec",)), 1)
            emptied(dve, "vec")
            step(tensor_scalar(one_minus_ka, vec("ka"), -1.0, 1.0, ALU.mult, ALU.add))
            dve.sem_inc(vec_ready, 1)
            for tt in range(TT + 1):
                if tt < TT:
                    normalize(tt, 0)
                if tt > 0:
                    for half in range(2):
                        take_transposed("hT", tt - 1, half, "g1")

            def chunks_of(ap):
                return ap.rearrange("p (c t) -> p c t", t=C)

            dve.wait_ge(consts_ready, 3)

            def mix(nth, m):
                emptied(dve, "u", m)
                cur = shiftbuf[:, nth % 2, 1:T + 1]
                prev = shiftbuf[:, nth % 2, 0:T]
                if m < 8:
                    dst = (AR if m < 4 else BK)[:, m % 4, :, C:2 * C]
                    cur, prev = (v.rearrange("p (c t) -> p c t", t=C) for v in (cur, prev))
                else:
                    dst = vT[:, m - 8, :] if m < 12 else wa if m == 12 else gl
                step(tensor_tensor(dst, prev, cur, ALU.subtract))
                nc.vector.scalar_tensor_tensor(dst, dst, vec("mu", m), cur, ALU.mult, ALU.add).then_inc(mixed, 1)
                dve.wait_ge(mixed, nth + 1)

            rwkv_order = [m for m in U_ORDER if m < 14]
            for nth, m in enumerate(rwkv_order[:10]):
                mix(nth, m)
            for j in range(JT):
                emptied(dve, "z", j)
                for cc in range(NC):
                    chunk = slice(cc * C, (cc + 1) * C)
                    step(nc.vector.tensor_tensor_scan(decay_c[:, j, chunk], stepm[:, OFF + P:OFF + P + C],
                                                      decay_s[:, j, chunk], 0.0, ALU.mult, ALU.add))
                dc, ds = chunks_of(decay_c[:, j, :]), chunks_of(decay_s[:, j, :])
                step(nc.vector.tensor_copy(mid[:, j, :], dc[:, :, MID - 1]))
                step(tensor_tensor(dc, dc, mid[:, j, :].unsqueeze(2).to_broadcast([P, NC, C]), ALU.subtract))
                step(tensor_tensor(dend[:, j, 0:NC - 1], dc[:, 0:NC - 1, C - 1], mid[:, j, 1:NC], ALU.add))
                tensor_tensor(ds, dc, ds, ALU.subtract).then_inc(cum_ready, 1)
                step(tensor_scalar(BK[:, j, :, 0:C], BK[:, j, :, C:2 * C], vec("kk", j), None, ALU.mult))
                tensor_tensor(AR[:, j, :, 0:C], BK[:, j, :, 0:C], BK[:, j, :, 0:C], ALU.mult).then_inc(kksq_ready, 1)
            for nth, m in enumerate(rwkv_order[10:]):
                mix(10 + nth, m)

            for j in range(JT):
                filled(dve, "ss", j)
                tensor_scalar(AR[:, j, :, 0:C], chunks_of(bank[plan[("ss", j)][0]][:, :]), 1e-24, None, ALU.max)\
                    .then_inc(free_of(("ss", j)), 1)
                emptied(dve, "ss", j)
                dve.sem_inc(kksum_ready, 1)
            for j in range(JT):
                A_, R_, B_, K_ = AR[:, j, :, 0:C], AR[:, j, :, C:2 * C], BK[:, j, :, 0:C], BK[:, j, :, C:2 * C]
                a_ = chunks_of(aT[:, j, :])
                dve.wait_ge(kknorm_ready, j + 1)
                step(nc.vector.reciprocal(A_, A_))
                step(tensor_tensor(B_, B_, A_, ALU.mult))
                dve.wait_ge(exps_ready, j + 1)
                step(tensor_tensor(A_, B_, chunks_of(decay_s[:, j, :]), ALU.mult))
                emptied(dve, "a", j)
                step(tensor_tensor(B_, B_, a_, ALU.mult))
                step(tensor_tensor(B_, B_, chunks_of(decay_c[:, j, :]), ALU.mult))
                step(tensor_scalar(a_, a_, vec("ka", j), one_minus_ka[:, j:j + 1], ALU.mult, ALU.add))
                step(tensor_tensor(K_, K_, a_, ALU.mult))
                step(nc.vector.scalar_tensor_tensor(a_, R_, vec("rk", j), K_, ALU.mult, ALU.mult))
                step(tensor_tensor(K_, K_, chunks_of(decay_c[:, j, :]), ALU.mult))
                tensor_tensor(R_, R_, chunks_of(decay_e[:, j, :]), ALU.mult).then_inc(elem_done, 1)
            dve.wait_ge(elem_done, JT)

            filled(dve, "ff")
            tensor_tensor(ffz[:, 0], bank[plan[("ff",)][0]][:, 0:TT * H].rearrange("p (t h) -> p t h", h=H),
                          fb[:, :].unsqueeze(1).to_broadcast([P, TT, H]), ALU.add).then_inc(free_of(("ff",)), 1)
            emptied(dve, "ff")
            step(tensor_scalar(ffz[:, 4], ffz[:, 0], 0.0, None, ALU.min))
            dve.wait_ge(ffln_ready, 1)
            tensor_tensor(ffz[:, 4], ffz[:, 3], ffz[:, 4], ALU.subtract).then_inc(nlf_ready, 1)
            filled(dve, "cT")
            nc.vector.tensor_copy(cf[:, :], bank[plan[("cT",)][0]][0:H, :]).then_inc(free_of(("cT",)), 1)
            emptied(dve, "cT")
            for g in range(2):
                step(nc.vector.tensor_copy(cb[:, g, :], cf[:, :]))
                step(tensor_tensor(cf[:, :], cf[:, :], cb[:, g, :], ALU.subtract))
                step(nc.vector.tensor_copy(c3[32 * g:32 * g + H, :], cb[:, g, :]))
            nc.vector.tensor_copy(c3[64:64 + H, :], cf[:, :]).then_inc(c3_ready, 1)

            def finish_fox(qb):
                dve.wait_ge(values_done, H * (qb + 1))
                u0 = qb * H
                emptied(dve, "S", qb, H - 1)
                step(nc.vector.reciprocal(rrec[:, :], rsum[:, u0:u0 + H]))
                if qb >= 2:
                    filled(dve, "foT", qb - 2)
                f = heads_of(fo[:, qb % 2, :])
                tensor_tensor(f, heads_of(bank[4 + qb % 2][:, :]), per_head(rrec[:, :]), ALU.mult).then_inc(fox_o_free, 1)
                dve.wait_ge(fox_o_free, qb + 1)
                step(tensor_tensor(heads_of(fsq), f, f, ALU.mult))
                nc.vector.tensor_reduce(fst[:, :], heads_of(fsq), AX, ALU.add).then_inc(fox_ms_ready, 1)
                dve.wait_ge(fox_rms_ready, qb + 1)
                step(nc.vector.reciprocal(fst[:, :], fst[:, :]))
                tensor_tensor(f, f, per_head(fst[:, :]), ALU.mult).then_inc(fo_ready, 1)

            for i in range(len(units) + 2):
                if i < len(units):
                    filled(dve, "S", *units[i])
                    nc.vector.tensor_reduce(nmx[:, i:i + 1], bank[i % 2][:, 0:(units[i][0] + 1) * P], AX, ALU.max,
                                            negate=True).then_inc(negmax_ready, 1)
                if 1 <= i <= len(units):
                    filled(dve, "PT", *units[i - 1])
                    if i >= 3:
                        dve.wait_ge(values_done, i - 2)
                    keys = (units[i - 1][0] + 1) * P
                    nc.vector.tensor_copy(fPT[:, (i - 1) % 2, 0:keys], bank[2 + (i - 1) % 2][:, 0:keys])\
                        .then_inc(free_of(("PT", *units[i - 1])), 1)
                if i >= H + 1 and (i - H - 1) % H == 0:
                    finish_fox((i - H - 1) // H)

            def parity(ap, g):
                return ap.rearrange("p (j g) t -> p j g t", g=2)[:, :, g, :]

            def four(ap):
                return ap.rearrange("p (h t) -> p h t", h=4)

            dve.wait_ge(consts_ready, 4)
            step(nc.vector.memset(STc, 0.0))
            nc.vector.memset(ST, 0.0).then_inc(state_ready, 1)
            for st in rwkv_stages:
                kind, tt, q = st[0], st[1], st[1] % 2
                ps = bank[plan[st][0]][:, :] if st in plan else None
                if kind == "L":
                    g = st[2]
                    filled(dve, *st)
                    if tt >= 2:
                        dve.wait_ge(ct_ready, 2 * (LEVELS - 1))
                    tensor_tensor(parity(Lm[:, q], g), four(ps), maskSC[:, 0:C].unsqueeze(1).to_broadcast([P, 4, C]),
                                  ALU.mult).then_inc(free_of(st), 1)
                    emptied(dve, *st)
                    if g == 1:
                        dve.sem_inc(scm_ready, 1)
                        step(tensor_tensor(XT[:, tt], Lm[:, q], levmask[:, 0, :].unsqueeze(1).to_broadcast([C, H, C]), ALU.mult))
                        tensor_tensor(XT[:, tt], ident[:, :].unsqueeze(1).to_broadcast([C, H, C]), XT[:, tt],
                                      ALU.subtract).then_inc(xt0_ready, 1)
                elif kind in ("X", "XT"):
                    lv, hf = st[2], st[3]
                    filled(dve, *st)
                    if kind == "XT" and lv == 1:
                        dve.wait_ge(xt0_ready, tt + 1)
                    elif lv > 1:
                        emptied(dve, kind, tt, lv - 1, hf)
                    x = (Xm[:, q] if kind == "X" else XT[:, tt])[:, 4 * hf:4 * hf + 4, :]
                    tensor_tensor(x, x, four(ps), ALU.subtract).then_inc(free_of(st), 1)
                elif kind == "KAR":
                    g, jj = st[2], st[3]
                    filled(dve, *st)
                    if 0 < tt < NC - 1:
                        filled(dve, "Y", tt - 1)
                    tensor_tensor(parity(KAR[tt][:, 4 * jj:4 * jj + 4, :], g), ps.rearrange("p (h t) -> p h t", h=2),
                                  maskSC[:, :].unsqueeze(1).to_broadcast([P, 2, 2 * C]), ALU.mult).then_inc(free_of(st), 1)
                    emptied(dve, *st)
                    dve.sem_inc(scores_masked, 1)
                elif kind == "BR":
                    filled(dve, *st)
                    tensor_tensor(parity(BR[tt], st[2]), four(ps), maskSC[:, C:2 * C].unsqueeze(1).to_broadcast([P, 4, C]),
                                  ALU.mult).then_inc(free_of(st), 1)
                    emptied(dve, *st)
                    dve.sem_inc(scores_masked, 1)
                elif kind == "U":
                    filled(dve, *st)
                    tensor_scalar(U[tt], ps, -1.0, None, ALU.mult).then_inc(free_of(st), 1)
                elif kind == "state":
                    filled(dve, *st)
                    dve.wait_ge(state_ready, tt + 1)
                    tensor_tensor(STt, STc, ps[:, 0:JT * N].rearrange("p (j v) -> p j v", j=JT), ALU.add)\
                        .then_inc(free_of(st), 1)
                    emptied(dve, *st)
                    for g in range(2):
                        r = slice(g * N, (g + 1) * N)
                        ins = tensor_tensor(ST[r, :, r], STt[r], dend[r, :, tt:tt + 1].to_broadcast([N, JT, N]), ALU.mult)
                    ins.then_inc(state_ready, 1)
                    step(tensor_tensor(STc, STt, dend[:, :, tt:tt + 1].to_broadcast([P, JT, N]), ALU.mult))
                elif kind == "Y":
                    filled(dve, *st)
                    y, yc, yq = heads_of(ps), heads_of(Yc), heads_of(Yq)
                    mean, var = gst[:, 0, :], gst[:, 1, :]
                    step(nc.vector.tensor_reduce(mean, y, AX, ALU.add))
                    step(tensor_scalar(mean, mean, 1.0 / N, None, ALU.mult))
                    if tt > 0:
                        filled(dve, "yT", tt - 1)
                    tensor_tensor(yc, y, per_head(mean), ALU.subtract).then_inc(free_of(st), 1)
                    emptied(dve, *st)
                    step(tensor_tensor(yq, yc, yc, ALU.mult))
                    nc.vector.tensor_reduce(var, yq, AX, ALU.add).then_inc(gn_var_ready, 1)
                    dve.wait_ge(gn_std_ready, tt + 1)
                    nc.vector.reciprocal(var, var).then_inc(gn_rstd_ready, 1)
                elif kind == "o":
                    filled(dve, *st)
                    o = xs[:, tt, st[2] * CW:(st[2] + 1) * CW]
                    tensor_tensor(o, o, ps, ALU.add).then_inc(free_of(st), 1)
                elif kind == "norm":
                    normalize(tt, 1)
                elif kind == "h2T":
                    take_transposed("h2T", tt, st[2], "g2")
                elif kind == "lg":
                    filled(dve, *st)
                    tensor_tensor(lg[:, tt, :], ps[:, 0:E], rb[:, :], ALU.add).then_inc(free_of(st), 1)
                    emptied(dve, *st)
                    step(nc.vector.max(m8[:, tt, :], lg[:, tt, :]))
                    tensor_scalar(nm0[:, tt:tt + 1], m8[:, tt, 0:1], -1.0, None, ALU.mult).then_inc(gmax_ready, 1)
                    step(nc.vector.max_index(i8[:, tt, :], m8[:, tt, :], lg[:, tt, :]))
                    step(nc.vector.tensor_copy(i8f[:, tt, :], i8[:, tt, :]))
                    step(tensor_tensor(onehot[:, tt], iotaE[:, :].unsqueeze(1).to_broadcast([P, TOPK, E]),
                                       i8f[:, tt, 0:TOPK].unsqueeze(2).to_broadcast([P, TOPK, E]), ALU.is_equal))
                    nc.vector.tensor_reduce(Msel[:, tt, :], onehot[:, tt].rearrange("p k e -> p e k"), AX, ALU.add)\
                        .then_inc(sel_ready, 1)

            filled(dve, "cnt")
            nc.vector.tensor_copy(cnt[:, :], bank[7][:, 0:E]).then_inc(free_of(("cnt",)), 1)
            emptied(dve, "cnt")
            extra = rt[:, 0, :]
            step(tensor_scalar(extra, cnt[:, :], float(NS), None, ALU.is_gt))
            for n in range(2, EXTRA + 1):
                step(nc.vector.scalar_tensor_tensor(extra, cnt[:, :], float(n * NS), extra, ALU.is_gt, ALU.add))
            step(nc.vector.tensor_tensor_scan(ovf_end[:, :], stepm[:, OFF + P:OFF + P + E], extra, 0.0, ALU.mult, ALU.add))
            step(tensor_tensor(ovf_base[:, :], ovf_end[:, :], extra, ALU.subtract))
            for tt in range(TT):
                filled(dve, "pos", tt)
                nc.vector.tensor_copy(pos[:, :], bank[plan[("pos", tt)][0]][:, 0:E]).then_inc(free_of(("pos", tt)), 1)
                emptied(dve, "pos", tt)
                step(tensor_scalar(qd[:, :], pos[:, :], float(NS), None, ALU.is_ge))
                for n in range(2, EXTRA + 1):
                    step(nc.vector.scalar_tensor_tensor(qd[:, :], pos[:, :], float(n * NS), qd[:, :], ALU.is_ge, ALU.add))
                first, later, blkid = rt[:, 2, :], rt[:, 3, :], rt[:, 4, :]
                step(tensor_scalar(first, qd[:, :], 0.0, None, ALU.is_equal))
                step(nc.vector.scalar_tensor_tensor(later, qd[:, :], float(E - 1), ovf_base[:, :], ALU.add, ALU.add))
                step(tensor_tensor(blkid, iotaE[:, :], later, ALU.subtract))
                step(tensor_tensor(blkid, blkid, first, ALU.mult))
                step(tensor_tensor(blkid, blkid, later, ALU.add))
                step(tensor_tensor(blkid, blkid, qd[:, :], ALU.subtract))
                step(nc.vector.scalar_tensor_tensor(slotm[:, :], blkid, float(NS), pos[:, :], ALU.mult, ALU.add))
                step(tensor_tensor(slotk[:, :, :], onehot[:, tt], slotm[:, :].unsqueeze(1).to_broadcast([P, TOPK, E]), ALU.mult))
                step(nc.vector.tensor_reduce(slotf[:, tt, :], slotk[:, :, :], AX, ALU.add))
                tensor_scalar(sloti[:, tt, :], slotf[:, tt, :], float(NS), None, ALU.add).then_inc(slots_ready, 1)
            step(tensor_scalar(rt[:, 1, 0:NOVF // 2], iotaO[:, 0:NOVF // 2], 2.0, ovf_end[:, E - 1:E], ALU.mult, ALU.is_lt))
            step(nc.vector.tensor_reduce(pairs_f[:, 0:1], rt[:, 1, 0:NOVF // 2], AX, ALU.add))
            step(tensor_scalar(pairs_f[:, 1:2], pairs_f[:, 0:1], float(E // 2), None, ALU.add))
            step(nc.vector.tensor_copy(pairs_i[:, :], pairs_f[:, 1:2]))
            step(tensor_tensor(ovcmp[:, :, :], ovf_end[:, :].unsqueeze(1).to_broadcast([P, NOVF, E]),
                               iotaO[:, :].unsqueeze(2).to_broadcast([P, NOVF, E]), ALU.is_le))
            step(nc.vector.tensor_reduce(ovexp[:, :], ovcmp[:, :, :], AX, ALU.add))
            step(tensor_scalar(ovexp[:, :], ovexp[:, :], float(E - 1), None, ALU.min))
            step(nc.vector.tensor_copy(blkexp[:, :], ovexp[:, :]))
            dve.sem_inc(tables_ready, 1)
            for tt in range(TT):
                dve.wait_ge(gates_ready, tt + 1)
                step(nc.vector.reciprocal(gsum[:, tt:tt + 1], gsum[:, tt:tt + 1]))
                step(tensor_scalar(gate[:, tt, :], gate[:, tt, :], gsum[:, tt:tt + 1], None, ALU.mult))

            dve.wait_ge(bias_split, 1)
            for dst, o, w in ((b1r, 0, F2), (b2r, F2, D)):
                ins = tensor_tensor(dst[E:2 * E, :], biasrows[E:2 * E, o:o + w], dst[E:2 * E, :], ALU.subtract)
            ins.then_inc(bias_split, 1)
            step(tensor_tensor(expert_row[:, :], ident[0:2 * E, 0:E], ident[0:2 * E, E:2 * E], ALU.add))

            for tt in range(TT):
                dve.wait_ge(h2_stored[tt], 16)

            def take_x(b):
                dve.wait_ge(xt_full, b + 2)
                for half in range(2):
                    ins = tensor_tensor(xTf.rearrange("p (k s) -> p k s", k=KT)[:, half * 4:half * 4 + 4, :],
                                        bank[half][:, 0:4 * NS].rearrange("p (k s) -> p k s", k=4),
                                        vec("g2")[:, half * 4:half * 4 + 4].unsqueeze(2).to_broadcast([P, 4, NS]), ALU.mult)
                ins.then_inc(xt_free, 1)
                dve.wait_ge(xt_free, b + 2)
                dve.wait_ge(x_hi_ready, b + 1)
                tensor_tensor(x_lo[:, :, :], xTf.rearrange("p (k s) -> p k s", k=KT), x_hi[:, :, :], ALU.subtract)\
                    .then_inc(x_lo_ready, 1)

            def act_low(b, c):
                dve.wait_ge(a_hi_ready, b * W1C + (c + 1))
                o = c // 2 * 2 * NS
                tensor_tensor(a_lo[:, 2 * c:2 * c + 2, :], bank[4 + c % 2][:, o:o + 2 * NS].rearrange("p (f s) -> p f s", f=2),
                              a_hi[:, 2 * c:2 * c + 2, :], ALU.subtract).then_inc(a_lo_ready, 1)

            def swiglu(i, q, c):
                b, p = i * 2 + q, c % 2
                wait_used(dve, i, q * UNITS + 2 * c + 1)
                pairs = bank[2 + p][0:NS, :].rearrange("p (f s) -> p f s", s=2)
                tensor_scalar(hg[0:NS, p], pairs[:, :, 0], 7.0, None, ALU.min).then_inc(glu_ready, 1)
                tensor_scalar(hl[0:NS, p], pairs[:, :, 1], 7.0, -7.0, ALU.min, ALU.max).then_inc(hid_free[p], 1)
                dve.wait_ge(glu_ready, b * W1C + (c + 1))
                dve.wait_ge(hid_free[p], b * 2 + (c // 2 + 2))
                step_(nc.vector.scalar_tensor_tensor(hl[0:NS, p], hl[0:NS, p], 1.0, hg[0:NS, p], ALU.add, ALU.mult), b, c)
                dve.wait_ge(sig_ready, b * W1C + (c + 1))
                tensor_tensor(act[0:NS, c * CW // 2:(c + 1) * CW // 2], hl[0:NS, p], hs[0:NS, p], ALU.mult).then_inc(act_ready, 1)

            def step_(ins, b, c):
                ins.then_inc(lin_ready, 1)
                dve.wait_ge(lin_ready, b * W1C + (c + 1))

            def block_work(i, q, e):
                b = i * 2 + q
                nc.vector.tensor_copy(sel[:, q, :].unsqueeze(2), expert_row[:, bass.ds(e, 1)].unsqueeze(1).to_broadcast([2 * E, NS, 1]))\
                    .then_inc(sel_set, 1)
                for u in range(UNITS):
                    n = q * UNITS + u
                    if not by_gpsimd(n):
                        wait_used(dve, i, n - LO)
                        dve.wait_ge(hi_ready, i * (2 * UNITS) + (n + 1))
                        tensor_tensor(w_lo[n % LO][:, :, :], raw[n % RAW], w_hi[n % HI][:, :, :], ALU.subtract)\
                            .then_inc(lo_ready[0], 1)
                    if u in (4, 6, 8, 10):
                        swiglu(i, q, (u - 4) // 2)
                    if u in (7, 9, 11):
                        act_low(b, (u - 7) // 2)
                take_x(b + 1)
                act_low(b, 3)

            dve.sem_inc(xt_free, 1)
            for p in range(2):
                dve.sem_inc(hid_free[p], 1)
            dve.sem_inc(lo_ready[0], RAW // 3 * 2)
            take_x(0)
            with dve.Fori(0, E // 2) as i:
                for q in range(2):
                    block_work(i, q, i * 2 + q)
            npairs = dve.value_load(pairs_i[0:1, 0:1], min_val=E // 2, max_val=NB // 2)
            with dve.Fori(E // 2, NB // 2) as i:
                with dve.If(i < npairs):
                    for q in range(2):
                        e = dve.value_load(blkexp[0:1, bass.ds(i * 2 + (q - E), 1)], min_val=0, max_val=E - 1)
                        block_work(i, q, e)

            dve.wait_ge(gfin_in, 16)
            for tt in range(TT):
                dve.wait_ge(gathered[tt], 16 * TOPK)
                for k in range(TOPK):
                    rows = slots[:, tt, 2 * k:2 * k + 2, :].rearrange("p a f -> p (a f)")
                    step(nc.vector.scalar_tensor_tensor(xs[:, tt, :], rows, gate[:, tt, k:k + 1], xs[:, tt, :],
                                                        ALU.mult, ALU.add))
                dve.sem_inc(summed, 1)
                dve.wait_ge(normed, tt + 1)
                step(nc.vector.reciprocal(ss[:, tt:tt + 1], ss[:, tt:tt + 1]))
                if tt >= 2:
                    dve.wait_ge(out_stored[tt - 2], 16)
                nc.vector.scalar_tensor_tensor(outb[tt % 2], xs[:, tt, :], ss[:, tt:tt + 1], gfin, ALU.mult, ALU.mult)\
                    .then_inc(out_ready, 1)


_INS = ['x', 'attn_norm_g', 'w_in', 'rwkv_mu', 'rwkv_w0', 'rwkv_w_up', 'rwkv_a0', 'rwkv_a_up', 'rwkv_g_up',
        'rwkv_k_k', 'rwkv_k_a', 'rwkv_r_k', 'rwkv_ln_w', 'rwkv_ln_b', 'fox_f_bias', 'fox_out_g', 'w_out',
        'ffn_norm_g', 'router_w', 'router_b', 'expert_w1', 'expert_b1', 'expert_w2', 'expert_b2', 'final_norm_g']
_OUTS = [((1, 512, 1024), 'float32')]


def kernel(**inputs):
    import numpy as _np
    import concourse.bacc as _bacc
    from concourse import mybir as _mybir
    from concourse.bass_utils import run_bass_kernel_spmd as _run

    nc = _bacc.Bacc("TRN2", target_bir_lowering=False, num_devices=1)
    arrays, args = {}, []
    for name in _INS:
        a = _np.ascontiguousarray(inputs[name])
        arrays[f"in_{name}_dram"] = a
        args.append(nc.dram_tensor(f"in_{name}_dram", a.shape, _mybir.dt.from_np(a.dtype), kind="ExternalInput").ap())
    for i, (shape, dtype) in enumerate(_OUTS):
        dt = _mybir.dt.from_np(_np.dtype(dtype))
        args.append(nc.dram_tensor(f"out_{i}_dram", shape, dt, kind="ExternalOutput").ap())
    hymba_layer(nc, *args)
    r = _run(nc, [arrays], core_ids=[0])
    got = tuple(r.results[0][f"out_{i}_dram"] for i in range(len(_OUTS)))
    return got[0]
```

```python
import concourse.bass as bass
from concourse import mybir
from contextlib import ExitStack


def hymba_layer(nc, x, attn_norm_g, w_in, mu, w0, w_up, a0, a_up, g_up, k_k, k_a, r_k, ln_w, ln_b,
                f_bias, out_g, w_out, ffn_norm_g, router_w, router_b, w1, b1, w2, b2, final_norm_g, out):
    f32 = mybir.dt.float32
    f32r = mybir.dt.float32r
    bf16 = mybir.dt.bfloat16
    i32 = mybir.dt.int32
    u32 = mybir.dt.uint32
    ALU = mybir.AluOpType
    ACT = mybir.ActivationFunctionType
    AX = mybir.AxisListType.X

    P = 128
    T, D = x.shape[1], x.shape[2]
    TT, KT = T // P, D // P
    H, N = r_k.shape[1], r_k.shape[2]
    HW = H * N
    JT = HW // P
    LORA = w_up.shape[1]
    C = P
    NC = T // C
    MID = C // 2
    FOX0 = 3 * HW + 2 * LORA + g_up.shape[1]
    E, F2 = router_w.shape[2], w1.shape[3]
    FT = F2 // 2 // P
    TOPK = 4
    NS = 96
    EXTRA = -(-T // NS) - 1
    NOVF = 22
    assert NOVF >= T * TOPK // NS and NOVF % 2 == 0
    NB = E + NOVF
    CH = 6
    CW = 512
    W1C = F2 // CW
    UNITS = 2 * CH
    RAW, HI, LO = 6, 4, 3
    assert 2 * UNITS % RAW == 0 and 2 * UNITS % HI == 0 and 2 * UNITS % LO == 0
    UNIT_OF = [(c, kh) for c in range(W1C) for kh in range(2)] + [(c, kh) for kh in range(2) for c in range(W1C, CH)]
    ROWB = NB + 6
    assert ROWB * NS % P == 0
    KAPPA = 0.6065306597126334
    LEVELS = 7
    RMS_EPS, GN_EPS = 1e-5, 64e-5

    slot_tokens = nc.dram_tensor("slot_tokens", [ROWB * NS, 1], i32).ap()
    h2_rows = nc.dram_tensor("h2_rows", [T, D], f32).ap()
    expert_rows = nc.dram_tensor("expert_rows", [(NB + 1) * NS, D], f32).ap()

    ctx = ExitStack()
    with ctx:
        end_of = {}

        def sb(name, shape, dt=f32):
            tensor = ctx.enter_context(nc.sbuf_tensor(name, shape, dt))
            end_of[name] = nc.sbuf_base
            return tensor

        def rounded(name, owner, owner_words, first_word, shape):
            return nc.alloc_sbuf_tensor_at(name, shape, f32r, offset=end_of[owner] - 4 * (owner_words - first_word))

        def sem(name):
            return ctx.enter_context(nc.semaphore(name))

        slots = sb("slots", [P, CH, KT, CW])
        xs = sb("xs", [P, TT, D])
        hT = sb("hT", [P, KT, T])
        AR = sb("AR", [P, JT, NC, 2 * C])
        BK = sb("BK", [P, JT, NC, 2 * C])
        qk = sb("qk", [P, 2, JT, T])
        shiftbuf = sb("shiftbuf", [P, 2, T + 1])

        def region(t2d, off, size):
            return t2d[:, off:off + size]

        slot_flat = [slots[:, s].rearrange("p k f -> p (k f)") for s in range(CH)]
        S4 = KT * CW
        decay_s = region(slot_flat[3], 0, JT * T).rearrange("p (j t) -> p j t", j=JT)
        decay_c = region(slot_flat[3], JT * T, JT * T).rearrange("p (j t) -> p j t", j=JT)
        vT = region(slot_flat[4], 0, JT * T).rearrange("p (j t) -> p j t", j=JT)
        aT = region(slot_flat[4], JT * T, JT * T).rearrange("p (j t) -> p j t", j=JT)
        G = region(slot_flat[5], 0, TT * HW).rearrange("p (t c) -> p t c", t=TT)
        foxv = region(slot_flat[5], TT * HW, TT * HW).rearrange("p (t c) -> p t c", t=TT)
        decay_e = region(slot_flat[2], 0, JT * T).rearrange("p (j t) -> p j t", j=JT)
        wa = region(slot_flat[2], 4 * T, T)
        gl = region(slot_flat[2], 5 * T, T)
        lora_up = region(slot_flat[2], 6 * T, HW)
        gup = region(slot_flat[2], 7 * T, HW)
        zrow = region(slot_flat[5], TT * HW, D)
        h_hi = rounded("h_hi", "hT", KT * T, 0, [P, KT, T])
        h_lo = rounded("h_lo", "qk", KT * T, 0, [P, KT, T])
        w_in_raw = [region(slot_flat[0], n * 2 * D, 2 * D).rearrange("p (k f) -> p k f", k=KT) for n in range(2)]
        u_hi, u_lo = ([rounded(f"u_{nm}{n}", "slots", CH * S4, S4 + (2 * o + n) * D, [P, KT, P]) for n in range(2)]
                      for o, nm in enumerate(("hi", "lo")))
        fqk = xs[:, :, :].rearrange("p t d -> p (t d)").rearrange("p (a j t) -> p a j t", a=2, j=JT)
        fz = [region(slot_flat[3], (4 + n) * T, T)[0:H, :] for n in range(3)]
        fP = region(slot_flat[0], 0, 2 * T).rearrange("p (b t) -> p b t", b=2)
        fPT = region(slot_flat[0], 2 * T, 2 * T).rearrange("p (b t) -> p b t", b=2)
        fo = region(slot_flat[0], 4 * T, 2 * HW).rearrange("p (b c) -> p b c", b=2)
        fsq = region(slot_flat[0], 6 * T, HW)
        cf = region(slot_flat[3], 7 * T, T)[0:H, :]
        cb = region(slot_flat[2], 0, T).bitcast(bf16).rearrange("p (g t) -> p g t", g=2)[0:H]
        blocks = region(slot_flat[3], 0, (LEVELS + 1) * C).rearrange("p (l c) -> p l c", c=C)
        s1 = slot_flat[1]
        Xm = region(s1, 0, 2 * H * C).rearrange("p (q h t) -> p q h t", q=2, h=H)
        Pm = region(s1, 2 * H * C, 2 * H * C).rearrange("p (q h t) -> p q h t", q=2, h=H)
        Lm = region(slot_flat[4], JT * T, 2 * H * C).rearrange("p (q h t) -> p q h t", q=2, h=H)
        s3 = slot_flat[3]
        CT = region(s3, 0, 2 * H * C).rearrange("p (q h t) -> p q h t", q=2, h=H)
        XT = region(slot_flat[2], 0, NC * H * C).rearrange("p (q h t) -> p q h t", q=NC, h=H)
        qkf = qk[:, :, :, :].rearrange("p a j t -> p (a j t)")
        fv2 = slot_flat[5]
        Lf, CTf, XTf = region(slot_flat[4], JT * T, 2 * H * C), region(s3, 0, 2 * H * C), slot_flat[2]

        def per_chunk(usual, last):
            return [usual] * (NC - 1) + [last]

        KAR = per_chunk(*(region(m, 0, H * 2 * C).rearrange("p (h t) -> p h t", h=H) for m in (qkf, CTf)))
        BR = per_chunk(*(region(m, o, H * C).rearrange("p (h t) -> p h t", h=H) for m, o in ((qkf, 2 * H * C), (Lf, 0))))
        Atok = per_chunk(region(qkf, 3 * H * C, HW), region(Lf, H * C, HW))
        MV = per_chunk(region(qkf, 3 * H * C + HW, HW), region(Lf, H * C + HW, HW))
        Btok = per_chunk(region(fv2, TT * HW, HW), region(XTf, 0, HW))
        Ktok = per_chunk(region(fv2, TT * HW + HW, HW), region(XTf, HW, HW))
        U = per_chunk(region(fv2, TT * HW + 2 * HW, HW), region(XTf, H * C, HW))
        V0 = region(fv2, TT * HW + 3 * HW, HW)
        sbf = shiftbuf[:, :, :].rearrange("p b t -> p (b t)")
        V = [V0, region(sbf, 0, HW)]
        WT = per_chunk(*(region(m, o, JT * C).rearrange("p (j t) -> p j t", j=JT)
                         for m, o in ((sbf, HW), (XTf, H * C + HW))))
        Yc = region(s3, 2 * H * C, HW)
        Yq = region(s3, 2 * H * C + HW, HW)
        ST = region(s3, 2 * H * C + 2 * HW, JT * P).rearrange("p (j v) -> p j v", j=JT)
        STc = region(s3, 2 * H * C + 3 * HW, JT * N).rearrange("p (j v) -> p j v", j=JT)
        STt = region(s3, 2 * H * C + 3 * HW + JT * N, JT * N).rearrange("p (j v) -> p j v", j=JT)
        ARf = AR[:, :, :, :].rearrange("p j c t -> p (j c t)")
        BKf = BK[:, :, :, :].rearrange("p j c t -> p (j c t)")
        hTf = hT[:, :, :].rearrange("p k t -> p (k t)")
        hrow = region(BKf, 0, 2 * D).rearrange("p (b d) -> p b d", b=2)
        junk = region(ARf, 0, D)
        squares = region(BKf, 2 * D, D)
        xg = region(ARf, 0, 2 * D).rearrange("p (b d) -> p b d", b=2)
        xTf = region(ARf, 2 * D, KT * NS)
        act = region(ARf, 2 * D + KT * NS, FT * P)
        hg, hs, hl = (region(BKf, n * CW, CW).rearrange("p (b s) -> p b s", b=2) for n in range(3))
        ovcmp = region(BKf, 3072, NOVF * E).rearrange("p (o e) -> p o e", e=E)
        rt = region(BKf, 3072 + NOVF * E, 6 * E).rearrange("p (n e) -> p n e", e=E)
        BW = JT * NC * 2 * C
        x_hi, x_lo = (rounded(f"x_{nm}", "BK", BW, o, [P, KT, NS]) for nm, o in (("hi", 3 * CW), ("lo", 3 * CW + KT * NS)))
        a_hi = rounded("a_hi", "BK", BW, 3072, [P, FT, NS])
        sel = rounded("sel", "BK", BW, 3072 + FT * NS, [2 * E, 2, NS])
        a_lo = rounded("a_lo", "hT", BW, 3 * D, [P, FT, NS])
        b2r = rounded("b2r", "hT", BW, 2 * D, [2 * E, D])
        b1r = rounded("b1r", "qk", BW, 2 * D, [2 * E, F2])
        raw = [slots[:, 2 + r // 2, r % 2 * 4:r % 2 * 4 + 4, :] for r in range(RAW)]
        w_hi = [rounded(f"hi{r}", "slots", CH * S4, r * S4 // 2, [P, KT // 2, CW]) for r in range(HI)]
        w_lo = [rounded(f"lo{r}", "slots", CH * S4, (10 + r) * S4 // 2, [P, KT // 2, CW]) for r in range(2)]
        w_lo.append(rounded("lo2", "qk", BW, 0, [P, KT // 2, CW]))
        onehot = region(qkf, 0, TT * TOPK * E).rearrange("p (t k e) -> p t k e", t=TT, e=E)
        ob = region(hTf, 0, 2 * D).rearrange("p (b d) -> p b d", b=2)
        gfin = region(hTf, 2048, D)
        outb = [region(hTf, 3072, D), region(hTf, 0, D)]
        biasrows = region(ARf, 0, F2 + D)

        VR = {}
        vrow = 0
        for nm, src in (("g1", attn_norm_g), ("mu", mu), ("w0", w0), ("a0", a0), ("kk", k_k), ("ka", k_a),
                        ("rk", r_k), ("og", out_g), ("g2", ffn_norm_g)):
            n = 1
            for d in src.shape:
                n *= d
            VR[nm] = (vrow, n // P)
            vrow += n // P
        vec_rows = sb("vec_rows", [vrow, P])
        vecT = sb("vecT", [P, vrow + JT])

        def vec(nm, j=None):
            a, n = VR[nm]
            return vecT[:, a:a + n] if j is None else vecT[:, a + j:a + j + 1]

        one_minus_ka = vecT[:, vrow:vrow + JT]
        lnw = sb("lnw", [P, HW])
        lnb = sb("lnb", [P, HW])
        rw = sb("rw", [P, KT, E])
        rb = sb("rb", [P, E])
        expert_row = sb("expert_row", [2 * E, E])
        fb = sb("fb", [H, 1])
        wff = sb("wff", [P, KT, H])
        ident = sb("ident", [P, P])
        blk = sb("blk", [P, P])
        OFF = (TT - 1) * P
        stepm = sb("stepm", [P, OFF + T])
        maskSC = sb("maskSC", [P, 2 * C])
        levmask = sb("levmask", [C, LEVELS, C])
        identb = sb("identb", [P, P], bf16)
        causal = sb("causal", [P, P], bf16)
        selh = sb("selh", [96, H, P], bf16)
        c3 = sb("c3", [96, T], bf16)
        ss = sb("ss", [P, TT])
        eps = sb("eps", [P, 2])
        rstd = sb("rstd", [P, TT])
        ff_hi = sb("ff_hi", [P, KT, H], f32r)
        ff_lo = sb("ff_lo", [P, KT, H], f32r)
        nmx = sb("nmx", [P, TT * H])
        rsum = sb("rsum", [P, TT * H])
        rrec = sb("rrec", [P, H])
        fst = sb("fst", [P, H])
        dend = sb("dend", [P, JT, NC])
        mid = sb("mid", [P, JT, NC])
        bonus = sb("bonus", [P, TT, H])
        gst = sb("gst", [P, 3, H])
        zero_i = sb("zero_i", [P, ROWB * NS // P], i32)
        iotaE = sb("iotaE", [P, E])
        iotaO = sb("iotaO", [P, NOVF])
        iotaEi = sb("iotaEi", [P, E], i32)
        iotaOi = sb("iotaOi", [P, NOVF], i32)
        tokid = sb("tokid", [P, TT], i32)
        lg = sb("lg", [P, TT, E])
        m8 = sb("m8", [P, TT, 8])
        i8 = sb("i8", [P, TT, 8], u32)
        i8f = sb("i8f", [P, TT, 8])
        Msel = sb("Msel", [P, TT, E])
        nm0 = sb("nm0", [P, TT])
        gate = sb("gate", [P, TT, TOPK])
        gsum = sb("gsum", [P, TT])
        cnt = sb("cnt", [P, E])
        ovf_end = sb("ovf_end", [P, E])
        ovf_base = sb("ovf_base", [P, E])
        pos = sb("pos", [P, E])
        qd = sb("qd", [P, E])
        slotm = sb("slotm", [P, E])
        slotk = sb("slotk", [P, TOPK, E])
        slotf = sb("slotf", [P, TT, TOPK])
        sloti = sb("sloti", [P, TT, TOPK], i32)
        ovexp = sb("ovexp", [P, NOVF])
        blkexp = sb("blkexp", [P, NOVF], i32)
        pairs_f = sb("pairs_f", [P, 2])
        pairs_i = sb("pairs_i", [P, 1], i32)
        idx_all = sb("idx_all", [NS, ROWB], i32)
        idx = sb("idx", [NS, 2], i32)

        bank = [ctx.enter_context(nc.psum_tensor(f"bank{b}", [P, 512], f32)) for b in range(8)]

        bank_full = [sem(f"bank_full{b}") for b in range(8)]
        bank_free = [sem(f"bank_free{b}") for b in range(8)]
        x_in = [sem(f"x_in{t}") for t in range(TT)]
        vec_in = sem("vec_in")
        bias_in = sem("bias_in")
        small_in = sem("small_in")
        w_in_loaded = [sem(f"w_in_loaded{s}") for s in range(2)]
        ff_in = sem("ff_in")
        w_out_loaded = [sem(f"w_out_loaded{s}") for s in range(2)]
        pool_step = sem("pool_step")
        consts_ready = sem("consts_ready")
        dve_step = sem("dve_step")
        act_step = sem("act_step")
        vec_ready = sem("vec_ready")
        hrow_ready = sem("hrow_ready")
        act_sq = sem("act_sq")
        sumsq_ready = sem("sumsq_ready")
        mixed = sem("mixed")
        lora_ready = sem("lora_ready")
        cum_ready = sem("cum_ready")
        kksq_ready = sem("kksq_ready")
        kksum_ready = sem("kksum_ready")
        kknorm_ready = sem("kknorm_ready")
        fox_ms_ready = sem("fox_ms_ready")
        fox_rms_ready = sem("fox_rms_ready")
        gn_var_ready = sem("gn_var_ready")
        gn_std_ready = sem("gn_std_ready")
        exps_ready = sem("exps_ready")
        elem_done = sem("elem_done")
        ffln_ready = sem("ffln_ready")
        c3_ready = sem("c3_ready")
        negmax_ready = sem("negmax_ready")
        fo_ready = sem("fo_ready")
        values_done = sem("values_done")
        fox_o_free = sem("fox_o_free")
        scm_ready = sem("scm_ready")
        xt0_ready = sem("xt0_ready")
        ct_ready = sem("ct_ready")
        state_ready = sem("state_ready")
        gn_rstd_ready = sem("gn_rstd_ready")
        scores_masked = sem("scores_masked")
        y_ready = sem("y_ready")
        gates_ready = sem("gates_ready")
        gmax_ready = sem("gmax_ready")
        sel_ready = sem("sel_ready")
        slots_ready = sem("slots_ready")
        tables_ready = sem("tables_ready")
        zeros_stored = sem("zeros_stored")
        rows_zeroed = sem("rows_zeroed")
        h_hi_ready = sem("h_hi_ready")
        h_lo_ready = sem("h_lo_ready")
        u_hi_ready = sem("u_hi_ready")
        u_lo_ready = sem("u_lo_ready")
        ff_split = sem("ff_split")
        tokens_stored = sem("tokens_stored")
        idx_in = sem("idx_in")
        h2_stored = [sem(f"h2_stored{t}") for t in range(TT)]
        idx_copied = sem("idx_copied")
        waited = sem("waited")
        xg_loaded = [sem(f"xg_loaded{q}") for q in range(2)]
        raw_loaded = [sem(f"raw_loaded{r}") for r in range(RAW)]
        hi_ready = sem("hi_ready")
        lo_ready = [sem(f"lo_ready{n}") for n in range(2)]
        unit_used = sem("unit_used")
        bias_split = sem("bias_split")
        xt_full = sem("xt_full")
        xt_free = sem("xt_free")
        x_hi_ready = sem("x_hi_ready")
        x_lo_ready = sem("x_lo_ready")
        sel_set = sem("sel_set")
        hid_free = [sem(f"hid_free{p}") for p in range(2)]
        glu_ready = sem("glu_ready")
        sig_ready = sem("sig_ready")
        lin_ready = sem("lin_ready")
        act_ready = sem("act_ready")
        at_full = sem("at_full")
        a_hi_ready = sem("a_hi_ready")
        a_lo_ready = sem("a_lo_ready")
        y_free = [sem(f"y_free{p}") for p in range(2)]
        store_done = [sem(f"store_done{q}") for q in range(2)]
        gathered = [sem(f"gathered{t}") for t in range(TT)]
        gfin_in = sem("gfin_in")
        summed = sem("summed")
        normed = sem("normed")
        out_ready = sem("out_ready")
        out_stored = [sem(f"out_stored{t}") for t in range(TT)]

        plan, uses = {}, [0] * 8

        def put(name, b):
            plan[name] = (b, uses[b])
            uses[b] += 1

        U_ORDER = [12, 13, 14, 15, 0, 1, 2, 3, 4, 5, 6, 7, 8, 9, 10, 11, 16, 17, 18, 19, 20, 21, 22, 23, 24, 25]
        put(("vec",), 0)
        for tt in range(TT):
            for half in range(2):
                put(("hT", tt, half), (1 + 2 * tt + half) % 4)
        nrot = 0

        def rot(name):
            nonlocal nrot
            put(name, nrot % 8)
            nrot += 1

        for m in U_ORDER:
            rot(("u", m))
            if m == 15:
                rot(("ff",))
            if m == 3:
                for j in range(JT):
                    rot(("z", j))
                for j in range(JT):
                    rot(("a", j))
            if m == 11:
                for tt in range(TT):
                    rot(("g", tt))
            if m == 16:
                for j in range(JT):
                    rot(("ss", j))
            if m > 22:
                rot(("fvT", m - 23))
        rot(("fvT", JT - 1))
        rot(("bonus",))
        units = [(qb, h) for qb in range(TT) for h in range(H)]
        uses_before_fox = list(uses)
        FOX_STEPS = len(units) + 4

        def inversion(pair):
            st = [("L", tt, g) for tt in pair for g in range(2)]
            st += [("X0", tt, hf) for tt in pair for hf in range(2)]
            for lv in range(1, LEVELS):
                st += [("P", tt, lv, hf) for tt in pair for hf in range(2)]
                for tt in pair:
                    for hf in range(2):
                        if lv < LEVELS - 1:
                            st.append(("X", tt, lv, hf))
                        st.append(("XT", tt, lv, hf))
            return st

        def prepare(tt):
            return [("vt", tt), ("bt", tt), ("kt", tt), ("at", tt)] \
                + [("KAR", tt, g, jj) for jj in range(2) for g in range(2)] + [("BR", tt, g) for g in range(2)] \
                + [("MV", tt), ("W", tt)]

        def between(a, b):
            st, taken = [], 0
            for n, stage in enumerate(a):
                st.append(stage)
                while taken * len(a) < (n + 1) * len(b) and taken < len(b):
                    st.append(b[taken])
                    taken += 1
            return st

        rwkv_stages = between([("fox", i) for i in range(FOX_STEPS)], inversion((0, 1)))
        rwkv_stages += between(inversion((2, 3)),
                               prepare(0) + [("U", 0), ("Yfrom", 0), ("state", 0), ("Y", 0)]
                               + prepare(1) + [("U", 1), ("yT", 0), ("Yfrom", 1), ("state", 1), ("Y", 1)]
                               + prepare(2)[:-1])
        rwkv_stages += [("W", 2)] + between(prepare(3), [("U", 2), ("Yfrom", 2), ("state", 2), ("yT", 1), ("Y", 2)])
        rwkv_stages += [("U", 3), ("o", 0, 0), ("Yfrom", 3), ("o", 0, 1), ("yT", 2), ("Y", 3), ("norm", 0),
                        ("o", 1, 0), ("h2T", 0, 0), ("h2T", 0, 1), ("o", 1, 1), ("lg", 0), ("norm", 1),
                        ("yT", 3), ("o", 2, 0), ("h2T", 1, 0), ("h2T", 1, 1), ("o", 2, 1), ("lg", 1), ("norm", 2),
                        ("o", 3, 0), ("h2T", 2, 0), ("h2T", 2, 1), ("o", 3, 1), ("lg", 2), ("norm", 3),
                        ("h2T", 3, 0), ("h2T", 3, 1), ("lg", 3)]
        nth_of = {0: 0, 1: 0, "r": 0}
        for st in rwkv_stages:
            kind, tt = st[0], st[1]
            if kind == "fox":
                if tt < len(units):
                    put(("S", *units[tt]), tt % 2)
                if 1 <= tt <= len(units):
                    put(("PT", *units[tt - 1]), 2)
                if tt >= H + 3 and tt % H == 3:
                    put(("foT", tt // H - 1), 2)
            elif kind in ("L", "X0", "P", "X", "XT") and tt < 2:
                put(st, 4 + 2 * tt + nth_of[tt] % 2)
                nth_of[tt] += 1
            elif kind in ("L", "X0", "P", "X", "XT"):
                put(st, 3 * (tt % 2) + nth_of[tt % 2] % 3)
                nth_of[tt % 2] += 1
            elif kind == "Yfrom":
                put(("Y", tt), 7)
            elif kind in ("U", "state", "yT") or kind in ("vt", "bt", "kt", "at", "KAR", "BR", "MV", "W") and tt < 3:
                put(st, 6)
            elif kind not in ("Y", "norm"):
                put(st, nth_of["r"] % 6)
                nth_of["r"] += 1
        put(("cnt",), 7)
        for tt in range(TT):
            put(("pos", tt), tt % 2)

        def filled(eng, *name):
            b, n = plan[name]
            eng.wait_ge(bank_full[b], n + 1)

        def emptied(eng, *name):
            b, n = plan[name]
            eng.wait_ge(bank_free[b], n + 1)

        def free_of(name):
            return bank_free[plan[name][0]]

        def by_gpsimd(n):
            return n % 3 == 1

        def low_part(i, n):
            m = 2 * UNITS // 3 * i
            if by_gpsimd(n):
                return lo_ready[1], m + (n // 3 + 1 + RAW // 3)
            return lo_ready[0], m * 2 + (n // 3 * 2 + 1 + (n % 3 == 2) + RAW // 3 * 2)

        def wait_used(eng, i, n):
            eng.wait_ge(unit_used, i * (2 * UNITS) + (n + 1 + HI))

        block = ctx.enter_context(nc.Block())

        W1_T = w1[0].rearrange("e (k p) f -> p e k f", p=P)
        W2_T = w2[0].rearrange("e (k p) f -> p e k f", p=P)

        def load_unit(eng, e, n):
            c, kh = UNIT_OF[n % UNITS]
            src, off = (W1_T, c * CW) if c < W1C else (W2_T, (c - W1C) * CW)
            k = slice(kh * KT // 2, (kh + 1) * KT // 2)
            eng.dma_start(raw[n % RAW], src[:, bass.ds(e, 1), k, off:off + CW].rearrange("p a k f -> p (a k) f"))\
               .then_inc(raw_loaded[n % RAW], 16)

        @block.sync
        def _(sp):
            for tt in range(TT):
                sp.dma_start(xs[:, tt, :], x[0, tt * P:(tt + 1) * P, :]).then_inc(x_in[tt], 16)
            at = 0
            for src in (attn_norm_g, mu, w0, a0, k_k, k_a, None, out_g, ffn_norm_g):
                v = r_k[0].rearrange("h n -> (h n)") if src is None else src[0]
                n = v.shape[0] // P
                sp.dma_start(vec_rows[at:at + n, :], v.rearrange("(j p) -> j p", p=P)).then_inc(vec_in, 16)
                at += n
            w_in_v = w_in[0].rearrange("(k p) f -> p k f", p=P)
            for n in range(len(U_ORDER) // 2):
                if n >= 2:
                    sp.wait_ge(u_lo_ready, 2 * (n - 1))
                o = U_ORDER[2 * n] * P
                sp.dma_start(w_in_raw[n % 2], w_in_v[:, :, o:o + 2 * P]).then_inc(w_in_loaded[n % 2], 16)
            w_out_v = w_out[0].rearrange("(k p) f -> p k f", p=P)
            for half in range(2):
                if half == 0:
                    filled(sp, "S", *units[-1])
                    for tt in range(TT):
                        sp.dma_start(xs[:, tt, :], x[0, tt * P:(tt + 1) * P, :]).then_inc(x_in[tt], 16)
                    filled(sp, "foT", TT - 1)
                else:
                    filled(sp, "XT", TT - 1, LEVELS - 1, 1)
                sp.dma_start(slots[:, half], w_out_v[:, :, half * CW:(half + 1) * CW]).then_inc(w_out_loaded[half], 16)
            filled(sp, "yT", TT - 1)
            emptied(sp, "Y", TT - 1)
            for n in range(RAW):
                load_unit(sp, 0, n)
            filled(sp, "Y", TT - 1)
            for g in range(2):
                sp.dma_start(biasrows[g * E:(g + 1) * E, 0:F2], b1[0]).then_inc(bias_in, 16)
                sp.dma_start(biasrows[g * E:(g + 1) * E, F2:F2 + D], b2[0]).then_inc(bias_in, 16)

            def next_units(i, q, e, first=0):
                for u in range(first, UNITS):
                    n = q * UNITS + u
                    sp.wait_ge(*low_part(i, n - RAW))
                    load_unit(sp, e, n)

            next_units(0, 0, 0, RAW)
            next_units(0, 1, 1)
            with sp.Fori(1, E // 2) as i:
                for q in range(2):
                    next_units(i, q, i * 2 + q)
            sp.wait_ge(tables_ready, 1)
            npairs = sp.value_load(pairs_i[0:1, 0:1], min_val=E // 2, max_val=NB // 2)
            with sp.Fori(E // 2, NB // 2) as i:
                with sp.If(i < npairs):
                    for q in range(2):
                        e = sp.value_load(blkexp[0:1, bass.ds(i * 2 + (q - E), 1)], min_val=0, max_val=E - 1)
                        next_units(i, q, e)
            for tt in range(TT):
                sp.wait_ge(out_ready, tt + 1)
                sp.dma_start(out[0, tt * P:(tt + 1) * P, :], outb[tt % 2]).then_inc(out_stored[tt], 16)
            for tt in range(TT):
                sp.wait_ge(out_stored[tt], 16)

        @block.gpsimd
        def _(pool):
            steps = [0]

            def step(ins):
                steps[0] += 1
                ins.then_inc(pool_step, 1)
                pool.wait_ge(pool_step, steps[0])

            def select(dst, pattern, op, fill, base, cm):
                step(nc.gpsimd.affine_select(out=dst, in_=dst, compare_op=op, fill=fill, base=base,
                                             pattern=pattern, channel_multiplier=cm))

            step(nc.gpsimd.memset(eps[:, 0:1], RMS_EPS))
            step(nc.gpsimd.memset(eps[:, 1:2], GN_EPS))
            step(nc.gpsimd.memset(ident[:, :], 0.0))
            select(ident[:, :], [[-1, P]], ALU.not_equal, 1.0, 0, 1)
            pool.sem_inc(consts_ready, 1)
            step(nc.gpsimd.memset(shiftbuf[:, :, 0:1], 0.0))
            step(nc.gpsimd.memset(blk[:, :], 0.0))
            step(nc.gpsimd.memset(blk[0:N, 0:N], 1.0))
            step(nc.gpsimd.memset(blk[N:P, N:P], 1.0))
            pool.sem_inc(consts_ready, 1)
            def w_in_low_part(n):
                pool.wait_ge(u_hi_ready, n + 1)
                nc.gpsimd.tensor_tensor(u_lo[n % 2][:, :, :], w_in_raw[n // 2 % 2][:, :, n % 2 * P:(n % 2 + 1) * P],
                                        u_hi[n % 2][:, :, :], ALU.subtract).then_inc(u_lo_ready, 1)

            w_in_low_part(0)
            w_in_low_part(1)
            step(nc.gpsimd.memset(stepm[:, :], 1.0))
            select(stepm[:, :], [[1, OFF + T]], ALU.is_ge, 0.0, -OFF, -1)
            step(nc.gpsimd.memset(identb[:, :], 0.0))
            select(identb[:, :], [[-1, P]], ALU.not_equal, 1.0, 0, 1)
            step(nc.gpsimd.memset(causal[:, :], 0.0))
            select(causal[:, :], [[-1, P]], ALU.is_ge, -1e30, 0, 1)
            w_in_low_part(2)
            step(nc.gpsimd.memset(selh[:, :, :], 0.0))
            for g in range(3):
                select(selh[:, :, :], [[-1, H], [0, P]], ALU.not_equal, 1.0, -32 * g, 1)
            step(nc.gpsimd.memset(c3[:, :], 0.0))
            step(nc.gpsimd.memset(maskSC[:, :], 1.0))
            select(maskSC[:, 0:C], [[1, C]], ALU.is_ge, 0.0, -1, -1)
            select(maskSC[:, C:2 * C], [[1, C]], ALU.is_ge, 0.0, 0, -1)
            w_in_low_part(3)
            step(nc.gpsimd.memset(blocks[:, :, :], 1.0))
            for lv in range(LEVELS):
                w = 1 << lv
                select(blocks[:, lv, :], [[-w, C // w], [0, w]], ALU.is_ge, 0.0, 0, 1)
                select(blocks[:, lv, :], [[w, C // w], [0, w]], ALU.is_ge, 0.0, w - 1, -1)
            step(nc.gpsimd.tensor_tensor(levmask[:, :, :], blocks[:, 1:, :], blocks[:, 0:LEVELS, :], ALU.subtract))
            pool.sem_inc(consts_ready, 1)
            for n in range(4, 8):
                w_in_low_part(n)
            step(nc.gpsimd.iota(iotaEi[:, :], pattern=[[1, E]], base=0, channel_multiplier=0))
            step(nc.gpsimd.iota(iotaOi[:, :], pattern=[[1, NOVF]], base=0, channel_multiplier=0))
            step(nc.gpsimd.iota(tokid[:, :], pattern=[[P, TT]], base=0, channel_multiplier=1))
            step(nc.gpsimd.tensor_copy(iotaE[:, :], iotaEi[:, :]))
            step(nc.gpsimd.tensor_copy(iotaO[:, :], iotaOi[:, :]))
            step(nc.gpsimd.memset(zero_i[:, :], 0))
            pool.sem_inc(consts_ready, 1)
            step(nc.gpsimd.memset(zrow, 0.0))
            for o in range(NOVF):
                if o % 2 == 1:
                    w_in_low_part(o // 2 + 8)
                pool.dma_start(expert_rows[(E + o + 1) * NS:(E + o + 2) * NS, :], zrow[0:NS, :]).then_inc(rows_zeroed, 16)
            for n in range(8 + NOVF // 2, len(U_ORDER)):
                w_in_low_part(n)
            nrow = ROWB * NS // P
            pool.dma_start(slot_tokens.rearrange("(p n) a -> p (n a)", p=P), zero_i[:, 0:nrow]).then_inc(zeros_stored, 16)

            for st in rwkv_stages:
                kind, tt = st[0], st[1]
                if kind == "X0" and st[2] == 1 or kind == "P" and st[3] == 1 and st[2] < LEVELS - 1:
                    lv = 1 if kind == "X0" else st[2] + 1
                    if lv == 1:
                        pool.wait_ge(scm_ready, tt + 1)
                        if tt >= 2:
                            filled(pool, "P", tt - 2, LEVELS - 1, 1)
                    else:
                        filled(pool, *st)
                    nc.gpsimd.tensor_tensor(CT[:, tt % 2], Lm[:, tt % 2],
                                            levmask[:, lv, :].unsqueeze(1).to_broadcast([C, H, C]), ALU.mult)\
                        .then_inc(ct_ready, 1)
                if kind == "yT":
                    def heads(ap):
                        return ap.rearrange("p (h v) -> p h v", h=H)
                    pool.wait_ge(gn_rstd_ready, tt + 1)
                    emptied(pool, "vt", tt)
                    emptied(pool, "bonus")
                    emptied(pool, "g", tt)
                    step(nc.gpsimd.tensor_tensor(heads(Yc), heads(Yc), gst[:, 1, :].unsqueeze(2).to_broadcast([P, H, N]), ALU.mult))
                    step(nc.gpsimd.tensor_tensor(heads(Yq), heads(V[tt % 2]),
                                                 bonus[:, tt, :].unsqueeze(2).to_broadcast([P, H, N]), ALU.mult))
                    step(nc.gpsimd.tensor_tensor(Yc, Yc, lnw[:, :], ALU.mult))
                    step(nc.gpsimd.tensor_tensor(Yq, Yq, lnb[:, :], ALU.add))
                    step(nc.gpsimd.tensor_tensor(Yc, Yc, Yq, ALU.add))
                    nc.gpsimd.tensor_tensor(Yq, Yc, G[:, tt, :], ALU.mult).then_inc(y_ready, 1)

            def low_parts(i, n):
                wait_used(pool, i, n - LO)
                pool.wait_ge(hi_ready, i * (2 * UNITS) + (n + 1))
                nc.gpsimd.tensor_tensor(w_lo[n % LO][:, :, :], raw[n % RAW], w_hi[n % HI][:, :, :], ALU.subtract)\
                    .then_inc(lo_ready[1], 1)

            pool.sem_inc(lo_ready[1], RAW // 3)
            pool.wait_ge(hi_ready, 1)
            nc.gpsimd.tensor_tensor(w_lo[0][:, :, :], raw[0], w_hi[0][:, :, :], ALU.subtract).then_inc(lo_ready[0], 1)
            low_parts(0, 1)
            pool.wait_ge(zeros_stored, 16)
            for tt in range(TT):
                pool.wait_ge(slots_ready, tt + 1)
                for k in range(TOPK):
                    pool.indirect_dma_start(
                        slot_tokens, bass.IndirectOffsetOnAxis(ap=sloti[:, tt, k:k + 1], axis=0),
                        tokid[:, tt:tt + 1], None).then_inc(tokens_stored, 16)
            pool.wait_ge(tokens_stored, 16 * TT * TOPK)
            pool.dma_start(idx_all[:, :], slot_tokens.rearrange("(b s) a -> s (b a)", s=NS),
                           allow_slow_non_contiguous=True).then_inc(idx_in, 16)
            pool.wait_ge(bias_split, 2)
            pool.wait_ge(idx_in, 16)
            for tt in range(TT):
                pool.wait_ge(h2_stored[tt], 16)

            def gather(b, q, reused=True):
                if reused:
                    pool.wait_ge(xt_full, b)
                    pool.sem_inc(waited, 1)
                nc.gpsimd.tensor_copy(idx[:, q:q + 1], idx_all[:, bass.ds(b + 1, 1)]).then_inc(idx_copied, 1)
                pool.wait_ge(idx_copied, b + 1)
                pool.sem_inc(waited, 1)
                pool.indirect_dma_start(xg[0:NS, q, :], None, h2_rows,
                                        bass.IndirectOffsetOnAxis(ap=idx[:, q:q + 1], axis=0))\
                    .then_inc(xg_loaded[q], 16)

            def block_work(i, q, done=()):
                for u in range(UNITS):
                    n = q * UNITS + u
                    if by_gpsimd(n) and u not in done:
                        low_parts(i, n)
                    if u == 1:
                        gather(i * 2 + (q + 1), 1 - q)

            gather(0, 0, False)
            block_work(0, 0, done=(1,))
            block_work(0, 1)
            with pool.Fori(1, E // 2) as i:
                for q in range(2):
                    block_work(i, q)
            pool.wait_ge(tables_ready, 1)
            npairs = pool.value_load(pairs_i[0:1, 0:1], min_val=E // 2, max_val=NB // 2)
            with pool.Fori(E // 2, NB // 2) as i:
                with pool.If(i < npairs):
                    for q in range(2):
                        block_work(i, q)
            for q in range(2):
                pool.wait_ge(store_done[q], npairs * 16 + (16 + 16 * q))
            pool.sem_inc(waited, 1)
            for tt in range(TT):
                for k in range(TOPK):
                    pool.indirect_dma_start(
                        slots[:, tt, 2 * k:2 * k + 2, :].rearrange("p a f -> p (a f)"), None, expert_rows,
                        bass.IndirectOffsetOnAxis(ap=sloti[:, tt, k:k + 1], axis=0)).then_inc(gathered[tt], 16)

        def fox_rms(act, qb):
            act.wait_ge(fox_ms_ready, qb + 1)
            nc.scalar.activation(fst[:, :], fst[:, :], ACT.Sqrt, bias=eps[:, 0:1], scale=1.0 / N).then_inc(fox_rms_ready, 1)

        def fox_out_T(act, qb):
            filled(act, "foT", qb)
            for j in range(JT):
                ins = nc.scalar.mul(hT[:, JT + j, qb * P:(qb + 1) * P], bank[2][:, j * P:(j + 1) * P], vec("og", j))
            ins.then_inc(free_of(("foT", qb)), 1)

        @block.scalar
        def _(act):
            steps = [0]

            def step(ins):
                steps[0] += 1
                ins.then_inc(act_step, 1)
                act.wait_ge(act_step, steps[0])

            def root_mean(tt, n, done):
                act.wait_ge(act_sq, n)
                nc.scalar.activation(ss[:, tt:tt + 1], ss[:, tt:tt + 1], ACT.Sqrt, bias=eps[:, 0:1], scale=1.0 / D)\
                    .then_inc(done, 1)

            act.wait_ge(consts_ready, 1)
            for tt in range(TT):
                act.wait_ge(x_in[tt], 16)
                nc.scalar.activation(junk, xs[:, tt, :], ACT.Square, accum_out=ss[:, tt:tt + 1]).then_inc(act_sq, 1)
                root_mean(tt, tt + 1, sumsq_ready)
            for tt in range(TT):
                for half in range(2):
                    emptied(act, "hT", tt, half)
                    nc.scalar.copy(h_hi[:, half * 4:half * 4 + 4, tt * P:(tt + 1) * P],
                                   shiftbuf[:, half, 1:T + 1].rearrange("p (k t) -> p k t", k=4)).then_inc(h_hi_ready, 1)

            def w_in_high_part(n):
                act.wait_ge(w_in_loaded[n // 2 % 2], 16 * (n // 4 + 1))
                if n >= 2:
                    filled(act, "u", U_ORDER[n - 2])
                nc.scalar.copy(u_hi[n % 2][:, :, :], w_in_raw[n // 2 % 2][:, :, n % 2 * P:(n % 2 + 1) * P])\
                    .then_inc(u_hi_ready, 1)

            w_in_high_part(0)
            w_in_high_part(1)

            def v_transposed(j):
                filled(act, "fvT", j)
                if j == 0:
                    act.wait_ge(rows_zeroed, 16 * NOVF)
                nc.scalar.copy(foxv[:, :, j * P:(j + 1) * P], bank[plan[("fvT", j)][0]][:, :].rearrange("p (t c) -> p t c", t=TT))\
                    .then_inc(free_of(("fvT", j)), 1)

            act.dma_start(wff[:, :, :], w_in[0, :, w_in.shape[2] - H:].rearrange("(k p) f -> p k f", p=P)).then_inc(ff_in, 16)
            act.dma_start(lora_up[0:LORA, :], w_up[0]).then_inc(small_in, 16)
            act.dma_start(lora_up[LORA:P, :], a_up[0]).then_inc(small_in, 16)
            act.dma_start(gup, g_up[0]).then_inc(small_in, 16)
            act.dma_start(lnw[:, :], ln_w.to_broadcast([P, HW])).then_inc(small_in, 16)
            act.dma_start(lnb[:, :], ln_b.to_broadcast([P, HW])).then_inc(small_in, 16)
            act.dma_start(rw[:, :, :], router_w[0].rearrange("(k p) e -> p k e", p=P)).then_inc(small_in, 16)
            act.dma_start(rb[:, :], router_b.to_broadcast([P, E])).then_inc(small_in, 16)
            act.dma_start(fb[:, :], f_bias[0].rearrange("(h a) -> h a", a=1)).then_inc(small_in, 16)
            act.wait_ge(vec_ready, 1)
            nth = 0
            for i, m in enumerate(U_ORDER):
                if i + 2 < len(U_ORDER):
                    w_in_high_part(i + 2)
                filled(act, "u", m)
                src = bank[plan[("u", m)][0]][:, :]
                if m < 14:
                    if nth >= 2:
                        act.wait_ge(mixed, nth - 1)
                    nc.scalar.copy(shiftbuf[:, nth % 2, 1:T + 1], src).then_inc(free_of(("u", m)), 1)
                    nth += 1
                elif m < 18:
                    nc.scalar.mul(fqk[:, 0, m - 14, :], src, float(N) ** -0.5).then_inc(free_of(("u", m)), 1)
                elif m < 22:
                    nc.scalar.copy(fqk[:, 1, m - 18, :], src).then_inc(free_of(("u", m)), 1)
                else:
                    if m < 24:
                        act.wait_ge(mixed, 14)
                    else:
                        filled(act, "fvT", m - 24)
                    nc.scalar.copy(shiftbuf[:, m % 2, 1:T + 1], src).then_inc(free_of(("u", m)), 1)
                if m == 13:
                    act.wait_ge(mixed, 2)
                    step(nc.scalar.activation(wa[0:LORA, :], wa[0:LORA, :], ACT.Tanh))
                    step(nc.scalar.activation(gl, gl, ACT.Sigmoid))
                    act.sem_inc(lora_ready, 1)
                if m == 0:
                    emptied(act, "ff")
                    step(nc.scalar.activation(fz[1], fz[0], ACT.Abs))
                    step(nc.scalar.activation(fz[1], fz[1], ACT.Exp, scale=-1.0))
                    nc.scalar.activation(fz[1], fz[1], ACT.Ln, bias=1.0).then_inc(ffln_ready, 1)
                if m == 3:
                    act.wait_ge(consts_ready, 3)
                    for nm, dst, bias in (("z", decay_s, "w0"), ("a", aT, "a0")):
                        for j in range(JT):
                            filled(act, nm, j)
                            nc.scalar.activation(dst[:, j, :], bank[plan[(nm, j)][0]][:, :], ACT.Sigmoid,
                                                 bias=vec(bias, j)).then_inc(free_of((nm, j)), 1)
                if m == 11:
                    for tt in range(TT):
                        filled(act, "g", tt)
                        nc.scalar.copy(G[:, tt, :], bank[plan[("g", tt)][0]][:, :]).then_inc(free_of(("g", tt)), 1)
                if m == 16:
                    for j in range(JT):
                        act.wait_ge(kksum_ready, j + 1)
                        nc.scalar.activation(AR[:, j, :, 0:C], AR[:, j, :, 0:C], ACT.Sqrt).then_inc(kknorm_ready, 1)
                if 17 <= m < 17 + JT:
                    j = m - 17
                    act.wait_ge(cum_ready, j + 1)
                    step(nc.scalar.activation(decay_e[:, j, :], decay_c[:, j, :], ACT.Exp, scale=-KAPPA))
                    step(nc.scalar.activation(decay_c[:, j, :], decay_c[:, j, :], ACT.Exp, scale=KAPPA))
                    step(nc.scalar.activation(dend[:, j, 0:NC - 1], dend[:, j, 0:NC - 1], ACT.Exp, scale=-KAPPA))
                    nc.scalar.activation(decay_s[:, j, :], decay_s[:, j, :], ACT.Exp, scale=-KAPPA).then_inc(exps_ready, 1)
                if m > 22:
                    v_transposed(m - 23)
            v_transposed(JT - 1)
            filled(act, "bonus")
            nc.scalar.copy(bonus[:, :, :], bank[plan[("bonus",)][0]][:, 0:TT * H].rearrange("p (t h) -> p t h", h=H))\
                .then_inc(free_of(("bonus",)), 1)
            act.wait_ge(elem_done, JT)
            def fox_step(i):
                if i < len(units):
                    qb, h = units[i]
                    keys = (qb + 1) * P
                    act.wait_ge(negmax_ready, i + 1)
                    if i >= 2:
                        filled(act, "PT", *units[i - 2])
                    nc.scalar.activation(fP[:, i % 2, 0:keys], bank[i % 2][:, 0:keys], ACT.Exp, bias=nmx[:, i:i + 1],
                                         accum_out=rsum[:, i:i + 1]).then_inc(free_of(("S", qb, h)), 1)
                if i > H and i % H == 1:
                    fox_rms(act, i // H - 1)
                if i > H and i % H == 3:
                    fox_out_T(act, i // H - 1)

            def move(name, dst, src):
                filled(act, *name)
                nc.scalar.copy(dst, src).then_inc(free_of(name), 1)

            def high_part(i, n):
                r = n % RAW
                act.wait_ge(raw_loaded[r], i * (2 * UNITS // RAW * 16) + (n // RAW + 1) * 16)
                wait_used(act, i, n - HI)
                nc.scalar.copy(w_hi[n % HI][:, :, :], raw[r]).then_inc(hi_ready, 1)

            def four_heads(ap, hf):
                return ap[:, 4 * hf:4 * hf + 4, :].rearrange("p h t -> p (h t)")

            for st in rwkv_stages:
                kind, tt, q = st[0], st[1], st[1] % 2
                if kind == "fox":
                    fox_step(tt)
                    continue
                ps = bank[plan[st][0]][:, :] if st in plan else None
                if kind == "X0":
                    move(st, four_heads(Xm[:, q], st[2]), ps)
                elif kind == "P":
                    move(st, four_heads(Pm[:, q], st[3]), ps)
                elif kind == "vt":
                    if tt >= 2:
                        act.wait_ge(y_ready, tt - 1)
                    move(st, V[q], ps)
                elif kind == "o":
                    if st[2] == 1:
                        emptied(act, "o", tt, 1)
                        emptied(act, "o", tt, 0)
                        nc.scalar.activation(squares, xs[:, tt, :], ACT.Square, accum_out=ss[:, tt:tt + 1]).then_inc(act_sq, 1)
                        root_mean(tt, TT + tt + 1, sumsq_ready)
                elif kind == "norm":
                    act.wait_ge(hrow_ready, TT + tt + 1)
                    act.dma_start(h2_rows[tt * P:(tt + 1) * P, :], hrow[:, tt % 2, :]).then_inc(h2_stored[tt], 16)
                    if tt == TT - 1:
                        filled(act, "o", TT - 1, 1)
                        filled(act, "o", TT - 1, 0)
                        for n in range(HI):
                            high_part(0, n)
                elif kind == "lg":
                    act.wait_ge(gmax_ready, tt + 1)
                    nc.scalar.activation(gate[:, tt, :], m8[:, tt, 0:TOPK], ACT.Exp, bias=nm0[:, tt:tt + 1],
                                         accum_out=gsum[:, tt:tt + 1]).then_inc(gates_ready, 1)
                elif kind in ("bt", "kt"):
                    if 0 < tt < NC - 1:
                        filled(act, "state", tt - 1)
                    move(st, (Btok if kind == "bt" else Ktok)[tt], ps)
                elif kind == "at":
                    move(st, Atok[tt], ps)
                elif kind == "W":
                    move(st, WT[tt], ps.rearrange("p (j t) -> p j t", j=JT))
                elif kind == "MV":
                    move(st, MV[tt], ps)
                elif kind == "Y":
                    act.wait_ge(gn_var_ready, tt + 1)
                    nc.scalar.activation(gst[:, 1, :], gst[:, 1, :], ACT.Sqrt, bias=eps[:, 1:2], scale=1.0 / N)\
                        .then_inc(gn_std_ready, 1)
                elif kind == "yT":
                    move(st, hT[:, 0:JT, tt * P:(tt + 1) * P], ps.rearrange("p (j t) -> p j t", j=JT))
            filled(act, "lg", TT - 1)
            act.wait_ge(bias_in, 64)
            nc.scalar.copy(b1r[:, :], biasrows[0:2 * E, 0:F2])
            nc.scalar.copy(b2r[:, :], biasrows[0:2 * E, F2:F2 + D]).then_inc(bias_split, 1)

            def x_high(b):
                act.wait_ge(xt_free, b + 2)
                nc.scalar.copy(x_hi[:, :, :], xTf.rearrange("p (k s) -> p k s", k=KT)).then_inc(x_hi_ready, 1)

            def act_high(b, c):
                act.wait_ge(at_full, b * W1C + (c + 1))
                o = c // 2 * 2 * NS
                nc.scalar.copy(a_hi[:, 2 * c:2 * c + 2, :], bank[4 + c % 2][:, o:o + 2 * NS].rearrange("p (f s) -> p f s", f=2))\
                    .then_inc(a_hi_ready, 1)

            def store_previous(i, q):
                b = i * 2 + q
                act.wait_ge(store_done[1 - q], i * 16 + 16)
                wait_used(act, i, q * UNITS - 1)
                for h in range(2):
                    nc.scalar.copy(ob[0:NS, 1 - q, h * CW:(h + 1) * CW], bank[6 + h][0:NS, :]).then_inc(y_free[h], 1)
                for h in range(2):
                    act.wait_ge(y_free[h], b + 1)
                act.dma_start(expert_rows[bass.ds(b * NS, NS), :], ob[0:NS, 1 - q, :]).then_inc(store_done[1 - q], 16)

            def block_work(i, q, first=False):
                b = i * 2 + q
                for u in range(UNITS):
                    if not (first and u < HI):
                        high_part(i, q * UNITS + u)
                    if u == 3:
                        if first:
                            x_high(0)
                        store_previous(i, q)
                    if u in (5, 7, 9, 11):
                        c = (u - 5) // 2
                        act.wait_ge(glu_ready, b * W1C + (c + 1))
                        nc.scalar.activation(hs[0:NS, c % 2], hg[0:NS, c % 2], ACT.Sigmoid, scale=1.702).then_inc(sig_ready, 1)
                    if u in (8, 10, 11):
                        act_high(b, {8: 0, 10: 1, 11: 2}[u])
                act_high(b, 3)
                x_high(b + 1)

            for q in range(2):
                act.sem_inc(store_done[q], 16)
            block_work(0, 0, first=True)
            block_work(0, 1)
            with act.Fori(1, E // 2) as i:
                for q in range(2):
                    block_work(i, q)
            act.wait_ge(tables_ready, 1)
            npairs = act.value_load(pairs_i[0:1, 0:1], min_val=E // 2, max_val=NB // 2)
            with act.Fori(E // 2, NB // 2) as i:
                with act.If(i < npairs):
                    for q in range(2):
                        block_work(i, q)
            store_previous(npairs, 0)
            act.dma_start(gfin, final_norm_g.rearrange("(a d) -> a d", a=1).to_broadcast([P, D])).then_inc(gfin_in, 16)
            for tt in range(TT):
                act.wait_ge(summed, tt + 1)
                nc.scalar.activation(junk, xs[:, tt, :], ACT.Square, accum_out=ss[:, tt:tt + 1]).then_inc(act_sq, 1)
                root_mean(tt, 2 * TT + tt + 1, normed)

        @block.tensor
        def _(pe):
            def begin(*name):
                b, n = plan[name]
                if n > 0:
                    pe.wait_ge(bank_free[b], n)
                return bank[b]

            def end(ins, *name):
                ins.then_inc(bank_full[plan[name][0]], 1)

            pe.sem_inc(unit_used, HI)
            pe.wait_ge(consts_ready, 1)
            pe.wait_ge(vec_in, 16 * 9)
            ps = begin("vec")
            end(nc.tensor.transpose(ps[:, 0:vrow], vec_rows[:, :], ident[0:vrow, 0:vrow]), "vec")
            for tt in range(TT):
                pe.wait_ge(hrow_ready, tt + 1)
                for half in range(2):
                    ps = begin("hT", tt, half)
                    for k in range(4):
                        o = (half * 4 + k) * P
                        ins = nc.tensor.transpose(ps[:, k * P:(k + 1) * P], hrow[:, tt % 2, o:o + P], ident[:, :])
                    end(ins, "hT", tt, half)
            pe.wait_ge(h_lo_ready, 2 * TT)

            def v_transposes(j):
                ps = begin("fvT", j)
                emptied(pe, "u", 22 + j)
                for tt in range(TT):
                    ins = nc.tensor.transpose(ps[:, tt * P:(tt + 1) * P], shiftbuf[:, j % 2, 1 + tt * P:1 + (tt + 1) * P], ident[:, :])
                end(ins, "fvT", j)

            def in_product(out, w_h, w_l):
                for k in range(KT):
                    nc.tensor.matmul(out, w_l(k), h_hi[:, k, :], start=(k == 0), stop=False)
                    nc.tensor.matmul(out, w_h(k), h_lo[:, k, :], start=False, stop=False)
                    ins = nc.tensor.matmul(out, w_h(k), h_hi[:, k, :], start=False, stop=(k == KT - 1))
                return ins

            for i, m in enumerate(U_ORDER):
                ps = begin("u", m)
                pe.wait_ge(u_lo_ready, i + 1)
                end(in_product(ps[:, :], lambda k: u_hi[i % 2][:, k, :], lambda k: u_lo[i % 2][:, k, :]), "u", m)
                if m == 15:
                    pe.wait_ge(ff_split, 2)
                    ps = begin("ff")
                    end(in_product(ps[0:H, :], lambda k: ff_hi[:, k, :], lambda k: ff_lo[:, k, :]), "ff")
                if m == 3:
                    pe.wait_ge(lora_ready, 1)
                    pe.wait_ge(small_in, 16 * 8)
                    for nm, lo in (("z", 0), ("a", LORA)):
                        for j in range(JT):
                            ps = begin(nm, j)
                            end(nc.tensor.matmul(ps[:, :], lora_up[lo:lo + LORA, j * P:(j + 1) * P],
                                                 wa[lo:lo + LORA, :], start=True, stop=True), nm, j)
                if m == 11:
                    for tt in range(TT):
                        ps = begin("g", tt)
                        end(nc.tensor.matmul(ps[:, :], gl[:, tt * P:(tt + 1) * P], gup, start=True, stop=True), "g", tt)
                if m == 16:
                    for j in range(JT):
                        ps = begin("ss", j)
                        pe.wait_ge(kksq_ready, j + 1)
                        end(nc.tensor.matmul(ps[:, :], blk[:, :], AR[:, j, :, 0:C], start=True, stop=True), "ss", j)
                if m > 22:
                    v_transposes(m - 23)
            v_transposes(JT - 1)
            pe.wait_ge(elem_done, JT)
            ps = begin("bonus")
            for tt in range(TT):
                for j in range(JT):
                    ins = nc.tensor.matmul(ps[:, tt * H + 2 * j:tt * H + 2 * j + 2], aT[:, j, tt * P:(tt + 1) * P],
                                           blk[:, 0:P:N], start=True, stop=True)
            end(ins, "bonus")

            pe.wait_ge(c3_ready, 1)
            for j in range(JT):
                emptied(pe, "fvT", j)
            for m in range(14, 22):
                emptied(pe, "u", m)

            def scores(i):
                qb, h = units[i]
                j, lo = h // 2, (h % 2) * N
                keys = (qb + 1) * P
                ps = begin("S", qb, h)
                nc.tensor.matmul(ps[:, 0:keys], fqk[lo:lo + N, 0, j, qb * P:(qb + 1) * P], fqk[lo:lo + N, 1, j, 0:keys],
                                 start=True, stop=False)
                nc.tensor.matmul(ps[:, qb * P:keys], identb[:, :], causal[:, :], start=False, stop=False,
                                 skip_group_check=True)
                end(nc.tensor.matmul(ps[:, 0:keys], selh[:, h, :], c3[:, 0:keys], start=False, stop=True), "S", qb, h)

            def transposes(i):
                qb, h = units[i]
                ps = begin("PT", qb, h)
                emptied(pe, "S", qb, h)
                for kb in range(qb + 1):
                    ins = nc.tensor.transpose(ps[:, kb * P:(kb + 1) * P], fP[:, i % 2, kb * P:(kb + 1) * P], ident[:, :])
                end(ins, "PT", qb, h)

            def values(i):
                qb, h = units[i]
                ps = bank[3]
                if h == 0 and qb == 0:
                    pe.wait_ge(bank_free[3], uses_before_fox[3])
                elif h == 0:
                    pe.wait_ge(fox_o_free, qb)
                emptied(pe, "PT", qb, h)
                for kb in range(qb + 1):
                    ins = nc.tensor.matmul(ps[:, h * N:(h + 1) * N], fPT[:, i % 2, kb * P:(kb + 1) * P],
                                           foxv[:, kb, h * N:(h + 1) * N], start=(kb == 0), stop=(kb == qb))
                ins.then_inc(values_done, 1)

            def fo_transposes(qb):
                ps = begin("foT", qb)
                pe.wait_ge(fo_ready, qb + 1)
                for j in range(JT):
                    ins = nc.tensor.transpose(ps[:, j * P:(j + 1) * P], fo[:, qb % 2, j * P:(j + 1) * P], ident[:, :])
                end(ins, "foT", qb)

            def fox_step(i):
                if i < len(units):
                    scores(i)
                if 1 <= i <= len(units):
                    transposes(i - 1)
                if 2 <= i < len(units) + 2:
                    values(i - 2)
                if i > H and i % H == 3:
                    fo_transposes(i // H - 1)

            heads = [(h, h // 2, (h % 2) * N) for h in range(H)]

            def token_tile_T(st, src):
                ps = begin(*st)
                for j in range(JT):
                    ins = nc.tensor.transpose(ps[:, j * P:(j + 1) * P], src(j), ident[:, :])
                end(ins, *st)

            ncts = 0
            for st in rwkv_stages:
                kind, tt, q = st[0], st[1], st[1] % 2
                if kind == "fox":
                    fox_step(tt)
                    continue
                if kind == "L":
                    ps = begin(*st)
                    for h, j, lo in heads[st[2]::2]:
                        ins = nc.tensor.matmul(ps[:, j * C:(j + 1) * C], BK[lo:lo + N, j, tt, 0:C], AR[lo:lo + N, j, tt, 0:C],
                                               start=True, stop=True)
                    end(ins, *st)
                elif kind == "X0":
                    ps = begin(*st)
                    pe.wait_ge(xt0_ready, tt + 1)
                    for n in range(4):
                        ins = nc.tensor.transpose(ps[:, n * C:(n + 1) * C], XT[:, tt, 4 * st[2] + n, :], ident[:, :])
                    end(ins, *st)
                elif kind == "P":
                    lv, hf = st[2], st[3]
                    ps = begin(*st)
                    if hf == 0:
                        ncts += 1
                        pe.wait_ge(ct_ready, ncts)
                    emptied(pe, *(("X0", tt, hf) if lv == 1 else ("X", tt, lv - 1, hf)))
                    for n in range(4):
                        h = 4 * hf + n
                        ins = nc.tensor.matmul(ps[:, n * C:(n + 1) * C], CT[:, q, h, :], Xm[:, q, h, :], start=True, stop=True)
                    end(ins, *st)
                elif kind in ("X", "XT"):
                    lv, hf = st[2], st[3]
                    ps = begin(*st)
                    emptied(pe, "P", tt, lv, hf)
                    if lv > 1:
                        emptied(pe, "XT", tt, lv - 1, hf)
                    for n in range(4):
                        h = 4 * hf + n
                        lhsT, rhs = (XT[:, tt, h, :], Pm[:, q, h, :]) if kind == "X" else (Pm[:, q, h, :], XT[:, tt, h, :])
                        ins = nc.tensor.matmul(ps[:, n * C:(n + 1) * C], lhsT, rhs, start=True, stop=True)
                    end(ins, *st)
                elif kind == "vt":
                    token_tile_T(st, lambda j: vT[:, j, tt * P:(tt + 1) * P])
                elif kind == "bt":
                    token_tile_T(st, lambda j: BK[:, j, tt, 0:C])
                elif kind == "kt":
                    token_tile_T(st, lambda j: BK[:, j, tt, C:2 * C])
                elif kind == "at":
                    token_tile_T(st, lambda j: AR[:, j, tt, 0:C])
                elif kind == "KAR":
                    ps = begin(*st)
                    for n in range(2):
                        h, j, lo = heads[4 * st[3] + 2 * n + st[2]]
                        ins = nc.tensor.matmul(ps[:, n * 2 * C:(n + 1) * 2 * C], BK[lo:lo + N, j, tt, C:2 * C],
                                               AR[lo:lo + N, j, tt, :], start=True, stop=True)
                    end(ins, *st)
                elif kind == "BR":
                    ps = begin(*st)
                    for h, j, lo in heads[st[2]::2]:
                        ins = nc.tensor.matmul(ps[:, j * C:(j + 1) * C], BK[lo:lo + N, j, tt, 0:C],
                                               AR[lo:lo + N, j, tt, C:2 * C], start=True, stop=True)
                    end(ins, *st)
                elif kind == "W":
                    ps = begin(*st)
                    emptied(pe, "at", tt)
                    for hf in range(2):
                        emptied(pe, "XT", tt, LEVELS - 1, hf)
                    for h, j, lo in heads:
                        ins = nc.tensor.matmul(ps[lo:lo + N, j * C:(j + 1) * C], Atok[tt][:, h * N:(h + 1) * N], XT[:, tt, h, :],
                                               start=True, stop=True)
                    end(ins, *st)
                elif kind == "MV":
                    ps = begin(*st)
                    emptied(pe, "vt", tt)
                    pe.wait_ge(scores_masked, 6 * tt + 4)
                    for h in range(H):
                        ins = nc.tensor.matmul(ps[:, h * N:(h + 1) * N], KAR[tt][:, h, 0:C], V[q][:, h * N:(h + 1) * N],
                                               start=True, stop=True)
                    end(ins, *st)
                elif kind == "U":
                    ps = begin(*st)
                    emptied(pe, "W", tt)
                    emptied(pe, "MV", tt)
                    pe.wait_ge(state_ready, tt + 1)
                    for h in range(H):
                        nc.tensor.matmul(ps[:, h * N:(h + 1) * N], XT[:, tt, h, :], MV[tt][:, h * N:(h + 1) * N],
                                         start=(h == 0), stop=False, skip_group_check=True)
                    for j in range(JT):
                        ins = nc.tensor.matmul(ps[:, j * P:(j + 1) * P], WT[tt][:, j, :], ST[:, j, :],
                                               start=False, stop=True, skip_group_check=True)
                    end(ins, *st)
                elif kind == "Yfrom":
                    ps = begin("Y", tt)
                    for j in range(JT):
                        nc.tensor.matmul(ps[:, j * P:(j + 1) * P], AR[:, j, tt, C:2 * C], ST[:, j, :],
                                         start=(j == 0), stop=False, skip_group_check=True)
                    for h in range(H):
                        nc.tensor.matmul(ps[:, h * N:(h + 1) * N], KAR[tt][:, h, C:2 * C], V[q][:, h * N:(h + 1) * N],
                                         start=False, stop=False, skip_group_check=True)
                elif kind == "state":
                    ps = begin(*st)
                    emptied(pe, "U", tt)
                    emptied(pe, "bt", tt)
                    emptied(pe, "kt", tt)
                    for h, j, lo in heads:
                        hv = slice(h * N, (h + 1) * N)
                        nc.tensor.matmul(ps[lo:lo + N, j * N:(j + 1) * N], Ktok[tt][:, hv], V[q][:, hv], start=True, stop=False)
                        ins = nc.tensor.matmul(ps[lo:lo + N, j * N:(j + 1) * N], Btok[tt][:, hv], U[tt][:, hv], start=False, stop=True)
                    end(ins, *st)
                elif kind == "Y":
                    emptied(pe, "U", tt)
                    pe.wait_ge(scores_masked, 6 * tt + 6)
                    for h in range(H):
                        hv = slice(h * N, (h + 1) * N)
                        ins = nc.tensor.matmul(bank[7][:, hv], BR[tt][:, h, :], U[tt][:, hv], start=False, stop=True,
                                               skip_group_check=True)
                    end(ins, *st)
                elif kind == "yT":
                    ps = begin(*st)
                    pe.wait_ge(y_ready, tt + 1)
                    for j in range(JT):
                        ins = nc.tensor.transpose(ps[:, j * P:(j + 1) * P], Yq[:, j * P:(j + 1) * P], ident[:, :])
                    end(ins, *st)
                elif kind == "o":
                    if st == ("o", 0, 0):
                        for qb in range(TT):
                            emptied(pe, "foT", qb)
                    if tt == 0:
                        pe.wait_ge(w_out_loaded[st[2]], 16)
                    emptied(pe, "yT", tt)
                    ps = begin(*st)
                    for k in range(KT):
                        ins = nc.tensor.matmul(ps[:, :], hT[:, k, tt * P:(tt + 1) * P], slots[:, st[2], k, :],
                                               start=(k == 0), stop=(k == KT - 1))
                    end(ins, *st)
                elif kind == "h2T":
                    pe.wait_ge(hrow_ready, TT + tt + 1)
                    ps = begin(*st)
                    for k in range(4):
                        o = (st[2] * 4 + k) * P
                        ins = nc.tensor.transpose(ps[:, k * P:(k + 1) * P], hrow[:, tt % 2, o:o + P], ident[:, :])
                    end(ins, *st)
                elif kind == "lg":
                    emptied(pe, "h2T", tt, 0)
                    emptied(pe, "h2T", tt, 1)
                    ps = begin(*st)
                    for k in range(KT):
                        ins = nc.tensor.matmul(ps[:, 0:E], hT[:, k, tt * P:(tt + 1) * P], rw[:, k, :],
                                               start=(k == 0), stop=(k == KT - 1))
                    end(ins, *st)

            pe.wait_ge(sel_ready, TT)
            ps = begin("cnt")
            for t2 in range(TT):
                ins = nc.tensor.matmul(ps[:, 0:E], stepm[:, OFF + P:OFF + 2 * P], Msel[:, t2, :],
                                       start=(t2 == 0), stop=(t2 == TT - 1))
            end(ins, "cnt")
            for tt in range(TT):
                ps = begin("pos", tt)
                for t2 in range(tt):
                    nc.tensor.matmul(ps[:, 0:E], stepm[:, OFF + P:OFF + 2 * P], Msel[:, t2, :],
                                     start=(t2 == 0), stop=False)
                end(nc.tensor.matmul(ps[:, 0:E], stepm[:, OFF - 1:OFF - 1 + P], Msel[:, tt, :],
                                     start=(tt == 0), stop=True), "pos", tt)
            for b in range(8):
                pe.wait_ge(bank_free[b], uses[b])

            def x_transposes(b, q, n):
                pe.wait_ge(xg_loaded[q], n * 16 + 16)
                pe.wait_ge(xt_free, b + 1)
                for k in range(KT):
                    ins = nc.tensor.transpose(bank[k // 4][:, (k % 4) * NS:(k % 4 + 1) * NS],
                                              xg[0:NS, q, k * P:(k + 1) * P], ident[0:NS, 0:NS])
                ins.then_inc(xt_full, 1)

            def unit(i, q, u, bank_, x_of, midway=None):
                n = q * UNITS + u
                c, kh = UNIT_OF[u]
                pe.wait_ge(*low_part(i, n))
                if kh == 0:
                    bias = b1r[:, c * CW:(c + 1) * CW] if c < W1C else b2r[:, (c - W1C) * CW:(c - W1C + 1) * CW]
                    nc.tensor.matmul(bank_[0:NS, :], sel[:, q, :], bias, start=True, stop=False)
                for k in range(KT // 2):
                    x_h, x_l = (x[:, kh * KT // 2 + k, :] for x in x_of)
                    w_h, w_l = w_hi[n % HI][:, k, :], w_lo[n % LO][:, k, :]
                    last = kh == 1 and k == KT // 2 - 1
                    nc.tensor.matmul(bank_[0:NS, :], x_h, w_l, start=False, stop=False)
                    nc.tensor.matmul(bank_[0:NS, :], x_h, w_h, start=False, stop=False)
                    ins = nc.tensor.matmul(bank_[0:NS, :], x_l, w_h, start=False, stop=last)
                    if k == 1 and midway:
                        midway()
                ins.then_inc(unit_used, 1)

            def act_transposes(b, c):
                pe.wait_ge(act_ready, b * W1C + (c + 1))
                if c >= 2:
                    pe.wait_ge(a_lo_ready, b * W1C + (c - 1))
                for f in range(2):
                    o = (c // 2 * 2 + f) * NS
                    ins = nc.tensor.transpose(bank[4 + c % 2][:, o:o + NS], act[0:NS, (2 * c + f) * P:(2 * c + f + 1) * P],
                                              ident[0:NS, 0:NS])
                ins.then_inc(at_full, 1)

            def block_work(i, q):
                b = i * 2 + q
                pe.wait_ge(x_lo_ready, b + 1)
                pe.wait_ge(sel_set, b + 1)
                for c in range(W1C):
                    pe.wait_ge(hid_free[c % 2], b * 2 + (c // 2 + 1))
                    for kh in range(2):
                        unit(i, q, 2 * c + kh, bank[2 + c % 2], (x_hi, x_lo))
                    if c > 0:
                        act_transposes(b, c - 1)
                for h in range(2):
                    pe.wait_ge(y_free[h], b + 1)
                pe.wait_ge(a_lo_ready, b * W1C + 2)
                unit(i, q, 8, bank[6], (a_hi, a_lo))
                x_transposes(b + 1, 1 - q, i + q)
                unit(i, q, 9, bank[7], (a_hi, a_lo), midway=lambda: act_transposes(b, 3))
                pe.wait_ge(a_lo_ready, b * W1C + 4)
                unit(i, q, 10, bank[6], (a_hi, a_lo))
                unit(i, q, 11, bank[7], (a_hi, a_lo))

            pe.sem_inc(xt_full, 1)
            x_transposes(0, 0, 0)
            with pe.Fori(0, E // 2) as i:
                for q in range(2):
                    block_work(i, q)
            pe.wait_ge(tables_ready, 1)
            npairs = pe.value_load(pairs_i[0:1, 0:1], min_val=E // 2, max_val=NB // 2)
            with pe.Fori(E // 2, NB // 2) as i:
                with pe.If(i < npairs):
                    for q in range(2):
                        block_work(i, q)

        @block.vector
        def _(dve):
            steps = [0]

            def step(ins):
                steps[0] += 1
                ins.then_inc(dve_step, 1)
                dve.wait_ge(dve_step, steps[0])

            tensor_tensor, tensor_scalar = nc.vector.tensor_tensor, nc.vector.tensor_scalar

            def heads_of(ap):
                return ap.rearrange("p (h v) -> p h v", h=H)

            def per_head(st, parts=P):
                return st.unsqueeze(2).to_broadcast([parts, H, N])

            def normalize(tt, again):
                dve.wait_ge(sumsq_ready, TT * again + tt + 1)
                step(nc.vector.reciprocal(ss[:, tt:tt + 1], ss[:, tt:tt + 1]))
                if tt >= 2:
                    for half in range(2):
                        filled(dve, "h2T" if again else "hT", tt - 2, half)
                    if again:
                        dve.wait_ge(h2_stored[tt - 2], 16)
                tensor_scalar(hrow[:, tt % 2, :], xs[:, tt, :], ss[:, tt:tt + 1], None, ALU.mult).then_inc(hrow_ready, 1)

            def take_transposed(name, tt, half, gain):
                filled(dve, name, tt, half)
                b = plan[(name, tt, half)][0]
                tensor_tensor(hT[:, half * 4:half * 4 + 4, tt * P:(tt + 1) * P],
                              bank[b][:, :].rearrange("p (k t) -> p k t", k=4),
                              vec(gain)[:, half * 4:half * 4 + 4].unsqueeze(2).to_broadcast([P, 4, P]),
                              ALU.mult).then_inc(free_of((name, tt, half)), 1)

            def split_transposed(tt):
                for half in range(2):
                    filled(dve, "hT", tt, half)
                    if tt > 0:
                        dve.wait_ge(h_lo_ready, 2 * tt - 1 + half)
                    tensor_tensor(shiftbuf[:, half, 1:T + 1].rearrange("p (k t) -> p k t", k=4),
                                  bank[plan[("hT", tt, half)][0]][:, :].rearrange("p (k t) -> p k t", k=4),
                                  vec("g1")[:, half * 4:half * 4 + 4].unsqueeze(2).to_broadcast([P, 4, P]),
                                  ALU.mult).then_inc(free_of(("hT", tt, half)), 1)
                for half in range(2):
                    dve.wait_ge(h_hi_ready, 2 * tt + half + 1)
                    k = slice(half * 4, half * 4 + 4)
                    tensor_tensor(h_lo[:, k, tt * P:(tt + 1) * P], shiftbuf[:, half, 1:T + 1].rearrange("p (k t) -> p k t", k=4),
                                  h_hi[:, k, tt * P:(tt + 1) * P], ALU.subtract).then_inc(h_lo_ready, 1)

            dve.sem_inc(lo_ready[0], RAW // 3 * 2)
            filled(dve, "vec")
            nc.vector.tensor_copy(vecT[:, 0:vrow], bank[0][:, 0:vrow]).then_inc(free_of(("vec",)), 1)
            emptied(dve, "vec")
            step(tensor_scalar(one_minus_ka, vec("ka"), -1.0, 1.0, ALU.mult, ALU.add))
            dve.sem_inc(vec_ready, 1)
            for tt in range(TT + 1):
                if tt < TT:
                    normalize(tt, 0)
                if tt > 0:
                    split_transposed(tt - 1)

            def chunks_of(ap):
                return ap.rearrange("p (c t) -> p c t", t=C)

            dve.wait_ge(ff_in, 16)
            nc.vector.tensor_copy(ff_hi[:, :, :], wff[:, :, :]).then_inc(ff_split, 1)
            dve.wait_ge(ff_split, 1)
            tensor_tensor(ff_lo[:, :, :], wff[:, :, :], ff_hi[:, :, :], ALU.subtract).then_inc(ff_split, 1)

            dve.wait_ge(consts_ready, 2)

            def mix(nth, m):
                emptied(dve, "u", m)
                cur = shiftbuf[:, nth % 2, 1:T + 1]
                prev = shiftbuf[:, nth % 2, 0:T]
                if m < 8:
                    dst = (AR if m < 4 else BK)[:, m % 4, :, C:2 * C]
                    cur, prev = (v.rearrange("p (c t) -> p c t", t=C) for v in (cur, prev))
                else:
                    dst = vT[:, m - 8, :] if m < 12 else wa if m == 12 else gl
                step(tensor_tensor(dst, prev, cur, ALU.subtract))
                nc.vector.scalar_tensor_tensor(dst, dst, vec("mu", m), cur, ALU.mult, ALU.add).then_inc(mixed, 1)
                dve.wait_ge(mixed, nth + 1)

            rwkv_order = [m for m in U_ORDER if m < 14]
            for nth, m in enumerate(rwkv_order):
                mix(nth, m)
                if m == 0:
                    dve.wait_ge(consts_ready, 3)
                    dve.wait_ge(small_in, 16 * 8)
                    filled(dve, "ff")
                    tensor_scalar(fz[0], bank[plan[("ff",)][0]][0:H, :], fb[:, 0:1], None, ALU.add).then_inc(free_of(("ff",)), 1)
                    emptied(dve, "ff")
                    step(tensor_scalar(fz[2], fz[0], 0.0, None, ALU.min))
                    dve.wait_ge(ffln_ready, 1)
                    step(tensor_tensor(fz[2], fz[1], fz[2], ALU.subtract))
                    step(nc.vector.memset(fz[0], 1.0))
                    step(nc.vector.tensor_tensor_scan(cf, fz[0], fz[2], 0.0, ALU.mult, ALU.add))
                    for g in range(2):
                        step(nc.vector.tensor_copy(cb[:, g, :], cf[:, :]))
                        step(tensor_tensor(cf[:, :], cf[:, :], cb[:, g, :], ALU.subtract))
                        step(nc.vector.tensor_copy(c3[32 * g:32 * g + H, :], cb[:, g, :]))
                    nc.vector.tensor_copy(c3[64:64 + H, :], cf[:, :]).then_inc(c3_ready, 1)

                if m < 8 or m > 11:
                    continue
                j = m - 8
                emptied(dve, "z", j)
                for cc in range(NC):
                    chunk = slice(cc * C, (cc + 1) * C)
                    step(nc.vector.tensor_tensor_scan(decay_c[:, j, chunk], stepm[:, OFF + P:OFF + P + C],
                                                      decay_s[:, j, chunk], 0.0, ALU.mult, ALU.add))
                dc, ds = chunks_of(decay_c[:, j, :]), chunks_of(decay_s[:, j, :])
                step(nc.vector.tensor_copy(mid[:, j, :], dc[:, :, MID - 1]))
                step(tensor_tensor(dc, dc, mid[:, j, :].unsqueeze(2).to_broadcast([P, NC, C]), ALU.subtract))
                step(tensor_tensor(dend[:, j, 0:NC - 1], dc[:, 0:NC - 1, C - 1], mid[:, j, 1:NC], ALU.add))
                tensor_tensor(ds, dc, ds, ALU.subtract).then_inc(cum_ready, 1)
                step(tensor_scalar(BK[:, j, :, 0:C], BK[:, j, :, C:2 * C], vec("kk", j), None, ALU.mult))
                tensor_tensor(AR[:, j, :, 0:C], BK[:, j, :, 0:C], BK[:, j, :, 0:C], ALU.mult).then_inc(kksq_ready, 1)

            for j in range(JT):
                filled(dve, "ss", j)
                tensor_scalar(AR[:, j, :, 0:C], chunks_of(bank[plan[("ss", j)][0]][:, :]), 1e-24, None, ALU.max)\
                    .then_inc(free_of(("ss", j)), 1)
                emptied(dve, "ss", j)
                dve.sem_inc(kksum_ready, 1)
            for j in range(JT):
                A_, R_, B_, K_ = AR[:, j, :, 0:C], AR[:, j, :, C:2 * C], BK[:, j, :, 0:C], BK[:, j, :, C:2 * C]
                a_ = chunks_of(aT[:, j, :])
                dve.wait_ge(kknorm_ready, j + 1)
                step(nc.vector.reciprocal(A_, A_))
                step(tensor_tensor(B_, B_, A_, ALU.mult))
                dve.wait_ge(exps_ready, j + 1)
                step(tensor_tensor(A_, B_, chunks_of(decay_s[:, j, :]), ALU.mult))
                emptied(dve, "a", j)
                step(tensor_tensor(B_, B_, a_, ALU.mult))
                step(tensor_tensor(B_, B_, chunks_of(decay_c[:, j, :]), ALU.mult))
                step(tensor_scalar(a_, a_, vec("ka", j), one_minus_ka[:, j:j + 1], ALU.mult, ALU.add))
                step(tensor_tensor(K_, K_, a_, ALU.mult))
                step(nc.vector.scalar_tensor_tensor(a_, R_, vec("rk", j), K_, ALU.mult, ALU.mult))
                step(tensor_tensor(K_, K_, chunks_of(decay_c[:, j, :]), ALU.mult))
                tensor_tensor(R_, R_, chunks_of(decay_e[:, j, :]), ALU.mult).then_inc(elem_done, 1)
            dve.wait_ge(elem_done, JT)

            def finish_fox(qb):
                dve.wait_ge(values_done, H * (qb + 1))
                u0 = qb * H
                emptied(dve, "S", qb, H - 1)
                step(nc.vector.reciprocal(rrec[:, :], rsum[:, u0:u0 + H]))
                if qb >= 2:
                    filled(dve, "foT", qb - 2)
                f = heads_of(fo[:, qb % 2, :])
                tensor_tensor(f, heads_of(bank[3][:, :]), per_head(rrec[:, :]), ALU.mult).then_inc(fox_o_free, 1)
                dve.wait_ge(fox_o_free, qb + 1)
                step(tensor_tensor(heads_of(fsq), f, f, ALU.mult))
                nc.vector.tensor_reduce(fst[:, :], heads_of(fsq), AX, ALU.add).then_inc(fox_ms_ready, 1)
                dve.wait_ge(fox_rms_ready, qb + 1)
                step(nc.vector.reciprocal(fst[:, :], fst[:, :]))
                tensor_tensor(f, f, per_head(fst[:, :]), ALU.mult).then_inc(fo_ready, 1)

            def fox_step(i):
                if i < len(units):
                    filled(dve, "S", *units[i])
                    nc.vector.tensor_reduce(nmx[:, i:i + 1], bank[i % 2][:, 0:(units[i][0] + 1) * P], AX, ALU.max,
                                            negate=True).then_inc(negmax_ready, 1)
                if 1 <= i <= len(units):
                    filled(dve, "PT", *units[i - 1])
                    if i >= 3:
                        dve.wait_ge(values_done, i - 2)
                    keys = (units[i - 1][0] + 1) * P
                    nc.vector.tensor_copy(fPT[:, (i - 1) % 2, 0:keys], bank[2][:, 0:keys])\
                        .then_inc(free_of(("PT", *units[i - 1])), 1)
                if i > H and i % H == 1:
                    finish_fox(i // H - 1)

            def parity(ap, g):
                return ap.rearrange("p (j g) t -> p j g t", g=2)[:, :, g, :]

            def four(ap):
                return ap.rearrange("p (h t) -> p h t", h=4)

            dve.wait_ge(consts_ready, 4)
            step(nc.vector.memset(STc, 0.0))
            nc.vector.memset(ST, 0.0).then_inc(state_ready, 1)
            for st in rwkv_stages:
                kind, tt, q = st[0], st[1], st[1] % 2
                if kind == "fox":
                    fox_step(tt)
                    continue
                ps = bank[plan[st][0]][:, :] if st in plan else None
                if kind == "L":
                    g = st[2]
                    filled(dve, *st)
                    if tt >= 2:
                        dve.wait_ge(ct_ready, 2 * (LEVELS - 1))
                    tensor_tensor(parity(Lm[:, q], g), four(ps), maskSC[:, 0:C].unsqueeze(1).to_broadcast([P, 4, C]),
                                  ALU.mult).then_inc(free_of(st), 1)
                    emptied(dve, *st)
                    if g == 1:
                        dve.sem_inc(scm_ready, 1)
                        step(tensor_tensor(XT[:, tt], Lm[:, q], levmask[:, 0, :].unsqueeze(1).to_broadcast([C, H, C]), ALU.mult))
                        tensor_tensor(XT[:, tt], ident[:, :].unsqueeze(1).to_broadcast([C, H, C]), XT[:, tt],
                                      ALU.subtract).then_inc(xt0_ready, 1)
                elif kind in ("X", "XT"):
                    lv, hf = st[2], st[3]
                    filled(dve, *st)
                    if kind == "XT" and lv == 1:
                        dve.wait_ge(xt0_ready, tt + 1)
                    elif lv > 1:
                        emptied(dve, kind, tt, lv - 1, hf)
                    x = (Xm[:, q] if kind == "X" else XT[:, tt])[:, 4 * hf:4 * hf + 4, :]
                    tensor_tensor(x, x, four(ps), ALU.subtract).then_inc(free_of(st), 1)
                elif kind == "KAR":
                    g, jj = st[2], st[3]
                    filled(dve, *st)
                    if 0 < tt < NC - 1:
                        filled(dve, "Y", tt - 1)
                    tensor_tensor(parity(KAR[tt][:, 4 * jj:4 * jj + 4, :], g), ps.rearrange("p (h t) -> p h t", h=2),
                                  maskSC[:, :].unsqueeze(1).to_broadcast([P, 2, 2 * C]), ALU.mult).then_inc(free_of(st), 1)
                    emptied(dve, *st)
                    dve.sem_inc(scores_masked, 1)
                elif kind == "BR":
                    filled(dve, *st)
                    tensor_tensor(parity(BR[tt], st[2]), four(ps), maskSC[:, C:2 * C].unsqueeze(1).to_broadcast([P, 4, C]),
                                  ALU.mult).then_inc(free_of(st), 1)
                    emptied(dve, *st)
                    dve.sem_inc(scores_masked, 1)
                elif kind == "U":
                    filled(dve, *st)
                    tensor_scalar(U[tt], ps, -1.0, None, ALU.mult).then_inc(free_of(st), 1)
                elif kind == "state":
                    filled(dve, *st)
                    dve.wait_ge(state_ready, tt + 1)
                    tensor_tensor(STt, STc, ps[:, 0:JT * N].rearrange("p (j v) -> p j v", j=JT), ALU.add)\
                        .then_inc(free_of(st), 1)
                    emptied(dve, *st)
                    for g in range(2):
                        r = slice(g * N, (g + 1) * N)
                        ins = tensor_tensor(ST[r, :, r], STt[r], dend[r, :, tt:tt + 1].to_broadcast([N, JT, N]), ALU.mult)
                    ins.then_inc(state_ready, 1)
                    step(tensor_tensor(STc, STt, dend[:, :, tt:tt + 1].to_broadcast([P, JT, N]), ALU.mult))
                elif kind == "Y":
                    filled(dve, *st)
                    y, yc, yq = heads_of(ps), heads_of(Yc), heads_of(Yq)
                    mean, var = gst[:, 0, :], gst[:, 1, :]
                    step(nc.vector.tensor_reduce(mean, y, AX, ALU.add))
                    step(tensor_scalar(mean, mean, 1.0 / N, None, ALU.mult))
                    if tt > 0:
                        filled(dve, "yT", tt - 1)
                    tensor_tensor(yc, y, per_head(mean), ALU.subtract).then_inc(free_of(st), 1)
                    emptied(dve, *st)
                    step(tensor_tensor(yq, yc, yc, ALU.mult))
                    nc.vector.tensor_reduce(var, yq, AX, ALU.add).then_inc(gn_var_ready, 1)
                    dve.wait_ge(gn_std_ready, tt + 1)
                    nc.vector.reciprocal(var, var).then_inc(gn_rstd_ready, 1)
                elif kind == "o":
                    filled(dve, *st)
                    dve.wait_ge(x_in[tt], 32)
                    o = xs[:, tt, st[2] * CW:(st[2] + 1) * CW]
                    tensor_tensor(o, o, ps, ALU.add).then_inc(free_of(st), 1)
                elif kind == "norm":
                    normalize(tt, 1)
                elif kind == "h2T":
                    take_transposed("h2T", tt, st[2], "g2")
                elif kind == "lg":
                    filled(dve, *st)
                    tensor_tensor(lg[:, tt, :], ps[:, 0:E], rb[:, :], ALU.add).then_inc(free_of(st), 1)
                    emptied(dve, *st)
                    step(nc.vector.max(m8[:, tt, :], lg[:, tt, :]))
                    tensor_scalar(nm0[:, tt:tt + 1], m8[:, tt, 0:1], -1.0, None, ALU.mult).then_inc(gmax_ready, 1)
                    step(nc.vector.max_index(i8[:, tt, :], m8[:, tt, :], lg[:, tt, :]))
                    step(nc.vector.tensor_copy(i8f[:, tt, :], i8[:, tt, :]))
                    step(tensor_tensor(onehot[:, tt], iotaE[:, :].unsqueeze(1).to_broadcast([P, TOPK, E]),
                                       i8f[:, tt, 0:TOPK].unsqueeze(2).to_broadcast([P, TOPK, E]), ALU.is_equal))
                    nc.vector.tensor_reduce(Msel[:, tt, :], onehot[:, tt].rearrange("p k e -> p e k"), AX, ALU.add)\
                        .then_inc(sel_ready, 1)

            filled(dve, "cnt")
            nc.vector.tensor_copy(cnt[:, :], bank[7][:, 0:E]).then_inc(free_of(("cnt",)), 1)
            emptied(dve, "cnt")
            extra = rt[:, 0, :]
            step(tensor_scalar(extra, cnt[:, :], float(NS), None, ALU.is_gt))
            for n in range(2, EXTRA + 1):
                step(nc.vector.scalar_tensor_tensor(extra, cnt[:, :], float(n * NS), extra, ALU.is_gt, ALU.add))
            step(nc.vector.tensor_tensor_scan(ovf_end[:, :], stepm[:, OFF + P:OFF + P + E], extra, 0.0, ALU.mult, ALU.add))
            step(tensor_tensor(ovf_base[:, :], ovf_end[:, :], extra, ALU.subtract))
            for tt in range(TT):
                filled(dve, "pos", tt)
                nc.vector.tensor_copy(pos[:, :], bank[plan[("pos", tt)][0]][:, 0:E]).then_inc(free_of(("pos", tt)), 1)
                emptied(dve, "pos", tt)
                step(tensor_scalar(qd[:, :], pos[:, :], float(NS), None, ALU.is_ge))
                for n in range(2, EXTRA + 1):
                    step(nc.vector.scalar_tensor_tensor(qd[:, :], pos[:, :], float(n * NS), qd[:, :], ALU.is_ge, ALU.add))
                first, later, blkid = rt[:, 2, :], rt[:, 3, :], rt[:, 4, :]
                step(tensor_scalar(first, qd[:, :], 0.0, None, ALU.is_equal))
                step(nc.vector.scalar_tensor_tensor(later, qd[:, :], float(E - 1), ovf_base[:, :], ALU.add, ALU.add))
                step(tensor_tensor(blkid, iotaE[:, :], later, ALU.subtract))
                step(tensor_tensor(blkid, blkid, first, ALU.mult))
                step(tensor_tensor(blkid, blkid, later, ALU.add))
                step(tensor_tensor(blkid, blkid, qd[:, :], ALU.subtract))
                step(nc.vector.scalar_tensor_tensor(slotm[:, :], blkid, float(NS), pos[:, :], ALU.mult, ALU.add))
                step(tensor_tensor(slotk[:, :, :], onehot[:, tt], slotm[:, :].unsqueeze(1).to_broadcast([P, TOPK, E]), ALU.mult))
                step(nc.vector.tensor_reduce(slotf[:, tt, :], slotk[:, :, :], AX, ALU.add))
                tensor_scalar(sloti[:, tt, :], slotf[:, tt, :], float(NS), None, ALU.add).then_inc(slots_ready, 1)
            dve.wait_ge(bias_split, 1)
            for dst, o, w in ((b1r, 0, F2), (b2r, F2, D)):
                ins = tensor_tensor(dst[E:2 * E, :], biasrows[E:2 * E, o:o + w], dst[E:2 * E, :], ALU.subtract)
            ins.then_inc(bias_split, 1)
            dve.wait_ge(bias_split, 2)

            def low_part_of(i, n):
                wait_used(dve, i, n - LO)
                dve.wait_ge(hi_ready, i * (2 * UNITS) + (n + 1))
                tensor_tensor(w_lo[n % LO][:, :, :], raw[n % RAW], w_hi[n % HI][:, :, :], ALU.subtract)\
                    .then_inc(lo_ready[0], 1)

            dve.wait_ge(*low_part(0, 0))
            low_part_of(0, 2)
            step(tensor_scalar(rt[:, 1, 0:NOVF // 2], iotaO[:, 0:NOVF // 2], 2.0, ovf_end[:, E - 1:E], ALU.mult, ALU.is_lt))
            step(nc.vector.tensor_reduce(pairs_f[:, 0:1], rt[:, 1, 0:NOVF // 2], AX, ALU.add))
            step(tensor_scalar(pairs_f[:, 1:2], pairs_f[:, 0:1], float(E // 2), None, ALU.add))
            step(nc.vector.tensor_copy(pairs_i[:, :], pairs_f[:, 1:2]))
            step(tensor_tensor(ovcmp[:, :, :], ovf_end[:, :].unsqueeze(1).to_broadcast([P, NOVF, E]),
                               iotaO[:, :].unsqueeze(2).to_broadcast([P, NOVF, E]), ALU.is_le))
            step(nc.vector.tensor_reduce(ovexp[:, :], ovcmp[:, :, :], AX, ALU.add))
            step(tensor_scalar(ovexp[:, :], ovexp[:, :], float(E - 1), None, ALU.min))
            step(nc.vector.tensor_copy(blkexp[:, :], ovexp[:, :]))
            dve.sem_inc(tables_ready, 1)
            for tt in range(TT):
                dve.wait_ge(gates_ready, tt + 1)
                step(nc.vector.reciprocal(gsum[:, tt:tt + 1], gsum[:, tt:tt + 1]))
                step(tensor_scalar(gate[:, tt, :], gate[:, tt, :], gsum[:, tt:tt + 1], None, ALU.mult))

            step(tensor_tensor(expert_row[:, :], ident[0:2 * E, 0:E], ident[0:2 * E, E:2 * E], ALU.add))


            for tt in range(TT):
                dve.wait_ge(h2_stored[tt], 16)

            def take_x(b):
                dve.wait_ge(xt_full, b + 2)
                for half in range(2):
                    ins = tensor_tensor(xTf.rearrange("p (k s) -> p k s", k=KT)[:, half * 4:half * 4 + 4, :],
                                        bank[half][:, 0:4 * NS].rearrange("p (k s) -> p k s", k=4),
                                        vec("g2")[:, half * 4:half * 4 + 4].unsqueeze(2).to_broadcast([P, 4, NS]), ALU.mult)
                ins.then_inc(xt_free, 1)

            def split_x(b):
                dve.wait_ge(xt_free, b + 2)
                dve.wait_ge(x_hi_ready, b + 1)
                tensor_tensor(x_lo[:, :, :], xTf.rearrange("p (k s) -> p k s", k=KT), x_hi[:, :, :], ALU.subtract)\
                    .then_inc(x_lo_ready, 1)

            def act_low(b, c):
                dve.wait_ge(a_hi_ready, b * W1C + (c + 1))
                o = c // 2 * 2 * NS
                tensor_tensor(a_lo[:, 2 * c:2 * c + 2, :], bank[4 + c % 2][:, o:o + 2 * NS].rearrange("p (f s) -> p f s", f=2),
                              a_hi[:, 2 * c:2 * c + 2, :], ALU.subtract).then_inc(a_lo_ready, 1)

            def swiglu(i, q, c):
                b, p = i * 2 + q, c % 2
                wait_used(dve, i, q * UNITS + 2 * c + 1)
                pairs = bank[2 + p][0:NS, :].rearrange("p (f s) -> p f s", s=2)
                tensor_scalar(hg[0:NS, p], pairs[:, :, 0], 7.0, None, ALU.min).then_inc(glu_ready, 1)
                tensor_scalar(hl[0:NS, p], pairs[:, :, 1], 7.0, -7.0, ALU.min, ALU.max).then_inc(hid_free[p], 1)
                dve.wait_ge(glu_ready, b * W1C + (c + 1))
                dve.wait_ge(hid_free[p], b * 2 + (c // 2 + 2))
                step_(nc.vector.scalar_tensor_tensor(hl[0:NS, p], hl[0:NS, p], 1.0, hg[0:NS, p], ALU.add, ALU.mult), b, c)
                dve.wait_ge(sig_ready, b * W1C + (c + 1))
                tensor_tensor(act[0:NS, c * CW // 2:(c + 1) * CW // 2], hl[0:NS, p], hs[0:NS, p], ALU.mult).then_inc(act_ready, 1)

            def step_(ins, b, c):
                ins.then_inc(lin_ready, 1)
                dve.wait_ge(lin_ready, b * W1C + (c + 1))

            def block_work(i, q, e, done=()):
                b = i * 2 + q
                nc.vector.tensor_copy(sel[:, q, :].unsqueeze(2), expert_row[:, bass.ds(e, 1)].unsqueeze(1).to_broadcast([2 * E, NS, 1]))\
                    .then_inc(sel_set, 1)
                for u in range(UNITS):
                    n = q * UNITS + u
                    if not by_gpsimd(n) and u not in done:
                        low_part_of(i, n)
                    if u in (4, 6, 8, 10):
                        swiglu(i, q, (u - 4) // 2)
                    if u in (7, 9, 11):
                        act_low(b, (u - 7) // 2)
                take_x(b + 1)
                act_low(b, 3)
                split_x(b + 1)

            dve.sem_inc(xt_free, 1)
            for p in range(2):
                dve.sem_inc(hid_free[p], 1)
            take_x(0)
            split_x(0)
            block_work(0, 0, 0, done=(0, 2))
            block_work(0, 1, 1)
            with dve.Fori(1, E // 2) as i:
                for q in range(2):
                    block_work(i, q, i * 2 + q)
            npairs = dve.value_load(pairs_i[0:1, 0:1], min_val=E // 2, max_val=NB // 2)
            with dve.Fori(E // 2, NB // 2) as i:
                with dve.If(i < npairs):
                    for q in range(2):
                        e = dve.value_load(blkexp[0:1, bass.ds(i * 2 + (q - E), 1)], min_val=0, max_val=E - 1)
                        block_work(i, q, e)

            dve.wait_ge(gfin_in, 16)
            for tt in range(TT + 1):
                if tt < TT:
                    dve.wait_ge(gathered[tt], 16 * TOPK)
                    for k in range(TOPK):
                        rows = slots[:, tt, 2 * k:2 * k + 2, :].rearrange("p a f -> p (a f)")
                        step(nc.vector.scalar_tensor_tensor(xs[:, tt, :], rows, gate[:, tt, k:k + 1], xs[:, tt, :],
                                                            ALU.mult, ALU.add))
                    dve.sem_inc(summed, 1)
                if tt > 0:
                    done = tt - 1
                    dve.wait_ge(normed, done + 1)
                    step(nc.vector.reciprocal(ss[:, done:done + 1], ss[:, done:done + 1]))
                    if done >= 2:
                        dve.wait_ge(out_stored[done - 2], 16)
                    nc.vector.scalar_tensor_tensor(outb[done % 2], xs[:, done, :], ss[:, done:done + 1], gfin,
                                                   ALU.mult, ALU.mult).then_inc(out_ready, 1)


_INS = ['x', 'attn_norm_g', 'w_in', 'rwkv_mu', 'rwkv_w0', 'rwkv_w_up', 'rwkv_a0', 'rwkv_a_up', 'rwkv_g_up',
        'rwkv_k_k', 'rwkv_k_a', 'rwkv_r_k', 'rwkv_ln_w', 'rwkv_ln_b', 'fox_f_bias', 'fox_out_g', 'w_out',
        'ffn_norm_g', 'router_w', 'router_b', 'expert_w1', 'expert_b1', 'expert_w2', 'expert_b2', 'final_norm_g']
_OUTS = [((1, 512, 1024), 'float32')]


def kernel(**inputs):
    import numpy as _np
    import concourse.bacc as _bacc
    from concourse import mybir as _mybir
    from concourse.bass_utils import run_bass_kernel_spmd as _run

    nc = _bacc.Bacc("TRN2", target_bir_lowering=False, num_devices=1)
    arrays, args = {}, []
    for name in _INS:
        a = _np.ascontiguousarray(inputs[name])
        arrays[f"in_{name}_dram"] = a
        args.append(nc.dram_tensor(f"in_{name}_dram", a.shape, _mybir.dt.from_np(a.dtype), kind="ExternalInput").ap())
    for i, (shape, dtype) in enumerate(_OUTS):
        dt = _mybir.dt.from_np(_np.dtype(dtype))
        args.append(nc.dram_tensor(f"out_{i}_dram", shape, dt, kind="ExternalOutput").ap())
    hymba_layer(nc, *args)
    r = _run(nc, [arrays], core_ids=[0])
    got = tuple(r.results[0][f"out_{i}_dram"] for i in range(len(_OUTS)))
    return got[0]
```
